# Optimizing a Trainium2 kernel written in Bass

```python
import numpy as np
import jax, jax.numpy as jnp
from jax import lax
import math

D_MODEL = 1024
BATCH = 1
SEQ = 256
DEPTH = 2

N_A_LAYERS = max(1, DEPTH // 2)
N_B_LAYERS = DEPTH - N_A_LAYERS

D_RNN = 1536
N_RNN_BLOCKS = 16
RNN_BLOCK = D_RNN // N_RNN_BLOCKS
CONV_WIDTH = 4
RGLRU_C = 8.0

D_FF = -(-8 * D_MODEL // (3 * 256)) * 256

N_HEADS = 16
N_KV_GROUPS = 4
HEADS_PER_GROUP = N_HEADS // N_KV_GROUPS
D_QK = 96
D_V = 64
ROPE_DIMS = D_QK // 4
ROPE_THETA = 500000.0
CMP_BLOCK = 32
CMP_STRIDE = 16
CMP_HIDDEN = 256
SEL_BLOCK = 64
SEL_TOPK = 8
WINDOW = 512
Q_BLOCK = 128
N_BRANCH = 3
EPS = 1e-6


def rmsnorm(x, g):
    xf = x.astype(jnp.float32)
    y = xf * lax.rsqrt(jnp.mean(xf * xf, axis=-1, keepdims=True) + EPS)
    return (y * g.astype(jnp.float32)).astype(x.dtype)

def apply_partial_rope(x):
    S = x.shape[1]
    half = ROPE_DIMS // 2
    inv = ROPE_THETA ** (-jnp.arange(half, dtype=jnp.float32) * 2.0 / ROPE_DIMS)
    ang = jnp.arange(S, dtype=jnp.float32)[:, None] * inv[None, :]
    bshape = (1, S) + (1,) * (x.ndim - 3) + (half,)
    cos = jnp.cos(ang).reshape(bshape)
    sin = jnp.sin(ang).reshape(bshape)
    xr = x[..., :ROPE_DIMS].astype(jnp.float32)
    x1, x2 = xr[..., :half], xr[..., half:]
    rot = jnp.concatenate([x1 * cos - x2 * sin, x2 * cos + x1 * sin], axis=-1)
    return jnp.concatenate([rot.astype(x.dtype), x[..., ROPE_DIMS:]], axis=-1)

def masked_softmax(s, mask):
    s = jnp.where(mask, s, -jnp.inf)
    m = jnp.max(s, axis=-1, keepdims=True)
    m = jnp.where(jnp.isfinite(m), m, 0.0)
    e = jnp.where(mask, jnp.exp(s - m), 0.0)
    d = jnp.sum(e, axis=-1, keepdims=True)
    return e / jnp.where(d > 0, d, 1.0)

def swiglu(h, w_gu, w_down):
    u = h @ w_gu
    g, v = u[..., :D_FF], u[..., D_FF:]
    return (jax.nn.silu(g) * v) @ w_down

def rglru_mixer(h, w_in, conv_w, conv_b, w_ra, b_ra, w_ix, b_ix, lam, w_out):
    B, S, _ = h.shape
    u = h @ w_in
    xb, yb = u[..., :D_RNN], u[..., D_RNN:]
    y = jax.nn.gelu(yb)
    xc = lax.conv_general_dilated(
        xb, conv_w[:, None, :], window_strides=(1,), padding=[(CONV_WIDTH - 1, 0)],
        dimension_numbers=('NWC', 'WIO', 'NWC'), feature_group_count=D_RNN) + conv_b
    xg = xc.reshape(B, S, N_RNN_BLOCKS, RNN_BLOCK)
    r = jax.nn.sigmoid(jnp.einsum('bsni,nij->bsnj', xg, w_ra) + b_ra).reshape(B, S, D_RNN)
    i = jax.nn.sigmoid(jnp.einsum('bsni,nij->bsnj', xg, w_ix) + b_ix).reshape(B, S, D_RNN)
    log_a = -RGLRU_C * r.astype(jnp.float32) * jax.nn.softplus(-lam.astype(jnp.float32))
    a = jnp.exp(log_a)
    mult = jnp.sqrt(-jnp.expm1(2.0 * log_a))
    bx = mult * (i * xc).astype(jnp.float32)

    def step(hprev, inp):
        a_t, b_t = inp
        hn = a_t * hprev + b_t
        return hn, hn

    _, hs = lax.scan(step, jnp.zeros((B, D_RNN), jnp.float32),
                     (a.transpose(1, 0, 2), bx.transpose(1, 0, 2)))
    rec = hs.transpose(1, 0, 2).astype(h.dtype)
    return (rec * y) @ w_out

def compress_blocks(raw, pos, w1, w2):
    B, S, G, Dh = raw.shape
    nc = (S - CMP_BLOCK) // CMP_STRIDE + 1
    idx = np.arange(nc)[:, None] * CMP_STRIDE + np.arange(CMP_BLOCK)[None, :]
    blk = raw[:, idx] + pos[None, None, :, None, :]
    blk = blk.transpose(0, 1, 3, 2, 4).reshape(B, nc, G, CMP_BLOCK * Dh)
    return jax.nn.gelu(blk @ w1) @ w2

def shared_kv(h, kv_norm_g, kv_w, cmp_pos_k, cmp_w1_k, cmp_w2_k, cmp_pos_v, cmp_w1_v, cmp_w2_v):
    B, S, _ = h.shape
    hn = rmsnorm(h, kv_norm_g)
    kv = hn @ kv_w
    gk, gv = N_KV_GROUPS * D_QK, N_KV_GROUPS * D_V
    sizes = [gk, gv, gk, gv, gk, gv]
    offs = np.concatenate([[0], np.cumsum(sizes)])
    parts = [kv[..., offs[j]:offs[j + 1]] for j in range(6)]
    k_cmp, v_cmp, k_sel, v_sel, k_win, v_win = [
        p.reshape(B, S, N_KV_GROUPS, -1) for p in parts]
    kc = compress_blocks(k_cmp, cmp_pos_k, cmp_w1_k, cmp_w2_k)
    vc = compress_blocks(v_cmp, cmp_pos_v, cmp_w1_v, cmp_w2_v)
    ks = apply_partial_rope(k_sel)
    kw = apply_partial_rope(k_win)
    pad = ((0, 0), (WINDOW, 0), (0, 0), (0, 0))
    kw_pad = jnp.pad(kw, pad)
    vw_pad = jnp.pad(v_win, pad)
    return (kc, vc, ks, v_sel, kw_pad, vw_pad)

def nsa_mixer(h, w_q, gate_bias, w_o, kc, vc, ks, vs, kw_pad, vw_pad):
    B, S, _ = h.shape
    G, HPG = N_KV_GROUPS, HEADS_PER_GROUP
    nc = kc.shape[1]
    ns = S // SEL_BLOCK
    nq = S // Q_BLOCK
    k_top = min(SEL_TOPK, ns)
    cs = np.arange(nc) * CMP_STRIDE
    ss = np.arange(ns) * SEL_BLOCK
    overlap = jnp.asarray(((cs[:, None] < ss[None, :] + SEL_BLOCK) &
                           (cs[:, None] + CMP_BLOCK > ss[None, :])).astype(np.float32))
    c_end = jnp.arange(nc) * CMP_STRIDE + CMP_BLOCK - 1
    blk_ids = jnp.arange(ns)

    u = h @ w_q
    q = (u[..., :N_HEADS * D_QK] * (D_QK ** -0.5)).reshape(B, S, G, HPG, D_QK)
    gates = jax.nn.sigmoid(u[..., N_HEADS * D_QK:] + gate_bias).reshape(B, S, G, HPG, N_BRANCH)
    q_rope = apply_partial_rope(q)

    def per_seq(args):
        qn, qr, gt, kc_b, vc_b, ks_s, vs_s, kw_b, vw_b = args
        ks_blk = ks_s.reshape(ns, SEL_BLOCK, G, D_QK).transpose(2, 0, 1, 3)
        vs_blk = vs_s.reshape(ns, SEL_BLOCK, G, D_V).transpose(2, 0, 1, 3)
        gidx = jnp.arange(G)[None, :, None]

        def per_block(bargs):
            qn_t, qr_t, g_t, qi = bargs
            s0 = qi * Q_BLOCK
            t = s0 + jnp.arange(Q_BLOCK)
            s_c = jnp.einsum('tghd,cgd->tghc', qn_t, kc_b).astype(jnp.float32)
            mask_c = (c_end[None, :] <= t[:, None])[:, None, None, :]
            p_c = masked_softmax(s_c, mask_c)
            o_c = jnp.einsum('tghc,cgv->tghv', p_c.astype(vc_b.dtype), vc_b)
            imp = jnp.einsum('tghc,cn->tgn', p_c, overlap)
            cur = (t // SEL_BLOCK)[:, None, None]
            visible = (blk_ids * SEL_BLOCK)[None, None, :] <= t[:, None, None]
            forced = (blk_ids == 0) | (blk_ids == cur) | (blk_ids == cur - 1)
            score = jnp.where(forced, jnp.inf, jnp.where(visible, imp, -jnp.inf))
            _, idx = lax.top_k(score, k_top)
            kg = ks_blk[gidx, idx]
            vg = vs_blk[gidx, idx]
            s_s = jnp.einsum('tghd,tgjld->tghjl', qr_t, kg).astype(jnp.float32)
            pos = idx[..., None] * SEL_BLOCK + jnp.arange(SEL_BLOCK)
            mask_s = (pos <= t[:, None, None, None]).reshape(Q_BLOCK, G, 1, k_top * SEL_BLOCK)
            p_s = masked_softmax(s_s.reshape(Q_BLOCK, G, HPG, k_top * SEL_BLOCK), mask_s)
            p_s = p_s.reshape(Q_BLOCK, G, HPG, k_top, SEL_BLOCK)
            o_s = jnp.einsum('tghjl,tgjlv->tghv', p_s.astype(vg.dtype), vg)
            kwin = lax.dynamic_slice_in_dim(kw_b, s0, WINDOW + Q_BLOCK, axis=0)
            vwin = lax.dynamic_slice_in_dim(vw_b, s0, WINDOW + Q_BLOCK, axis=0)
            p_pos = s0 - WINDOW + jnp.arange(WINDOW + Q_BLOCK)
            mask_w = ((p_pos[None, :] >= 0) & (p_pos[None, :] <= t[:, None]) &
                      (p_pos[None, :] > t[:, None] - WINDOW))[:, None, None, :]
            s_w = jnp.einsum('tghd,sgd->tghs', qr_t, kwin).astype(jnp.float32)
            p_w = masked_softmax(s_w, mask_w)
            o_w = jnp.einsum('tghs,sgv->tghv', p_w.astype(vwin.dtype), vwin)
            return g_t[..., 0:1] * o_c + g_t[..., 1:2] * o_s + g_t[..., 2:3] * o_w

        out = lax.map(per_block, (
            qn.reshape(nq, Q_BLOCK, G, HPG, D_QK),
            qr.reshape(nq, Q_BLOCK, G, HPG, D_QK),
            gt.reshape(nq, Q_BLOCK, G, HPG, N_BRANCH),
            jnp.arange(nq)))
        return out.reshape(S, N_HEADS * D_V)

    o = lax.map(per_seq, (q, q_rope, gates, kc, vc, ks, vs, kw_pad, vw_pad))
    return o @ w_o

def first_inputs(seed: int = 0) -> dict:
    key = jax.random.key(seed)
    ks = jax.random.split(key, 32)
    f32 = jnp.float32
    res = (2.0 * DEPTH) ** -0.5

    def nrm(k, shape, scale):
        return jax.random.normal(k, shape, f32) * scale

    kv_cols = N_BRANCH * N_KV_GROUPS * (D_QK + D_V)
    q_cols = N_HEADS * D_QK + N_HEADS * N_BRANCH
    u = jax.random.uniform(ks[9], (N_A_LAYERS, D_RNN), f32, 0.9, 0.999)
    s = u ** (1.0 / RGLRU_C)
    a_lambda = jnp.log(s) - jnp.log1p(-s)
    return {
        'x': nrm(ks[0], (BATCH, SEQ, D_MODEL), 1.0),
        'norm_g': 1.0 + nrm(ks[1], (DEPTH, 2, D_MODEL), 0.02),
        'ffn_w_gu': nrm(ks[2], (DEPTH, D_MODEL, 2 * D_FF), D_MODEL ** -0.5),
        'ffn_w_down': nrm(ks[3], (DEPTH, D_FF, D_MODEL), res * D_FF ** -0.5),
        'a_w_in': nrm(ks[4], (N_A_LAYERS, D_MODEL, 2 * D_RNN), D_MODEL ** -0.5),
        'a_conv_w': nrm(ks[5], (N_A_LAYERS, CONV_WIDTH, D_RNN), CONV_WIDTH ** -0.5),
        'a_conv_b': nrm(ks[6], (N_A_LAYERS, D_RNN), 0.01),
        'a_w_ra': nrm(ks[7], (N_A_LAYERS, N_RNN_BLOCKS, RNN_BLOCK, RNN_BLOCK), RNN_BLOCK ** -0.5),
        'a_b_ra': nrm(ks[8], (N_A_LAYERS, N_RNN_BLOCKS, RNN_BLOCK), 0.01),
        'a_w_ix': nrm(ks[10], (N_A_LAYERS, N_RNN_BLOCKS, RNN_BLOCK, RNN_BLOCK), RNN_BLOCK ** -0.5),
        'a_b_ix': nrm(ks[11], (N_A_LAYERS, N_RNN_BLOCKS, RNN_BLOCK), 0.01),
        'a_lambda': a_lambda,
        'a_w_out': nrm(ks[12], (N_A_LAYERS, D_RNN, D_MODEL), res * D_RNN ** -0.5),
        'kv_norm_g': 1.0 + nrm(ks[13], (D_MODEL,), 0.02),
        'kv_w': nrm(ks[14], (D_MODEL, kv_cols), D_MODEL ** -0.5),
        'cmp_pos_k': nrm(ks[15], (CMP_BLOCK, D_QK), 0.1),
        'cmp_w1_k': nrm(ks[16], (CMP_BLOCK * D_QK, CMP_HIDDEN), (CMP_BLOCK * D_QK) ** -0.5),
        'cmp_w2_k': nrm(ks[17], (CMP_HIDDEN, D_QK), CMP_HIDDEN ** -0.5),
        'cmp_pos_v': nrm(ks[18], (CMP_BLOCK, D_V), 0.1),
        'cmp_w1_v': nrm(ks[19], (CMP_BLOCK * D_V, CMP_HIDDEN), (CMP_BLOCK * D_V) ** -0.5),
        'cmp_w2_v': nrm(ks[20], (CMP_HIDDEN, D_V), CMP_HIDDEN ** -0.5),
        'b_w_q': nrm(ks[21], (N_B_LAYERS, D_MODEL, q_cols), D_MODEL ** -0.5),
        'b_gate_bias': nrm(ks[22], (N_B_LAYERS, N_HEADS * N_BRANCH), 0.01),
        'b_w_o': nrm(ks[23], (N_B_LAYERS, N_HEADS * D_V, D_MODEL), res * (N_HEADS * D_V) ** -0.5),
        'final_g': 1.0 + nrm(ks[24], (D_MODEL,), 0.02),
    }

def first_block(x, norm_g, ffn_w_gu, ffn_w_down, a_w_in, a_conv_w, a_conv_b, a_w_ra, a_b_ra,
              a_w_ix, a_b_ix, a_lambda, a_w_out, kv_norm_g, kv_w, cmp_pos_k, cmp_w1_k, cmp_w2_k,
              cmp_pos_v, cmp_w1_v, cmp_w2_v, b_w_q, b_gate_bias, b_w_o, final_g):
    h = x
    shared = None
    for layer in range(DEPTH):
        hn = rmsnorm(h, norm_g[layer, 0])
        if layer < N_A_LAYERS:
            h = h + rglru_mixer(hn, a_w_in[layer], a_conv_w[layer], a_conv_b[layer],
                                a_w_ra[layer], a_b_ra[layer], a_w_ix[layer], a_b_ix[layer],
                                a_lambda[layer], a_w_out[layer])
        else:
            j = layer - N_A_LAYERS
            kc, vc, ks_, vs_, kw_pad, vw_pad = shared
            h = h + nsa_mixer(hn, b_w_q[j], b_gate_bias[j], b_w_o[j],
                              kc, vc, ks_, vs_, kw_pad, vw_pad)
        h = h + swiglu(rmsnorm(h, norm_g[layer, 1]), ffn_w_gu[layer], ffn_w_down[layer])
        if layer == N_A_LAYERS - 1:
            shared = shared_kv(h, kv_norm_g, kv_w, cmp_pos_k, cmp_w1_k, cmp_w2_k,
                               cmp_pos_v, cmp_w1_v, cmp_w2_v)
    return rmsnorm(h, final_g)


N_MIXERS = 2
N_A = (DEPTH + 1) // N_MIXERS
N_B = DEPTH // N_MIXERS

S5_WIDTH = D_MODEL
S5_GROUP = 16
S5_GROUPS = S5_WIDTH // S5_GROUP
S5_STATE = 64
S5_CHUNK = 128
S5_DT_MIN = 1e-3
S5_DT_MAX = 1e-1

N_HEADS_2 = 8
HEAD_DIM = D_MODEL // N_HEADS_2
ATTN_WIDTH = N_HEADS_2 * HEAD_DIM
MOBA_BLOCK = 256
MOBA_TOPK = 3
ROT_DIM = HEAD_DIM // 4

D_FF_2 = 2816
MACARON_WEIGHT = 0.5


def rms_norm(x, g):
    xf = x.astype(jnp.float32)
    y = xf * lax.rsqrt(jnp.mean(xf * xf, axis=-1, keepdims=True) + EPS)
    return (y * g.astype(jnp.float32)).astype(x.dtype)

def swiglu_2(h, w_gate, w_up, w_down):
    return (jax.nn.silu(h @ w_gate) * (h @ w_up)) @ w_down

def cmul(ar, ai, br, bi):
    return ar * br - ai * bi, ar * bi + ai * br

def s5_mixer(h, w_in, a_re, a_im, log_dt, b_re, b_im, c_re, c_im, d_skip, w_glu, w_out):
    f32 = jnp.float32
    bsz, seq, _ = h.shape
    u = (h @ w_in).astype(f32)
    dt = jnp.exp(log_dt.astype(f32))[:, None]
    a_re = a_re.astype(f32)
    a_im = a_im.astype(f32)
    mag = jnp.exp(a_re * dt)
    lam_re = mag * jnp.cos(a_im * dt)
    lam_im = mag * jnp.sin(a_im * dt)
    den = a_re * a_re + a_im * a_im
    num_re = lam_re - 1.0
    coef_re = (num_re * a_re + lam_im * a_im) / den
    coef_im = (lam_im * a_re - num_re * a_im) / den
    bb_re, bb_im = cmul(coef_re[..., None], coef_im[..., None], b_re.astype(f32), b_im.astype(f32))
    c_re = c_re.astype(f32)
    c_im = c_im.astype(f32)
    n_chunks = seq // S5_CHUNK
    u_chunks = u.reshape(bsz, n_chunks, S5_CHUNK, S5_GROUPS, S5_GROUP).transpose(1, 0, 2, 3, 4)
    lam_re_b = jnp.broadcast_to(lam_re, (bsz, S5_CHUNK, S5_GROUPS, S5_STATE))
    lam_im_b = jnp.broadcast_to(lam_im, (bsz, S5_CHUNK, S5_GROUPS, S5_STATE))

    def combine(left, right):
        a1r, a1i, b1r, b1i = left
        a2r, a2i, b2r, b2i = right
        ar, ai = cmul(a2r, a2i, a1r, a1i)
        br, bi = cmul(a2r, a2i, b1r, b1i)
        return ar, ai, br + b2r, bi + b2i

    def step(carry, u_c):
        h_re0, h_im0 = carry
        bu_re = jnp.einsum('bcgn,gpn->bcgp', u_c, bb_re)
        bu_im = jnp.einsum('bcgn,gpn->bcgp', u_c, bb_im)
        pr, pi, sr, si = lax.associative_scan(combine, (lam_re_b, lam_im_b, bu_re, bu_im), axis=1)
        cr, ci = cmul(pr, pi, h_re0[:, None], h_im0[:, None])
        st_re = sr + cr
        st_im = si + ci
        y = jnp.einsum('bcgp,gnp->bcgn', st_re, c_re) - jnp.einsum('bcgp,gnp->bcgn', st_im, c_im)
        return (st_re[:, -1], st_im[:, -1]), y

    init = (jnp.zeros((bsz, S5_GROUPS, S5_STATE), f32), jnp.zeros((bsz, S5_GROUPS, S5_STATE), f32))
    _, ys = lax.scan(step, init, u_chunks)
    y = ys.transpose(1, 0, 2, 3, 4).reshape(bsz, seq, S5_WIDTH) + d_skip.astype(f32) * u
    g = jax.nn.gelu(y)
    g = g * jax.nn.sigmoid(g @ w_glu.astype(f32))
    return g.astype(h.dtype) @ w_out

def partial_rope(x, cos, sin):
    half = ROT_DIM // 2
    x1 = x[..., :half]
    x2 = x[..., half:ROT_DIM]
    c = cos[None, :, None, :]
    s = sin[None, :, None, :]
    return jnp.concatenate([x1 * c - x2 * s, x2 * c + x1 * s, x[..., ROT_DIM:]], axis=-1)

def moba_mixer(h, w_qkv, q_gain, k_gain, w_out):
    f32 = jnp.float32
    bsz, seq, _ = h.shape
    qkv = (h @ w_qkv).reshape(bsz, seq, 3, N_HEADS_2, HEAD_DIM)
    q = rms_norm(qkv[:, :, 0], q_gain).astype(f32)
    k = rms_norm(qkv[:, :, 1], k_gain).astype(f32)
    v = qkv[:, :, 2].astype(f32)
    pos = jnp.arange(seq, dtype=f32)
    inv_freq = ROPE_THETA ** (-jnp.arange(0, ROT_DIM, 2, dtype=f32) / ROT_DIM)
    ang = pos[:, None] * inv_freq[None, :]
    cos, sin = jnp.cos(ang), jnp.sin(ang)
    q = partial_rope(q, cos, sin) * (HEAD_DIM ** -0.5)
    k = partial_rope(k, cos, sin)
    n_blocks = -(-seq // MOBA_BLOCK)
    pad = n_blocks * MOBA_BLOCK - seq
    k_pad = jnp.pad(k, ((0, 0), (0, pad), (0, 0), (0, 0)))
    v_pad = jnp.pad(v, ((0, 0), (0, pad), (0, 0), (0, 0)))
    k_blk = k_pad.reshape(bsz, n_blocks, MOBA_BLOCK, N_HEADS_2, HEAD_DIM)
    v_blk = v_pad.reshape(bsz, n_blocks, MOBA_BLOCK, N_HEADS_2, HEAD_DIM)
    k_mean = k_blk.mean(axis=2)
    k_bh = k_blk.transpose(0, 3, 1, 2, 4)
    v_bh = v_blk.transpose(0, 3, 1, 2, 4)
    top_k = min(MOBA_TOPK, n_blocks)
    b_idx = jnp.arange(bsz)[:, None, None]
    h_idx = jnp.arange(N_HEADS_2)[None, None, :]
    blk_ids = jnp.arange(n_blocks)

    def attend_chunk(c):
        start = c * Q_BLOCK
        q_c = lax.dynamic_slice_in_dim(q, start, Q_BLOCK, axis=1)
        q_pos = start + jnp.arange(Q_BLOCK)
        own = start // MOBA_BLOCK
        gate = jnp.einsum('bqhd,bnhd->bqhn', q_c, k_mean)
        gate = jnp.where(blk_ids < own, gate, -jnp.inf)
        _, sel = lax.top_k(gate, top_k)
        k_own = lax.dynamic_slice_in_dim(k_pad, own * MOBA_BLOCK, MOBA_BLOCK, axis=1)
        v_own = lax.dynamic_slice_in_dim(v_pad, own * MOBA_BLOCK, MOBA_BLOCK, axis=1)
        k_pos = own * MOBA_BLOCK + jnp.arange(MOBA_BLOCK)
        s_own = jnp.einsum('bqhd,bkhd->bqhk', q_c, k_own)
        causal = (k_pos[None, :] <= q_pos[:, None])[None, :, None, :]
        s_own = jnp.where(causal, s_own, -jnp.inf)
        scores = []
        for j in range(top_k):
            k_sel = k_bh[b_idx, h_idx, sel[..., j]]
            s_j = jnp.einsum('bqhd,bqhkd->bqhk', q_c, k_sel)
            scores.append(jnp.where(j < own, s_j, -jnp.inf))
        scores.append(s_own)
        p = jax.nn.softmax(jnp.concatenate(scores, axis=-1), axis=-1)
        p_parts = jnp.split(p, top_k + 1, axis=-1)
        out = jnp.einsum('bqhk,bkhd->bqhd', p_parts[-1], v_own)
        for j in range(top_k):
            v_sel = v_bh[b_idx, h_idx, sel[..., j]]
            out = out + jnp.einsum('bqhk,bqhkd->bqhd', p_parts[j], v_sel)
        return out

    outs = lax.map(attend_chunk, jnp.arange(seq // Q_BLOCK))
    o = outs.transpose(1, 0, 2, 3, 4).reshape(bsz, seq, ATTN_WIDTH).astype(h.dtype)
    return o @ w_out

def second_inputs(seed: int = 0) -> dict:
    key = jax.random.key(seed)
    ks = jax.random.split(key, 24)
    f32 = jnp.float32
    nrm = lambda k, shape, scale: jax.random.normal(k, shape, f32) * scale
    x = nrm(ks[0], (BATCH, SEQ, D_MODEL), 1.0)
    ffn_norm = 1.0 + nrm(ks[1], (DEPTH, 2, D_MODEL), 0.02)
    ffn_w_gate = nrm(ks[2], (DEPTH, 2, D_MODEL, D_FF_2), D_MODEL ** -0.5)
    ffn_w_up = nrm(ks[3], (DEPTH, 2, D_MODEL, D_FF_2), D_MODEL ** -0.5)
    ffn_w_down = nrm(ks[4], (DEPTH, 2, D_FF_2, D_MODEL), D_FF_2 ** -0.5)
    mix_norm = 1.0 + nrm(ks[5], (DEPTH, D_MODEL), 0.02)
    s5_w_in = nrm(ks[6], (N_A, D_MODEL, S5_WIDTH), D_MODEL ** -0.5)
    s5_a_re = -0.5 + nrm(ks[7], (N_A, S5_GROUPS, S5_STATE), 0.01)
    s5_a_im = math.pi * jnp.arange(S5_STATE, dtype=f32)[None, None, :] + nrm(ks[8], (N_A, S5_GROUPS, S5_STATE), 0.01)
    s5_log_dt = jax.random.uniform(ks[9], (N_A, S5_GROUPS), f32, math.log(S5_DT_MIN), math.log(S5_DT_MAX))
    s5_b_re = nrm(ks[10], (N_A, S5_GROUPS, S5_STATE, S5_GROUP), (2 * S5_GROUP) ** -0.5)
    s5_b_im = nrm(ks[11], (N_A, S5_GROUPS, S5_STATE, S5_GROUP), (2 * S5_GROUP) ** -0.5)
    s5_c_re = nrm(ks[12], (N_A, S5_GROUPS, S5_GROUP, S5_STATE), S5_STATE ** -0.5)
    s5_c_im = nrm(ks[13], (N_A, S5_GROUPS, S5_GROUP, S5_STATE), S5_STATE ** -0.5)
    s5_d = nrm(ks[14], (N_A, S5_WIDTH), 1.0)
    s5_w_glu = nrm(ks[15], (N_A, S5_WIDTH, S5_WIDTH), S5_WIDTH ** -0.5)
    s5_w_out = nrm(ks[16], (N_A, S5_WIDTH, D_MODEL), S5_WIDTH ** -0.5)
    moba_w_qkv = nrm(ks[17], (N_B, D_MODEL, 3 * ATTN_WIDTH), D_MODEL ** -0.5)
    moba_q_norm = 1.0 + nrm(ks[18], (N_B, HEAD_DIM), 0.02)
    moba_k_norm = 1.0 + nrm(ks[19], (N_B, HEAD_DIM), 0.02)
    moba_w_out = nrm(ks[20], (N_B, ATTN_WIDTH, D_MODEL), ATTN_WIDTH ** -0.5)
    return {'x': x, 'ffn_norm': ffn_norm, 'ffn_w_gate': ffn_w_gate, 'ffn_w_up': ffn_w_up,
            'ffn_w_down': ffn_w_down, 'mix_norm': mix_norm, 's5_w_in': s5_w_in,
            's5_a_re': s5_a_re, 's5_a_im': s5_a_im, 's5_log_dt': s5_log_dt,
            's5_b_re': s5_b_re, 's5_b_im': s5_b_im, 's5_c_re': s5_c_re, 's5_c_im': s5_c_im,
            's5_d': s5_d, 's5_w_glu': s5_w_glu, 's5_w_out': s5_w_out,
            'moba_w_qkv': moba_w_qkv, 'moba_q_norm': moba_q_norm, 'moba_k_norm': moba_k_norm,
            'moba_w_out': moba_w_out}

def second_block(x, ffn_norm, ffn_w_gate, ffn_w_up, ffn_w_down, mix_norm, s5_w_in,
              s5_a_re, s5_a_im, s5_log_dt, s5_b_re, s5_b_im, s5_c_re, s5_c_im,
              s5_d, s5_w_glu, s5_w_out, moba_w_qkv, moba_q_norm, moba_k_norm, moba_w_out):
    h = x
    for layer in range(DEPTH):
        h = h + MACARON_WEIGHT * swiglu_2(rms_norm(h, ffn_norm[layer, 0]), ffn_w_gate[layer, 0],
                                        ffn_w_up[layer, 0], ffn_w_down[layer, 0])
        hn = rms_norm(h, mix_norm[layer])
        i = layer // N_MIXERS
        if layer % N_MIXERS == 0:
            h = h + s5_mixer(hn, s5_w_in[i], s5_a_re[i], s5_a_im[i], s5_log_dt[i], s5_b_re[i],
                             s5_b_im[i], s5_c_re[i], s5_c_im[i], s5_d[i], s5_w_glu[i], s5_w_out[i])
        else:
            h = h + moba_mixer(hn, moba_w_qkv[i], moba_q_norm[i], moba_k_norm[i], moba_w_out[i])
        h = h + MACARON_WEIGHT * swiglu_2(rms_norm(h, ffn_norm[layer, 1]), ffn_w_gate[layer, 1],
                                        ffn_w_up[layer, 1], ffn_w_down[layer, 1])
    return h


def setup_inputs(seed=0):
    out = dict(first_inputs(seed))
    for name, value in second_inputs(seed + 1).items():
        if name != "x":
            out[name + "_2"] = value
    return out


def reference(
    x, norm_g, ffn_w_gu, ffn_w_down, a_w_in, a_conv_w, a_conv_b, a_w_ra, a_b_ra, a_w_ix, a_b_ix,
    a_lambda, a_w_out, kv_norm_g, kv_w, cmp_pos_k, cmp_w1_k, cmp_w2_k, cmp_pos_v, cmp_w1_v,
    cmp_w2_v, b_w_q, b_gate_bias, b_w_o, final_g, ffn_norm_2, ffn_w_gate_2, ffn_w_up_2,
    ffn_w_down_2, mix_norm_2, s5_w_in_2, s5_a_re_2, s5_a_im_2, s5_log_dt_2, s5_b_re_2,
    s5_b_im_2, s5_c_re_2, s5_c_im_2, s5_d_2, s5_w_glu_2, s5_w_out_2, moba_w_qkv_2,
    moba_q_norm_2, moba_k_norm_2, moba_w_out_2,
):
    x = first_block(
        x, norm_g, ffn_w_gu, ffn_w_down, a_w_in, a_conv_w, a_conv_b, a_w_ra, a_b_ra, a_w_ix,
        a_b_ix, a_lambda, a_w_out, kv_norm_g, kv_w, cmp_pos_k, cmp_w1_k, cmp_w2_k, cmp_pos_v,
        cmp_w1_v, cmp_w2_v, b_w_q, b_gate_bias, b_w_o, final_g,
    )
    return second_block(
        x, ffn_norm_2, ffn_w_gate_2, ffn_w_up_2, ffn_w_down_2, mix_norm_2, s5_w_in_2, s5_a_re_2,
        s5_a_im_2, s5_log_dt_2, s5_b_re_2, s5_b_im_2, s5_c_re_2, s5_c_im_2, s5_d_2, s5_w_glu_2,
        s5_w_out_2, moba_w_qkv_2, moba_q_norm_2, moba_k_norm_2, moba_w_out_2,
    )


_drawn_inputs = setup_inputs


def setup_inputs(seed=0):
    import zlib

    import numpy as np

    out = dict(_drawn_inputs(seed))
    spreads = {}
    factors = {'norm_g': 3.683,
     'a_conv_b': 3.6,
     'a_b_ra': 8.0,
     'a_b_ix': 8.0,
     'kv_norm_g': 8.0,
     'cmp_pos_k': 8.0,
     'cmp_pos_v': 3.093,
     'b_gate_bias': 8.0,
     'ffn_norm_2': 3.506,
     'mix_norm_2': 5.904,
     's5_a_re_2': 8.0,
     's5_b_re_2': 2.892,
     's5_b_im_2': 2.913,
     's5_c_re_2': 2.963,
     's5_c_im_2': 2.906,
     'moba_q_norm_2': 8.0,
     'moba_k_norm_2': 8.0}
    for name, (base, spread) in spreads.items():
        noise = np.random.default_rng([zlib.crc32(name.encode()), seed]).standard_normal(out[name].shape)
        drawn = base * np.exp(spread * noise) if base else spread * noise
        out[name] = __import__('jax').numpy.asarray(drawn.astype(out[name].dtype))
    for name, factor in factors.items():
        out[name] = (out[name] * factor).astype(out[name].dtype)
    return out
```

```python
from contextlib import ExitStack

import numpy as np
import concourse.bass as bass
import concourse.mybir as mybir

ALU = mybir.AluOpType
ACT = mybir.ActivationFunctionType
AX = mybir.AxisListType
F32 = mybir.dt.float32
F32R = mybir.dt.float32r
I32 = mybir.dt.int32

P = 128
T = 256
D = 1024
KT = D // P
FF = 2816
FT = FF // P
PAIRS = FT // 2
EPS = 1e-6
RT = 12
GT = 3
RAW = 4
SPLIT = 4
BODY = 4

NH = 16
NG = 4
CB = 32
CS = 16
NC = (T - CB) // CS + 1
CMP_BANK = [[2, 3], [5, 6]]
NA_CMASK = 3 * T + P
NA_TAB = NA_CMASK + 2 * NC
MO_TAB = 3 * T + P
NA_W2K = 2 * CB
NA_W2V = NA_W2K + 2 * 96
NA_GATE = NA_W2V + 2 * 64
NA_SMALL = NA_GATE + 48

ST = 32
S5_PAR = 3 * ST + T
S5_PLACE = (S5_PAR + 10 * ST) * 4
TWO_PI = 6.283185

VEC = {}
for _name, _n in (("norm_00", 8), ("norm_01", 8), ("norm_10", 8), ("norm_11", 8), ("kv", 8), ("final", 8),
                  ("ffn_00", 8), ("ffn_01", 8), ("ffn_10", 8), ("ffn_11", 8), ("mix_0", 8), ("mix_1", 8),
                  ("s5_d", 8), ("conv_0", 12), ("conv_1", 12), ("conv_2", 12), ("conv_3", 12),
                  ("conv_b", 12), ("lam", 12), ("b_ra", 12), ("b_ix", 12), ("q_gain", 1), ("k_gain", 1)):
    VEC[_name] = (sum(n for _, n in VEC.values()), _n)
NVEC = sum(n for _, n in VEC.values())

HALF = {"w8": 8 * P, "w22": 11 * P, "w12": 6 * P, "q96": 8 * 96, "gate": 8 * 24}
UNIT_MAX = 2 * HALF["w22"]


def layer_plan():
    return [
        dict(kind="rglru", gain="norm_00", scale=1.0),
        dict(kind="ffn", gain="norm_01", scale=1.0),
        dict(kind="nsa", gain="kv", scale=1.0),
        dict(kind="ffn", gain="norm_11", scale=1.0),
        dict(kind="final", gain=None, scale=1.0),
        dict(kind="ffn", gain="ffn_00", scale=0.5),
        dict(kind="s5", gain="mix_0", scale=1.0),
        dict(kind="ffn", gain="ffn_01", scale=0.5),
        dict(kind="ffn", gain="ffn_10", scale=0.5),
        dict(kind="moba", gain="mix_1", scale=1.0),
        dict(kind="ffn", gain="ffn_11", scale=0.5),
    ]


UNITS = {
    "rglru": [("w8", 12), ("w12", 8)],
    "ffn": [("w8", 22), ("w22", 8)],
    "nsa": [("q96", 2), ("w8", 1), ("q96", 4), ("w8", 2), ("w8", 4), ("w8", 4), ("q96", 8), ("gate", 1), ("w8", 4)],
    "final": [],
    "s5": [("w8", 12)],
    "moba": [("w8", 16)],
}


def number_phases(phases):
    units, at = [], {k: 0 for k in HALF}
    hg = 0
    for n, ph in enumerate(phases):
        ph["u0"] = len(units)
        ph["norm"] = ph["hw"] = n
        ph["hg"] = hg if ph["gain"] else None
        hg += ph["gain"] is not None
        ph["next"] = phases[n + 1]["gain"] if n + 1 < len(phases) else None
        ph["next_hg"] = hg
        ph["last"] = n + 1 == len(phases)
        ph["before_s5"] = ph["kind"] == "ffn" and n + 1 < len(phases) and phases[n + 1]["kind"] == "s5"
        ph["tables_early"] = n > 0 and phases[n - 1]["before_s5"]
        for kind, count in UNITS[ph["kind"]]:
            for _ in range(count):
                units.append((kind, at[kind]))
                at[kind] += 1
    return units


def two_blocks(nc, ins, out, phases):
    units = number_phases(phases)
    n_halves = 2 * len(units)

    with ExitStack() as ctx:
        def sem(name):
            return ctx.enter_context(nc.semaphore(name))

        base = (nc.sbuf_base + 31) // 32 * 32
        place = [base]

        def sb(name, shape, dt=F32, at=None):
            size = int(np.prod(shape[1:])) * 4
            size = (size + 31) // 32 * 32
            if at is None:
                at = place[0]
                place[0] += size
                assert place[0] <= nc.sbuf_usable_end, (name, place[0])
            return nc.alloc_sbuf_tensor_at(name, list(shape), dt, offset=at)

        class Region:

            def __init__(self, start, end):
                self.at, self.end = start, end

            def sb(self, name, shape, dt=F32):
                size = (int(np.prod(shape[1:])) * 4 + 31) // 32 * 32
                t = sb(name, shape, dt, at=self.at)
                self.at += size
                assert self.at <= self.end, (name, self.at - self.end)
                return t

        h = sb("h", [P, KT, T])
        hg_at = place[0]
        hg_hi = sb("hg_hi", [P, KT, T], F32R)
        hg_lo = sb("hg_lo", [P, KT, T], F32R)
        raw = [sb(f"raw{r}", [P, UNIT_MAX]) for r in range(RAW)]
        w_hi = [sb(f"w_hi{s}", [P, UNIT_MAX // 2], F32R) for s in range(SPLIT)]
        w_lo = [sb(f"w_lo{s}", [P, UNIT_MAX // 2], F32R) for s in range(SPLIT)]
        vec = sb("vec", [P, NVEC])
        ones_d = sb("ones_d", [P, P])
        eps = sb("eps", [P, 1])
        sumsq = sb("sumsq", [P, T])
        square = sb("square", [P, T])
        rms = sb("rms", [P, T])
        rstd = sb("rstd", [P, T])

        sp4 = sb("sp4", [P, RT])
        tiny = [sb(f"tiny{i}", [P, 32]) for i in range(5)]
        tiny_i = sb("tiny_i", [P, 32], I32)

        sb_small = sb("sb_small", [P, 32])
        rms_tok = sb("rms_tok", [P, 2])
        rstd_tok = sb("rstd_tok", [P, 2])
        half_pi = sb("half_pi", [P, 1])

        region = (place[0], nc.sbuf_usable_end // 32 * 32)
        ffn = Region(*region)
        hid_hi = ffn.sb("hid_hi", [P, FT * T], F32R)
        hid_lo = ffn.sb("hid_lo", [P, FT * T], F32R)
        gate_s = ffn.sb("gate_s", [P, 2 * T])
        silu_s = ffn.sb("silu_s", [P, 2 * T])
        up_s = ffn.sb("up_s", [P, 2 * T])
        hid_f = ffn.sb("hid_f", [P, 2 * T])
        after_ffn = ffn.at

        bank = [nc.alloc_psum_tensor(f"bank{b}", [P, 512], F32) for b in range(8)]
        NORM_BANK = 4

        raw_loaded = [sem(f"raw_loaded{r}") for r in range(RAW)]
        hi_made = sem("hi_made")
        lo_made = sem("lo_made")
        half_used = sem("half_used")
        consts_in = sem("consts_in")
        x_in = sem("x_in")
        pool_const = sem("pool_const")
        h_written = sem("h_written")
        hghi_made = sem("hghi_made")
        hg_made = sem("hg_made")
        sq_step = sem("sq_step")
        sumsq_made = sem("sumsq_made")
        ms_made = sem("ms_made")
        rms_made = sem("rms_made")
        rstd_made = sem("rstd_made")
        gate_scaled = sem("gate_scaled")
        silu_made = sem("silu_made")
        up_scaled = sem("up_scaled")
        hidf_made = sem("hidf_made")
        hidhi_made = sem("hidhi_made")
        hid_made = sem("hid_made")
        out_sent = sem("out_sent")

        n_ffn = 0
        for ph in phases:
            if ph["kind"] == "ffn":
                ph["f"] = n_ffn
                n_ffn += 1

        def half_size(half):
            return HALF[units[half // 2][0]]

        def gain(name, m):
            return vec[:, VEC[name][0] + m:VEC[name][0] + m + 1]

        def h_count(hw, m):
            return KT * hw + m + 1

        def phase_of(kind):
            return next((ph for ph in phases if ph["kind"] == kind), None)

        BD_TILES = [(0, 0), (1, 0), (0, 1), (1, 1), (2, 1), (1, 2), (2, 2)]
        rg = Region(*region)
        y_gelu = rg.sb("y_gelu", [P, RT, T])
        xb = rg.sb("xb", [P, 2 * GT, T + 4])
        xc = rg.sb("xc", [P, 2 * GT, T])
        gate_w = rg.sb("gate_w", [P, 2 * 4 * 7, P])
        rec_hi = rg.sb("rec_hi", [P, RT, T], F32R)
        rec_lo = rg.sb("rec_lo", [P, RT, T], F32R)
        r_s = rg.sb("r_s", [P, GT, T])
        i_s = rg.sb("i_s", [P, GT, T])
        tanh_s = rg.sb("tanh_s", [P, GT, T])
        root_s = rg.sb("root_s", [P, GT, T])
        inv_s = r_s
        rec_f = root_s
        y_s = r_s[:, 0:2, :]
        gate_w_in = sem("gate_w_in")
        pads_made = sem("pads_made")
        dve_step = sem("dve_step")
        y_scaled = sem("y_scaled")
        y_made = sem("y_made")
        xb_made = sem("xb_made")
        xc_made = sem("xc_made")
        gates_done = sem("gates_done")
        sigm_made = sem("sigm_made")
        tanh_made = sem("tanh_made")
        rroot_made = sem("rroot_made")
        recf_made = sem("recf_made")
        rechi_made = sem("rechi_made")
        rec_made = sem("rec_made")
        sp4_made = sem("sp4_made")

        na = Region(*region)
        hq_hi = na.sb("hq_hi", [P, KT, T], F32R)
        hq_lo = na.sb("hq_lo", [P, KT, T], F32R)
        early = Region(na.at, region[1])
        blk_k = early.sb("blk_k", [P, CB, NG * NC])
        blk_k_hi = early.sb("blk_k_hi", [P, CB, NG * NC], F32R)
        blk_k_lo = early.sb("blk_k_lo", [P, CB, NG * NC], F32R)
        blk_v = early.sb("blk_v", [P, CB, 2 * NC])
        blk_v_hi = early.sb("blk_v_hi", [P, CB, 2 * NC], F32R)
        blk_v_lo = early.sb("blk_v_lo", [P, CB, 2 * NC], F32R)
        q_s = na.sb("q_s", [P, NH, T])
        qr_s = na.sb("qr_s", [P, NH, T])
        na.at = max(na.at, early.at)
        early = Region(na.at, region[1])
        kc_raw = early.sb("kc_raw", [P, NG, T])
        vc_raw = early.sb("vc_raw", [P, 2, T])
        swap_s = [early.sb(f"swap{i}", [P, 2, T]) for i in range(2)]
        turn_s = early.sb("turn_s", [P, 2, T])
        prob = [na.sb(f"prob{i}", [P, 4, T]) for i in range(3)]
        ks_s = na.sb("ks_s", [P, NG, T])
        kw_s = na.sb("kw_s", [P, NG, T])
        v_sel = na.sb("v_sel", [P, 2, NG * 64])
        v_win = na.sb("v_win", [P, 2, NG * 64])
        na_tab = na.sb("na_tab", [P, NA_TAB])
        na_small = na.sb("na_small", [P, NA_SMALL])
        kc_s = na.sb("kc_s", [P, NG * NC])
        vc_s = na.sb("vc_s", [P, NG, 4, 64])
        hk_s = na.sb("hk_s", [P, 2, NG * NC])
        hv_s = na.sb("hv_s", [P, 2, 2, 2 * NC])
        gates_s = na.sb("gates_s", [P, 2, 48])
        cmp_max = na.sb("cmp_max", [P, 2, NH])
        cmp_den = na.sb("cmp_den", [P, 2, NH])
        late = Region(hg_at, hg_at + 2 * KT * T * 4)
        score_c = late.sb("score_c", [P, 2, NH, 32])
        prob_c = late.sb("prob_c", [P, 2, NG, P])
        prob_t = [late.sb(f"prob_t{i}", [P, 2, 4, P]) for i in range(2)]
        hv_rep = prob_t[1]

        mo = Region(*region)
        mo_o_hi = mo.sb("mo_o_hi", [P, KT, T], F32R)
        mo_o_lo = mo.sb("mo_o_lo", [P, KT, T], F32R)
        qk_s = mo.sb("qk_s", [P, 16, T])
        qk_f = [mo.sb(f"qk_f{i}", [P, 2, T]) for i in range(2)]
        qk_sq = [mo.sb(f"qk_sq{i}", [P, 2, T]) for i in range(2)]
        v_s = mo.sb("v_s", [P, 2, D])
        mo_swap = [mo.sb(f"mo_swap{i}", [P, 2, T]) for i in range(2)]
        mo_turn = mo.sb("mo_turn", [P, 2, T])
        mo_prob = [mo.sb(f"mo_prob{i}", [P, 4, T]) for i in range(3)]
        mo_prob_t = [mo.sb(f"mo_prob_t{i}", [P, 2, 4, P]) for i in range(2)]
        mo_tab = mo.sb("mo_tab", [P, MO_TAB])
        qk_rms = mo.sb("qk_rms", [P, 2, 16])
        qk_rstd = mo.sb("qk_rstd", [P, 2, 16])

        tok_rms_made = sem("tok_rms_made")
        tok_rstd_made = sem("tok_rstd_made")
        tabs_in = sem("tabs_in")
        hqhi_made = sem("hqhi_made")
        hq_made = sem("hq_made")
        proj_read = sem("proj_read")
        pads_zero = sem("pads_zero")
        blk_made = sem("blk_made")
        blkhi_made = sem("blkhi_made")
        blklo_made = sem("blklo_made")
        cmp_gelu = sem("cmp_gelu")
        hv_copied = sem("hv_copied")
        cmp_done = sem("cmp_done")
        cmp_kept = sem("cmp_kept")
        q_copied = sem("q_copied")
        swapped = [sem(f"swapped{i}") for i in range(2)]
        turn_step = sem("turn_step")
        turned = sem("turned")
        gate_lin = sem("gate_lin")
        gates_made = sem("gates_made")
        sc_done = sem("sc_done")
        sc_ready = sem("sc_ready")
        sc_exp = sem("sc_exp")
        pc_made = sem("pc_made")
        pc_turned = sem("pc_turned")
        pc_kept = sem("pc_kept")
        scores_done = sem("scores_done")
        masked = sem("masked")
        negmax = sem("negmax")
        exp_made = sem("exp_made")
        norm_made = sem("norm_made")
        prob_made = sem("prob_made")
        prob_turned = sem("prob_turned")
        prob_kept = sem("prob_kept")
        pv_done = sem("pv_done")
        ohi_made = sem("ohi_made")
        o_made = sem("o_made")
        qkf_made = sem("qkf_made")
        qksq_made = sem("qksq_made")
        qkms_made = sem("qkms_made")
        qkrms_made = sem("qkrms_made")
        qkrstd_made = sem("qkrstd_made")
        krs_made = sem("krs_made")
        k_scaled = sem("k_scaled")

        proj_n, turn_n, sub_n, job_n = {}, {}, {}, {}
        tot = [0, 0, 0, 0]
        for ph in phases:
            for k, table, c in ((0, proj_n, {"nsa": 17, "moba": 4}), (1, turn_n, {"nsa": 12, "moba": 8}),
                                (2, sub_n, {"nsa": 16, "moba": 4}), (3, job_n, {"nsa": 8, "moba": 4})):
                if ph["kind"] in c:
                    table[ph["kind"]] = tot[k]
                    tot[k] += c[ph["kind"]]

        class Attention:

            def __init__(self, kind):
                self.nsa = kind == "nsa"
                self.branches = 2 if self.nsa else 1
                self.jobs = 8 if self.nsa else 4
                self.steps = self.jobs * self.branches
                self.step0, self.job0 = sub_n[kind], job_n[kind]
                self.prob = prob if self.nsa else mo_prob
                self.prob_t = prob_t if self.nsa else mo_prob_t
                tab = na_tab if self.nsa else mo_tab
                self.mask = tab[:, 2 * T:3 * T]
                self.ident = tab[:, 3 * T:3 * T + P]
                self.o_hi, self.o_lo = (hq_hi, hq_lo) if self.nsa else (mo_o_hi, mo_o_lo)

            def step(self, n):
                job, branch = divmod(n, self.branches)
                group, b = divmod(job, 2)
                return job, branch, group, b, P * (b + 1)

            def score_bank(self, n, i, keys):
                first = 2 * (n % 2)
                return bank[first + i * keys // 512][:, i * keys % 512:i * keys % 512 + keys]

            def o_tile(self, group, b):
                tiles = slice(2 * group, 2 * group + 2) if self.nsa else slice(4 * group, 4 * group + 4)
                return tiles, slice(P * b, P * b + P)

        max_s = [sb_small[:, 0:4], sb_small[:, 4:8]]
        neg_s = [sb_small[:, 8:12], sb_small[:, 12:16]]
        den_s = [sb_small[:, 16:20], sb_small[:, 20:24]]
        fac_s = [sb_small[:, 24:28], sb_small[:, 28:32]]

        turn_q = {"nsa": 0, "moba": 8 if "nsa" in sub_n else 0}
        tok_n = {}
        for ph in phases:
            if ph["kind"] in ("nsa", "moba"):
                tok_n[ph["kind"]] = len(tok_n)

        s5_par_place = Region(region[1] - S5_PLACE, region[1])
        s5_par = s5_par_place.sb("s5_par", [P, S5_PAR])
        s5_mag, s5_turn, s5_turn_hi, s5_turn_lo, s5_kre, s5_kim, s5_den, s5_sin, s5_cos, s5_tmp = (
            s5_par_place.sb(f"s5_{n}", [P, ST]) for n in
            ("mag", "turn", "turn_hi", "turn_lo", "kre", "kim", "den", "sin", "cos", "tmp"))
        s5_tables = Region(after_ffn, region[1] - S5_PLACE)
        table = [s5_tables.sb(f"table{i}", [P, 4, 2, T]) for i in range(4)]
        s5 = Region(region[0], after_ffn)
        u_s = s5.sb("u_s", [P, KT, T])
        bt_s = [s5.sb(f"bt{i}", [P, 2, P]) for i in range(4)]
        c_s = s5.sb("c_s", [P, 3, ST, 32])
        bu_s = s5.sb("bu_s", [P, 2, 2, T])
        ring_at = s5.at
        ring_x = [s5.sb(f"ring_x{i}", [P, 2, 2, T]) for i in range(3)]
        ring_y = [s5.sb(f"ring_y{i}", [P, 2, 2, T]) for i in range(3)]
        c_raw = [ring_x[2][:, :, :, :], ring_y[2][:, :, :, :]]
        c_tmp = ring_y[1][:, :, :, :]
        s5_late = Region(ring_at, after_ffn)
        out_hi = s5_late.sb("out_hi", [P, KT, T], F32R)
        out_lo = s5_late.sb("out_lo", [P, KT, T], F32R)
        s5_par_in = sem("s5_par_in")
        c_in = sem("c_in")
        bt_in = [sem(f"bt_in{i}") for i in range(4)]
        turn_made = sem("turn_made")
        lam_made = sem("lam_made")
        coef_made = sem("coef_made")
        pool_step = sem("pool_step")
        turns_pool = sem("turns_pool")
        turns_dve = sem("turns_dve")
        abs_made = sem("abs_made")
        table_made = sem("table_made")
        c_made = sem("c_made")
        u_made = sem("u_made")
        b_done = sem("b_done")
        bu_kept = sem("bu_kept")
        xin_made = sem("xin_made")
        yin_made = sem("yin_made")
        z_made = sem("z_made")
        xout_made = sem("xout_made")
        yout_made = sem("yout_made")
        c_done = sem("c_done")
        skip_made = sem("skip_made")
        g_made = sem("g_made")
        ghi_made = sem("ghi_made")
        glo_made = sem("glo_made")
        glu_sig = sem("glu_sig")
        gated = sem("gated")
        outhi_made = sem("outhi_made")
        outlo_made = sem("outlo_made")
        G_RUNS = ((0, 6), (6, 7), (7, 8))

        def s5_early():
            return phase_of("s5") and phase_of("nsa")

        block = ctx.enter_context(nc.Block())

        @block.sync
        def _(sp):
            def load(unit, it=0, row_step=0):
                kind, row = units[unit]
                size = 2 * HALF[kind]
                if unit >= RAW:
                    sp.wait_ge(lo_made, 2 * (unit - RAW) + 2 + 2 * row_step * it)
                src = ins[kind]
                if row_step:
                    src = src[bass.ds(row + row_step * it, 1)].rearrange("a p n -> p (a n)")
                else:
                    src = src[row]
                sp.dma_start(raw[unit % RAW][:, 0:size], src).then_inc(raw_loaded[unit % RAW], 16)

            unit = 0
            while unit < len(units):
                run = 1
                while unit + run < len(units) and units[unit + run][0] == units[unit][0]:
                    run += 1
                if unit < RAW:
                    run = min(run, RAW)
                if run >= 2 * BODY:
                    trips = run // BODY
                    with sp.Fori(0, trips) as it:
                        for j in range(BODY):
                            load(unit + j, it, BODY)
                    unit += BODY * trips
                else:
                    for j in range(run):
                        load(unit + j)
                    unit += run

        @block.gpsimd
        def _(pool):
            steps = [0]
            pool.memset(ones_d[:, :], 1.0 / D).then_inc(pool_const, 1)
            pool.memset(eps[:, :], EPS).then_inc(pool_const, 1)
            if phase_of("s5") and not s5_early():
                pool.dma_start(s5_par[:, :], ins["s5_par"]).then_inc(s5_par_in, 16)
            if phase_of("rglru"):
                pool.memset(xb[:, :, 0:4], 0.0).then_inc(pads_made, 1)
            pool.memset(half_pi[:, :], float(np.pi / 2)).then_inc(pool_const, 1)

            def sum_squares(norm, ready):
                if norm >= 1:
                    pool.wait_ge(ms_made, norm)
                for m in range(KT):
                    ready(m)
                    if m == 0:
                        pool.tensor_tensor(sumsq[:, :], h[:, m, :], h[:, m, :], ALU.mult).then_inc(sq_step, 1)
                        steps[0] += 1
                        continue
                    pool.tensor_tensor(square[:, :], h[:, m, :], h[:, m, :], ALU.mult).then_inc(sq_step, 1)
                    steps[0] += 1
                    pool.wait_ge(sq_step, steps[0])
                    last = pool.tensor_tensor(sumsq[:, :], sumsq[:, :], square[:, :], ALU.add)
                    last.then_inc(sumsq_made if m == KT - 1 else sq_step, 1)
                    if m < KT - 1:
                        steps[0] += 1
                        pool.wait_ge(sq_step, steps[0])

            def load_tables(ph):
                if ph["u0"]:
                    pool.wait_ge(half_used, 2 * ph["u0"])
                if ph["kind"] == "nsa":
                    pool.dma_start(na_tab[:, :], ins["na_tab"]).then_inc(tabs_in, 16)
                    pool.dma_start(na_small[:, :], ins["na_small"]).then_inc(tabs_in, 16)
                    if phase_of("s5"):
                        load_s5_parameters()
                else:
                    pool.dma_start(mo_tab[:, :], ins["mo_tab"]).then_inc(tabs_in, 16)

            def rotations(items, base, tab, half_dim, swaps, turn):
                n2 = 2 * half_dim

                def swap(i):
                    src, _, (s, v) = items[i]
                    pool.wait_ge(s, v)
                    if i >= 2:
                        pool.wait_ge(turned, base + i - 1)
                    buf = swaps[i % 2]
                    pool.dma_start(buf[0:half_dim, :, :], src[half_dim:n2, :, :]).then_inc(swapped[i % 2], 16)
                    pool.dma_start(buf[half_dim:n2, :, :], src[0:half_dim, :, :]).then_inc(swapped[i % 2], 16)

                def bc(a):
                    return tab[0:n2, a * T:(a + 1) * T][:, None, :].broadcast_to([n2, 2, T])

                def rotate(i):
                    src, dst, _ = items[i]
                    buf = swaps[i % 2]
                    n = base + i
                    pool.wait_ge(swapped[i % 2], 32 * ((n - i % 2) // 2 + 1))
                    pool.tensor_tensor(buf[0:n2, :, :], buf[0:n2, :, :], bc(1), ALU.mult).then_inc(turn_step, 1)
                    if i:
                        pool.wait_ge(turned, n)
                    pool.tensor_tensor(turn[0:n2, :, :], src[0:n2, :, :], bc(0), ALU.mult).then_inc(turn_step, 1)
                    pool.wait_ge(turn_step, 2 * n + 2)
                    pool.tensor_tensor(dst[0:n2, :, :], turn[0:n2, :, :], buf[0:n2, :, :], ALU.add).then_inc(turned, 1)

                for i in range(len(items)):
                    swap(i)
                    if i:
                        rotate(i - 1)
                rotate(len(items) - 1)

            def scale_probs(att):
                for n in range(att.steps):
                    job, branch, group, b, keys = att.step(n)
                    pool.wait_ge(norm_made, att.step0 + n + 1)
                    p = att.prob[n % 3][:, :, 0:keys]
                    pool.tensor_tensor(p, p, fac_s[n % 2][:, :, None].broadcast_to([P, 4, keys]), ALU.mult).then_inc(prob_made, 1)

            def nsa_phase(ph):
                load_tables(ph)
                half0 = 2 * ph["u0"]
                base = proj_n["nsa"]
                pool.wait_ge(tabs_in, 32)
                items = []
                for u in range(4):
                    kt = (ks_s, kw_s)[u // 2][:, 2 * (u % 2):2 * (u % 2) + 2, :]
                    items.append((kt, kt, (proj_read, base + 4 + u)))
                for u in range(8):
                    items.append((q_s[:, 2 * u:2 * u + 2, :], qr_s[:, 2 * u:2 * u + 2, :], (q_copied, u + 1)))
                pool.memset(vc_s[:, :, :, :], 0.0).then_inc(pads_zero, 1)
                pool.wait_ge(half_used, half0 + 18)
                pool.memset(hv_rep[:, :, :, :], 0.0).then_inc(pads_zero, 1)
                pool.memset(score_c[:, :, :, :], 0.0).then_inc(pads_zero, 1)
                rotations(items, turn_n["nsa"], na_tab, 12, swap_s, turn_s)
                scale_probs(Attention("nsa"))

            def moba_phase(ph):
                load_tables(ph)
                pool.wait_ge(tabs_in, 16 * (2 * ("nsa" in sub_n) + 1))
                items = []
                for u in range(8):
                    x = qk_s[:, 2 * u:2 * u + 2, :]
                    items.append((x, x, (q_copied, turn_q["moba"] + u + 1)))
                rotations(items, turn_n["moba"], mo_tab, 16, mo_swap, mo_turn)
                scale_probs(Attention("moba"))

            small = [0]

            def own(instruction):
                small[0] += 1
                instruction.then_inc(pool_step, 1)
                pool.wait_ge(pool_step, small[0])

            def load_s5_parameters():
                pool.dma_start(s5_par[:, :], ins["s5_par"]).then_inc(s5_par_in, 16)

            def turns(kt, free):
                tab = table[kt % 4]
                r, k = tab[:, :, 0, :], tab[:, :, 1, :]
                iota = s5_par[:, 3 * ST:3 * ST + T]
                magic = 12582912.0

                def times(dst, factor):
                    for a in range(4):
                        last = pool.tensor_scalar(dst[:, a, :], iota, factor[:, 4 * kt + a:4 * kt + a + 1], None, ALU.mult)
                        if a < 3:
                            small[0] += 1
                            last.then_inc(pool_step, 1)
                    own(last)

                if kt == 0:
                    pool.wait_ge(turn_made, 1)
                    if free:
                        pool.wait_ge(half_used, free)
                times(k, s5_turn)
                own(pool.tensor_scalar(k, k, magic, magic, ALU.add, ALU.subtract))
                times(r, s5_turn_hi)
                own(pool.tensor_tensor(r, r, k, ALU.subtract))
                times(k, s5_turn_lo)
                own(pool.tensor_tensor(r, r, k, ALU.add))
                pool.tensor_scalar(r, r, 0.5, -0.5, ALU.min, ALU.max).then_inc(turns_pool, 1)

            def s5_phase(ph):
                if not ph["tables_early"]:
                    for kt in range(4):
                        turns(kt, 0)
                if ph["u0"]:
                    pool.wait_ge(half_used, 2 * ph["u0"])
                for part in range(2):
                    pool.dma_start(c_raw[part], ins["s5_c"][:, part]).then_inc(c_in, 16)
                pool.wait_ge(c_in, 32)
                pool.wait_ge(coef_made, 1)

                def wide(x):
                    return x[:, :, None].broadcast_to([P, ST, 32])

                re, im, tmp = (x.rearrange("p a b t -> p (a b t)").rearrange("p (j n) -> p j n", n=32) for x in (*c_raw, c_tmp))
                own(pool.tensor_tensor(c_s[:, 0], re, wide(s5_kre[:, :]), ALU.mult))
                own(pool.tensor_tensor(tmp, im, wide(s5_kim[:, :]), ALU.mult))
                own(pool.tensor_tensor(c_s[:, 0], c_s[:, 0], tmp, ALU.subtract))
                own(pool.tensor_tensor(tmp, re, wide(s5_kim[:, :]), ALU.mult))
                own(pool.tensor_tensor(c_s[:, 1], im, wide(s5_kre[:, :]), ALU.mult))
                own(pool.tensor_tensor(c_s[:, 1], c_s[:, 1], tmp, ALU.add))
                pool.tensor_scalar(c_s[:, 1], c_s[:, 1], -1.0, None, ALU.mult).then_inc(c_made, 1)
                pool.tensor_scalar(c_s[:, 2], c_s[:, 0], -1.0, None, ALU.mult).then_inc(c_made, 1)

                def sin_of(n):
                    kt, q = divmod(n, 2)
                    return table[kt % 4][:, 2 * q:2 * q + 2, 0, :][:, :, None, :].broadcast_to([P, 2, 2, T])

                for n in range(17):
                    if n < 16:
                        pool.wait_ge(bu_kept, 2 * n + 2)
                        if n % 2 == 0:
                            pool.wait_ge(table_made, 2 * (n // 2) + 2)
                        if n == 0:
                            pool.wait_ge(c_made, 2)
                        if n >= 3:
                            pool.wait_ge(c_done, n - 2)
                        pool.tensor_tensor(ring_y[n % 3][:, :, :, :], bu_s[:, :, :, :], sin_of(n), ALU.mult).then_inc(yin_made, 1)
                    if n >= 1:
                        m = n - 1
                        pool.wait_ge(z_made, 4 * m + 4)
                        pool.wait_ge(xout_made, m + 1)
                        x = ring_x[m % 3]
                        pool.tensor_tensor(x[:, :, :, :], x[:, :, :, :], sin_of(m), ALU.mult).then_inc(yout_made, 1)

            sum_squares(0, lambda m: pool.wait_ge(x_in, 16))
            for ph in phases:
                if ph["kind"] == "nsa":
                    nsa_phase(ph)
                if ph["kind"] == "moba":
                    moba_phase(ph)
                if ph.get("before_s5"):
                    for kt in range(4):
                        turns(kt, 2 * ph["u0"])
                if ph["kind"] == "s5":
                    s5_phase(ph)
                if not ph["last"]:
                    sum_squares(ph["norm"] + 1, lambda m: pool.wait_ge(h_written, h_count(ph["hw"], m)))

        @block.scalar
        def _(act):
            act.dma_start(vec[:, :], ins["vec"]).then_inc(consts_in, 16)
            act.dma_start(h[:, :, :], ins["x"]).then_inc(x_in, 16)
            if phase_of("rglru"):
                act.dma_start(gate_w[:, :, :], ins["gate_w"]).then_inc(gate_w_in, 16)

            def split_hi(half, it=0):
                if half >= n_halves:
                    return
                n, s, r = half_size(half), half % SPLIT, half // 2 % RAW
                c = half % 2
                act.wait_ge(raw_loaded[r], 16 * (half // (2 * RAW) + 1) + 16 * it)
                if half >= SPLIT:
                    act.wait_ge(half_used, half - SPLIT + 1 + 2 * BODY * it)
                act.activation(w_hi[s][:, 0:n], raw[r][:, c * n:(c + 1) * n], ACT.Copy).then_inc(hi_made, 1)

            def make_hg_hi(gain_name, hg, m):
                act.activation(hg_hi[:, m, :], h[:, m, :], ACT.Copy, scale=gain(gain_name, m)).then_inc(hghi_made, 1)

            def root(norm):
                act.wait_ge(ms_made, norm + 1)
                if norm == 0:
                    act.wait_ge(pool_const, 2)
                act.activation(rms[:, :], bank[NORM_BANK][:, 0:T], ACT.Sqrt, bias=eps[:, :]).then_inc(rms_made, 1)

            def after_tile(ph, m):
                if ph["next"]:
                    act.wait_ge(h_written, h_count(ph["hw"], m))
                    make_hg_hi(ph["next"], ph["next_hg"], m)
                if ph["last"]:
                    act.wait_ge(h_written, h_count(ph["hw"], m))
                    act.dma_start(out[:, m, :], h[:, m, :]).then_inc(out_sent, 16)

            def project(ph, half0, per_tile):
                for m in range(KT):
                    for j in range(per_tile):
                        split_hi(half0 + m * per_tile + j + SPLIT)
                    if ph["before_s5"] and m % 2:
                        s5_table(m // 2)
                    after_tile(ph, m)

            def ffn_phase(ph):
                half0 = 2 * ph["u0"]
                pairs0 = PAIRS * ph["f"]

                def pair(p, it=0):
                    half = half0 + 4 * p
                    split_hi(half + SPLIT, it)
                    split_hi(half + SPLIT + 1, it)
                    if p == 0:
                        root(ph["norm"])
                    act.wait_ge(gate_scaled, pairs0 + p + 1 + 2 * it)
                    act.activation(silu_s[:, :], gate_s[:, :], ACT.Silu).then_inc(silu_made, 1)
                    split_hi(half + SPLIT + 2, it)
                    split_hi(half + SPLIT + 3, it)
                    act.wait_ge(hidf_made, pairs0 + p + 1 + 2 * it)
                    act.activation(hid_hi[:, bass.ds(p * 2 * T + 4 * T * it, 2 * T)] if p else hid_hi[:, 0:2 * T],
                                   hid_f[:, :], ACT.Copy).then_inc(hidhi_made, 1)

                pair(0)
                with act.Fori(0, 4) as it:
                    pair(1, it)
                    pair(2, it)
                pair(9)
                pair(10)
                project(ph, half0 + 4 * PAIRS, 2)

            def rglru_phase(ph):
                half0 = 2 * ph["u0"]

                def gates(g):
                    act.wait_ge(gates_done, g + 1)
                    if g:
                        act.wait_ge(recf_made, g)
                    for q in range(GT):
                        act.activation(r_s[:, q, :], bank[5 + q // 2][:, q % 2 * T:(q % 2 + 1) * T], ACT.Sigmoid,
                                       bias=gain("b_ra", GT * g + q)).then_inc(sigm_made, 1)
                    for q in range(GT):
                        n = GT + q
                        act.activation(i_s[:, q, :], bank[5 + n // 2][:, n % 2 * T:(n % 2 + 1) * T], ACT.Sigmoid,
                                       bias=gain("b_ix", GT * g + q)).then_inc(sigm_made, 1)
                    if g == 0:
                        act.wait_ge(sp4_made, 1)
                    act.wait_ge(sigm_made, 2 * GT * g + GT)
                    for q in range(GT):
                        act.activation(tanh_s[:, q, :], r_s[:, q, :], ACT.Tanh,
                                       scale=sp4[:, GT * g + q:GT * g + q + 1]).then_inc(tanh_made, 1)
                    act.wait_ge(tanh_made, GT * g + GT)
                    if g:
                        act.wait_ge(rec_made, g)
                    act.activation(root_s[:, :, :], tanh_s[:, :, :], ACT.Sqrt).then_inc(rroot_made, 1)

                def hi_of_rec(g):
                    act.wait_ge(recf_made, g + 1)
                    act.activation(rec_hi[:, GT * g:GT * g + GT, :], rec_f[:, :, :], ACT.Copy).then_inc(rechi_made, 1)

                for j in range(2 * RT):
                    split_hi(half0 + j + SPLIT)
                    if j == 1:
                        root(ph["norm"])
                    if j < RT and j % 2:
                        act.wait_ge(y_scaled, j // 2 + 1)
                        act.activation(y_gelu[:, j - 1:j + 1, :], y_s,
                                       ACT.Gelu_apprx_tanh).then_inc(y_made, 1)
                    if j >= RT + 2 * GT - 1 and (j - RT - 2 * GT + 1) % GT == 0:
                        g = (j - RT - 2 * GT + 1) // GT
                        if g:
                            hi_of_rec(g - 1)
                        gates(g)
                hi_of_rec(2)
                gates(3)
                hi_of_rec(3)
                project(ph, half0 + 2 * RT, 2)

            def root_by_token(kind):
                act.activation(rms_tok[:, :], bank[NORM_BANK][:, T:T + 2], ACT.Sqrt, bias=eps[:, :]).then_inc(tok_rms_made, 1)

            def attention(att):
                def exps(n):
                    job, branch, group, b, keys = att.step(n)
                    act.wait_ge(negmax, att.step0 + n + 1)
                    p = att.prob[n % 3]
                    for i in range(4):
                        act.activation(p[:, i, 0:keys], p[:, i, 0:keys], ACT.Exp, bias=neg_s[n % 2][:, i:i + 1],
                                       accum_out=den_s[n % 2][:, i:i + 1]).then_inc(exp_made, 1)

                def keep(n):
                    job, branch, group, b, keys = att.step(n)
                    act.wait_ge(prob_turned, att.step0 + n + 1)
                    before = n // att.branches - (1 if att.branches == 2 else 2)
                    if before >= 0:
                        act.wait_ge(pv_done, att.job0 + before + 1)
                    for kt in range(b + 1):
                        act.activation(att.prob_t[n % 2][:, kt, :, :], bank[5 + kt][:, :].rearrange("p (i q) -> p i q", i=4),
                                       ACT.Copy).then_inc(prob_kept, 1)

                def hi_of_o(job):
                    group, b = divmod(job, 2)
                    tiles, tokens = att.o_tile(group, b)
                    width = 2 * P if att.nsa else 4 * P
                    act.wait_ge(pv_done, att.job0 + job + 1)
                    act.activation(att.o_hi[:, tiles, tokens], bank[(7, 4)[job % 2]][:, 0:width].rearrange("p (a q) -> p a q", q=P),
                                   ACT.Copy).then_inc(ohi_made, 1)

                for n in range(att.steps + 1):
                    if n < att.steps:
                        exps(n)
                    if n >= 1:
                        keep(n - 1)
                    if n >= 2 and (n - 1) % att.branches == att.branches - 1 and (n - 1) // att.branches >= 1:
                        hi_of_o((n - 1) // att.branches - 1)
                hi_of_o(att.jobs - 1)

            def nsa_phase(ph):
                half0 = 2 * ph["u0"]
                base = proj_n["nsa"]

                def hi_of_blocks(dst, src, n):
                    act.wait_ge(blk_made, n)
                    act.activation(dst[:, :, :], src[:, :, :], ACT.Copy).then_inc(blkhi_made, 1)

                for j in range(52):
                    split_hi(half0 + j + SPLIT)
                    if j == 1:
                        root(ph["norm"])
                        root_by_token("nsa")
                    if 2 <= j < 10:
                        act.activation(hq_hi[:, j - 2, :], h[:, j - 2, :], ACT.Copy, scale=gain("norm_10", j - 2)).then_inc(hqhi_made, 1)
                    if j == 10:
                        hi_of_blocks(blk_k_hi, blk_k, 1)
                    if j == 12:
                        hi_of_blocks(blk_v_hi, blk_v, 2)
                    if j == 33:
                        for m in range(2):
                            act.activation(hk_s[:, m, :], bank[m][:, 0:NG * NC], ACT.Gelu_apprx_tanh).then_inc(cmp_gelu, 1)
                        for m in range(2):
                            for e in range(2):
                                act.activation(hv_s[:, m, e, :], bank[CMP_BANK[m][e]][:, 0:2 * NC],
                                               ACT.Gelu_apprx_tanh).then_inc(cmp_gelu, 1)
                    if s5_early() and j == 44:
                        s5_lambda()
                    if j >= 34 and j < 50 and j % 2:
                        u = (j - 34) // 2
                        act.wait_ge(proj_read, base + 9 + u + 1)
                        act.activation(qr_s[0:96, 2 * u:2 * u + 2, :], q_s[0:96, 2 * u:2 * u + 2, :], ACT.Copy).then_inc(q_copied, 1)
                act.wait_ge(gate_lin, 2)
                act.activation(gates_s[:, :, :], gates_s[:, :, :], ACT.Sigmoid).then_inc(gates_made, 1)
                act.wait_ge(sc_ready, 1)
                act.activation(score_c[:, :, :, 0:NC], score_c[:, :, :, 0:NC], ACT.Exp).then_inc(sc_exp, 1)
                for b in range(2):
                    act.wait_ge(pc_turned, b + 1)
                    act.activation(prob_c[:, b, :, :], bank[5 + b][:, :].rearrange("p (g q) -> p g q", g=NG), ACT.Copy).then_inc(pc_kept, 1)
                attention(Attention("nsa"))
                project(ph, half0 + 52, 1)

            def moba_phase(ph):
                half0 = 2 * ph["u0"]
                for j in range(24):
                    split_hi(half0 + j + SPLIT)
                    if j == 1:
                        root(ph["norm"])
                        root_by_token("moba")
                    if j < 16 and j % 2:
                        u = j // 2
                        act.wait_ge(qkf_made, u + 1)
                        if u >= 2:
                            act.wait_ge(qkms_made, u - 1)
                        act.activation(qk_sq[u % 2][:, :, :], qk_f[u % 2][:, :, :], ACT.Square).then_inc(qksq_made, 1)
                        act.activation(qk_s[:, 2 * u:2 * u + 2, :], qk_f[u % 2][:, :, :], ACT.Copy,
                                       scale=gain("q_gain" if u < 4 else "k_gain", 0)).then_inc(q_copied, 1)
                    if j == 17:
                        act.wait_ge(qkms_made, 8)
                        act.activation(qk_rms[:, :, :], bank[5][:, 0:32].rearrange("p (b n) -> p b n", b=2), ACT.Sqrt,
                                       bias=eps[:, :], scale=float(D // P)).then_inc(qkrms_made, 1)
                attention(Attention("moba"))
                project(ph, half0 + 24, 1)

            def s5_lambda():
                act.wait_ge(turn_made, 1)
                act.wait_ge(pool_const, 3)
                act.activation(s5_sin[:, :], s5_turn[:, :], ACT.Sin, scale=TWO_PI).then_inc(lam_made, 1)
                act.activation(s5_cos[:, :], s5_tmp[:, :], ACT.Sin, scale=-TWO_PI, bias=half_pi[:, :]).then_inc(lam_made, 1)

            def s5_table(kt):
                if kt < 4:
                    act.wait_ge(turns_pool, kt + 1)
                else:
                    act.wait_ge(turns_dve, kt - 3)
                tab = table[kt % 4]
                act.activation(tab[:, :, 1, :], tab[:, :, 0, :], ACT.Abs).then_inc(abs_made, 1)
                act.wait_ge(abs_made, kt + 1)
                act.activation(tab[:, :, 0, :], tab[:, :, 0, :], ACT.Sin, scale=TWO_PI).then_inc(table_made, 1)
                act.activation(tab[:, :, 1, :], tab[:, :, 1, :], ACT.Sin, scale=-TWO_PI, bias=half_pi[:, :]).then_inc(table_made, 1)

            def s5_phase(ph):
                half0 = 2 * ph["u0"]

                def load_b(kt):
                    if kt >= 4:
                        act.wait_ge(b_done, 2 * (kt - 4) + 2)
                    act.dma_start(bt_s[kt % 4][:, :, :], ins["s5_b"][:, kt, :, :]).then_inc(bt_in[kt % 4], 16)

                def gelu(kt):
                    act.wait_ge(skip_made, kt + 1)
                    act.activation(u_s[:, kt, :], u_s[:, kt, :], ACT.Gelu_apprx_tanh).then_inc(g_made, 1)

                def hi_of_g(run):
                    a, b = G_RUNS[run]
                    act.wait_ge(g_made, b)
                    act.activation(hg_hi[:, a:b, :], u_s[:, a:b, :], ACT.Copy).then_inc(ghi_made, 1)

                if not s5_early():
                    s5_lambda()
                if not ph["tables_early"]:
                    for kt in range(4):
                        s5_table(kt)
                act.wait_ge(half_used, half0)
                for kt in range(4):
                    load_b(kt)
                for n in range(16):
                    if n % 4 == 0:
                        split_hi(half0 + n // 2 + SPLIT)
                        split_hi(half0 + n // 2 + 1 + SPLIT)
                        if n == 0:
                            root(ph["norm"])
                    act.wait_ge(b_done, n + 1)
                    if n:
                        act.wait_ge(xin_made, n)
                        act.wait_ge(yin_made, n)
                    q = 2 * (n % 2)
                    for c in range(2):
                        act.activation(bu_s[:, c, :, :], bank[q + c][:, :].rearrange("p (a t) -> p a t", a=2), ACT.Copy).then_inc(bu_kept, 1)
                    if n % 2 == 0 and 4 <= n < 12:
                        load_b(n // 2 + 2)
                    if n % 2 and 5 <= n < 13:
                        s5_table(4 + (n - 5) // 2)
                    if n >= 7 and n % 2:
                        gelu((n - 7) // 2)
                act.wait_ge(half_used, half0 + 8)
                gelu(5)
                hi_of_g(0)
                gelu(6)
                hi_of_g(1)
                gelu(7)
                hi_of_g(2)
                for u in range(4):
                    for j in range(2):
                        split_hi(half0 + 8 + 2 * u + j + SPLIT)
                    act.wait_ge(half_used, half0 + 10 + 2 * u)
                    if u >= 2:
                        act.wait_ge(gated, u - 1)
                    act.activation(bu_s[:, u % 2, :, :], bank[u][:, :].rearrange("p (a t) -> p a t", a=2), ACT.Sigmoid).then_inc(glu_sig, 1)
                    act.wait_ge(gated, u + 1)
                    act.activation(out_hi[:, 2 * u:2 * u + 2, :], u_s[:, 2 * u:2 * u + 2, :], ACT.Copy).then_inc(outhi_made, 1)
                project(ph, half0 + 16, 1)
            act.wait_ge(x_in, 16)
            act.wait_ge(consts_in, 16)
            for m in range(KT):
                make_hg_hi(phases[0]["gain"], 0, m)
            for half in range(SPLIT):
                split_hi(half)
            for ph in phases:
                if ph["kind"] == "ffn":
                    ffn_phase(ph)
                elif ph["kind"] == "final":
                    root(ph["norm"])
                    for m in range(KT):
                        after_tile(ph, m)
                elif ph["kind"] == "rglru":
                    rglru_phase(ph)

                elif ph["kind"] == "nsa":
                    nsa_phase(ph)
                elif ph["kind"] == "moba":
                    moba_phase(ph)
                elif ph["kind"] == "s5":
                    s5_phase(ph)
            act.wait_ge(out_sent, 16 * KT)

        @block.vector
        def _(dve):
            def split_lo(half, it=0):
                if half >= n_halves:
                    return
                n, s, r = half_size(half), half % SPLIT, half // 2 % RAW
                c = half % 2
                dve.wait_ge(hi_made, half + 1 + 2 * BODY * it)
                dve.tensor_tensor(w_lo[s][:, 0:n], raw[r][:, c * n:(c + 1) * n], w_hi[s][:, 0:n].bitcast(F32),
                                  ALU.subtract).then_inc(lo_made, 1)

            def make_hg_lo(gain_name, hg, m):
                dve.wait_ge(hghi_made, KT * hg + m + 1)
                dve.scalar_tensor_tensor(hg_lo[:, m, :], h[:, m, :], gain(gain_name, m),
                                         hg_hi[:, m, :].bitcast(F32), ALU.mult, ALU.subtract).then_inc(hg_made, 1)

            def invert(norm):
                dve.wait_ge(rms_made, norm + 1)
                dve.reciprocal(rstd[:, :], rms[:, :]).then_inc(rstd_made, 1)
                dve.wait_ge(rstd_made, norm + 1)

            def twice(row):
                return row[:, None, :].broadcast_to([P, 2, T])

            def two(x):
                return x.rearrange("p (a t) -> p a t", a=2)

            def add_to_h(ph, m, psum):
                dve.scalar_tensor_tensor(h[:, m, :], psum, ph["scale"], h[:, m, :], ALU.mult, ALU.add)\
                   .then_inc(h_written, 1)

            def project(ph, half0, per_tile):
                for m in range(KT):
                    half = half0 + m * per_tile
                    if per_tile == 2:
                        split_lo(half + SPLIT)
                    dve.wait_ge(half_used, half + per_tile)
                    add_to_h(ph, m, bank[2 + m % 2][:, 0:T])
                    split_lo(half + per_tile - 1 + SPLIT)
                    if ph["next"]:
                        make_hg_lo(ph["next"], ph["next_hg"], m)

            def ffn_phase(ph):
                half0 = 2 * ph["u0"]
                pairs0 = PAIRS * ph["f"]

                def pair(p, it=0):
                    half = half0 + 4 * p
                    gate, up = bank[2 * (p % 2)], bank[2 * (p % 2) + 1]
                    nth = pairs0 + p + 1 + 2 * it
                    split_lo(half + SPLIT, it)
                    if p == 0:
                        invert(ph["norm"])
                    dve.wait_ge(half_used, half + 2 + 2 * BODY * it)
                    dve.tensor_tensor(two(gate_s[:, :]), two(gate[:, :]), twice(rstd), ALU.mult).then_inc(gate_scaled, 1)
                    split_lo(half + SPLIT + 1, it)
                    split_lo(half + SPLIT + 2, it)
                    dve.wait_ge(half_used, half + 4 + 2 * BODY * it)
                    dve.tensor_tensor(two(up_s[:, :]), two(up[:, :]), twice(rstd), ALU.mult).then_inc(up_scaled, 1)
                    dve.wait_ge(silu_made, nth)
                    dve.wait_ge(up_scaled, nth)
                    dve.tensor_tensor(hid_f[:, :], up_s[:, :], silu_s[:, :], ALU.mult).then_inc(hidf_made, 1)
                    split_lo(half + SPLIT + 3, it)
                    dve.wait_ge(hidhi_made, nth)
                    at = bass.ds(p * 2 * T + 4 * T * it, 2 * T) if p else slice(0, 2 * T)
                    dve.tensor_tensor(hid_lo[:, at], hid_f[:, :], hid_hi[:, at].bitcast(F32), ALU.subtract)\
                       .then_inc(hid_made, 1)

                pair(0)
                with dve.Fori(0, 4) as it:
                    pair(1, it)
                    pair(2, it)
                pair(9)
                pair(10)
                project(ph, half0 + 4 * PAIRS, 2)

            steps = [0]
            mask_count = [0]

            def own(instruction):
                steps[0] += 1
                instruction.then_inc(dve_step, 1)
                dve.wait_ge(dve_step, steps[0])

            def exp_tiny(out_ap, x, n):
                magic = 12582912.0
                k, r, p = (tiny[i][:, 0:n] for i in range(3))
                own(dve.tensor_scalar(k, x, 1.4426950408889634, magic, ALU.mult, ALU.add))
                own(dve.tensor_scalar(k, k, magic, -126.0, ALU.subtract, ALU.max))
                own(dve.tensor_scalar(k, k, 127.0, None, ALU.min))
                own(dve.scalar_tensor_tensor(r, k, -0.693359375, x, ALU.mult, ALU.add))
                own(dve.scalar_tensor_tensor(r, k, 2.12194440054690583e-4, r, ALU.mult, ALU.add))
                own(dve.tensor_scalar(r, r, 0.35, -0.35, ALU.min, ALU.max))
                own(dve.tensor_scalar(p, r, 1.0 / 5040.0, None, ALU.mult))
                for c in (1.0 / 720, 1.0 / 120, 1.0 / 24, 1.0 / 6, 0.5, 1.0):
                    own(dve.scalar_tensor_tensor(p, p, c, r, ALU.add, ALU.mult))
                own(dve.tensor_scalar(r, k, 127.0, None, ALU.add))
                own(dve.tensor_copy(tiny_i[:, 0:n], r))
                own(dve.tensor_scalar(tiny_i[:, 0:n], tiny_i[:, 0:n], 23, None, ALU.logical_shift_left))
                own(dve.scalar_tensor_tensor(out_ap, p, 1.0, tiny_i[:, 0:n].bitcast(F32), ALU.add, ALU.mult))

            def softplus_lambda():
                lam = vec[:, VEC["lam"][0]:VEC["lam"][0] + RT]
                a, e, s, s2, p = (t[:, 0:RT] for t in (tiny[3], tiny[4], tiny[3], tiny[0], tiny[1]))
                own(dve.tensor_scalar(a, lam, -1.0, None, ALU.mult))
                own(dve.tensor_tensor(a, a, lam, ALU.min))
                exp_tiny(e, a, RT)
                own(dve.tensor_scalar(s, e, 2.0, None, ALU.add))
                own(dve.reciprocal(s, s))
                own(dve.tensor_tensor(s, s, e, ALU.mult))
                own(dve.tensor_tensor(s2, s, s, ALU.mult))
                own(dve.tensor_scalar(p, s2, 1.0 / 17, None, ALU.mult))
                for n in (15, 13, 11, 9, 7, 5, 3):
                    own(dve.scalar_tensor_tensor(p, p, 1.0 / n, s2, ALU.add, ALU.mult))
                own(dve.scalar_tensor_tensor(p, p, 1.0, s, ALU.add, ALU.mult))
                own(dve.tensor_scalar(s, lam, -1.0, 0.0, ALU.mult, ALU.max))
                own(dve.scalar_tensor_tensor(p, p, 2.0, s, ALU.mult, ALU.add))
                dve.tensor_scalar(sp4[:, :], p, 4.0, None, ALU.mult).then_inc(sp4_made, 1)

            def rglru_phase(ph):
                half0 = 2 * ph["u0"]

                def conv(g):
                    slot = GT * (g % 2)
                    for j in range(4):
                        for q in range(GT):
                            m = GT * g + q
                            x = xb[:, slot + q, 1 + j:1 + j + T]
                            o = xc[:, slot + q, :]
                            if j == 0:
                                last = dve.tensor_scalar(o, x, gain("conv_0", m), gain("conv_b", m), ALU.mult, ALU.add)
                            else:
                                last = dve.scalar_tensor_tensor(o, x, gain(f"conv_{j}", m), o, ALU.mult, ALU.add)
                            if q < GT - 1:
                                steps[0] += 1
                                last.then_inc(dve_step, 1)
                        if j < 3:
                            own(last)
                        else:
                            last.then_inc(xc_made, 1)

                def recur(g):
                    slot = GT * (g % 2)
                    dve.wait_ge(tanh_made, GT * g + GT)
                    own(dve.tensor_scalar(inv_s[:, :, :], tanh_s[:, :, :], 1.0, None, ALU.add))
                    own(dve.reciprocal(inv_s[:, :, :], inv_s[:, :, :]))
                    dve.wait_ge(xc_made, g + 1)
                    own(dve.tensor_tensor(i_s[:, :, :], i_s[:, :, :], xc[:, slot:slot + GT, :], ALU.mult))
                    dve.wait_ge(rroot_made, g + 1)
                    steps[0] += 1
                    a = tanh_s
                    dve.tensor_scalar(a[:, :, :], inv_s[:, :, :], 2.0, -1.0, ALU.mult, ALU.add).then_inc(dve_step, 1)
                    own(dve.scalar_tensor_tensor(root_s[:, :, :], root_s[:, :, :], 2.0, inv_s[:, :, :], ALU.mult, ALU.mult))
                    own(dve.tensor_tensor(i_s[:, :, :], i_s[:, :, :], root_s[:, :, :], ALU.mult))
                    for q in range(GT):
                        last = dve.tensor_tensor_scan(rec_f[:, q, :], a[:, q, :], i_s[:, q, :], 0.0, ALU.mult, ALU.add)
                        if q < GT - 1:
                            steps[0] += 1
                            last.then_inc(dve_step, 1)
                    own(last)
                    if g == 0:
                        dve.wait_ge(y_made, RT // 2)
                    dve.tensor_tensor(rec_f[:, :, :], rec_f[:, :, :], y_gelu[:, GT * g:GT * g + GT, :], ALU.mult).then_inc(recf_made, 1)

                def lo_of_rec(g):
                    dve.wait_ge(rechi_made, g + 1)
                    dve.tensor_tensor(rec_lo[:, GT * g:GT * g + GT, :], rec_f[:, :, :], rec_hi[:, GT * g:GT * g + GT, :].bitcast(F32),
                                      ALU.subtract).then_inc(rec_made, 1)

                for j in range(2 * RT):
                    split_lo(half0 + j + SPLIT)
                    if j == 1:
                        invert(ph["norm"])
                    if j < RT and j % 2:
                        u = j // 2
                        dve.wait_ge(half_used, half0 + j + 1)
                        if u:
                            dve.wait_ge(y_made, u)
                        dve.tensor_tensor(y_s, two(bank[u % 4][:, :]), twice(rstd), ALU.mult).then_inc(y_scaled, 1)
                    if j >= RT and j % 2:
                        m = j - RT - 1
                        if m == 0:
                            dve.wait_ge(pads_made, 1)
                        dve.wait_ge(half_used, half0 + j + 1)
                        dve.tensor_tensor(xb[:, m % (2 * GT):m % (2 * GT) + 2, 4:4 + T], two(bank[(RT + m) // 2 % 4][:, :]), twice(rstd),
                                          ALU.mult).then_inc(xb_made, 1)
                        if m // 2 in (1, 2, 4, 5):
                            g = (m + 2) // GT - 1
                            dve.wait_ge(xb_made, m // 2 + 1)
                            if g >= 2:
                                dve.wait_ge(gates_done, g - 1)
                            conv(g)
                    if j >= RT + 2 * GT - 1 and (j - RT - 2 * GT + 1) % GT == 0:
                        g = (j - RT - 2 * GT + 1) // GT
                        if g:
                            lo_of_rec(g - 1)
                        recur(g)
                lo_of_rec(2)
                recur(3)
                lo_of_rec(3)
                project(ph, half0 + 2 * RT, 2)

            def invert_by_token(kind):
                dve.wait_ge(tok_rms_made, tok_n[kind] + 1)
                dve.reciprocal(rstd_tok[:, :], rms_tok[:, :]).then_inc(tok_rstd_made, 1)
                dve.wait_ge(tok_rstd_made, tok_n[kind] + 1)

            def attention(att):
                def mask(n):
                    job, branch, group, b, keys = att.step(n)
                    dve.wait_ge(scores_done, att.step0 + n + 1)
                    if n >= 3:
                        dve.wait_ge(prob_turned, att.step0 + n - 2)
                    p = att.prob[n % 3]
                    m = att.mask[:, T - keys:T]
                    if att.nsa:
                        banks = 1 if keys == P else 2
                        per = 4 // banks
                        for a in range(banks):
                            last = dve.tensor_tensor(p[:, per * a:per * a + per, 0:keys],
                                                     bank[2 * (n % 2) + a][:, :].rearrange("p (i k) -> p i k", i=per),
                                                     m[:, None, :].broadcast_to([P, per, keys]), ALU.add)
                            last.then_inc(masked, 1)
                    else:
                        for i in range(4):
                            last = dve.scalar_tensor_tensor(p[:, i, 0:keys], att.score_bank(n, i, keys),
                                                            qk_rstd[:, b, 4 * group + i:4 * group + i + 1], m, ALU.mult, ALU.add)
                            last.then_inc(masked, 1)
                    mask_count[0] += (1 if keys == P else 2) if att.nsa else 4
                    dve.wait_ge(masked, mask_count[0])
                    own(dve.tensor_reduce(max_s[n % 2], p[:, :, 0:keys], AX.X, ALU.max))
                    dve.tensor_scalar(neg_s[n % 2], max_s[n % 2], -1.0, None, ALU.mult).then_inc(negmax, 1)

                def factor(n):
                    job, branch, group, b, keys = att.step(n)
                    dve.wait_ge(exp_made, 4 * (att.step0 + n) + 4)
                    if n >= 2:
                        dve.wait_ge(prob_made, att.step0 + n - 1)
                    if att.nsa:
                        own(dve.reciprocal(den_s[n % 2], den_s[n % 2]))
                        g = gates_s[:, b, :].rearrange("p (h s) -> p h s", s=3)[:, 4 * group:4 * group + 4, 1 + branch]
                        dve.tensor_tensor(fac_s[n % 2], den_s[n % 2], g, ALU.mult).then_inc(norm_made, 1)
                    else:
                        dve.reciprocal(fac_s[n % 2], den_s[n % 2]).then_inc(norm_made, 1)

                def lo_of_o(job):
                    group, b = divmod(job, 2)
                    tiles, tokens = att.o_tile(group, b)
                    width = 2 * P if att.nsa else 4 * P
                    dve.wait_ge(ohi_made, att.job0 + job + 1)
                    dve.tensor_tensor(att.o_lo[:, tiles, tokens], bank[(7, 4)[job % 2]][:, 0:width].rearrange("p (a q) -> p a q", q=P),
                                      att.o_hi[:, tiles, tokens].bitcast(F32), ALU.subtract).then_inc(o_made, 1)

                split_jobs = 0
                for n in range(att.steps + 1):
                    if n < att.steps:
                        mask(n)
                    if n >= 1:
                        factor(n - 1)
                    if n - 1 >= (split_jobs + 2) * att.branches:
                        lo_of_o(split_jobs)
                        split_jobs += 1
                for job in range(split_jobs, att.jobs):
                    lo_of_o(job)

            def nsa_phase(ph):
                half0 = 2 * ph["u0"]
                base = proj_n["nsa"]

                def blocks(dst, src, groups, pos):
                    windows = src.rearrange("p g (n j) -> p g n j", j=CS)
                    for part in range(2):
                        last = dve.tensor_tensor(
                            dst[:, CS * part:CS * part + CS, :].rearrange("p j (g n) -> p j g n", g=groups),
                            windows[:, :, part:part + NC, :].rearrange("p g n j -> p j g n"),
                            pos[:, CS * part:CS * part + CS][:, :, None, None].broadcast_to([P, CS, groups, NC]), ALU.add)
                        if part == 0:
                            steps[0] += 1
                            last.then_inc(dve_step, 1)
                    last.then_inc(blk_made, 1)

                def lo_of_blocks(dst, src, hi, n):
                    dve.wait_ge(blkhi_made, n)
                    dve.tensor_tensor(dst[:, :, :], src[:, :, :], hi[:, :, :].bitcast(F32), ALU.subtract).then_inc(blklo_made, 1)

                targets = {0: kc_raw[0:96, 0:2, :], 1: kc_raw[0:96, 2:4, :], 2: vc_raw[:, :, :],
                           3: ks_s[0:96, 0:2, :], 4: ks_s[0:96, 2:4, :], 5: kw_s[0:96, 0:2, :], 6: kw_s[0:96, 2:4, :]}
                own(dve.memset(kc_raw[:, :, :], 0.0))
                for j in range(52):
                    split_lo(half0 + j + SPLIT)
                    if j == 1:
                        invert(ph["norm"])
                        invert_by_token("nsa")
                    if 2 <= j < 10:
                        dve.wait_ge(hqhi_made, j - 1)
                        dve.scalar_tensor_tensor(hq_lo[:, j - 2, :], h[:, j - 2, :], gain("norm_10", j - 2),
                                                 hq_hi[:, j - 2, :].bitcast(F32), ALU.mult, ALU.subtract).then_inc(hq_made, 1)
                    if j < 14 and j % 2:
                        u = j // 2
                        rows = P if u == 2 else 96
                        dve.wait_ge(half_used, half0 + j + 1)
                        dve.tensor_tensor(targets[u], two(bank[u % 4][0:rows, :]), rstd[0:rows, None, :].broadcast_to([rows, 2, T]),
                                          ALU.mult).then_inc(proj_read, 1)
                    if j in (15, 17):
                        u = j // 2
                        dve.wait_ge(half_used, half0 + j + 1)
                        dst = (v_sel, v_win)[u - 7]
                        for b in range(2):
                            last = dve.tensor_scalar(dst[:, b, :], two(bank[u % 4][:, :])[:, b, :], rstd_tok[:, b:b + 1], None, ALU.mult)
                            if b == 0:
                                steps[0] += 1
                                last.then_inc(dve_step, 1)
                        last.then_inc(proj_read, 1)
                    if j == 7:
                        dve.wait_ge(tabs_in, 32)
                        dve.wait_ge(proj_read, base + 3)
                        blocks(blk_k, kc_raw, NG, na_small[:, 0:CB])
                    if j == 9:
                        blocks(blk_v, vc_raw, 2, na_small[:, CB:2 * CB])
                    if j == 11:
                        lo_of_blocks(blk_k_lo, blk_k, blk_k_hi, 1)
                    if j == 13:
                        lo_of_blocks(blk_v_lo, blk_v, blk_v_hi, 2)
                    if j == 34:
                        dve.wait_ge(cmp_gelu, 6)
                        dve.wait_ge(pads_zero, 2)
                        for m in range(2):
                            for e in range(2):
                                for i in range(4):
                                    for a in range(2):
                                        g = 2 * a + e
                                        last = dve.tensor_copy(hv_rep[:, m, g, 32 * i:32 * i + NC], hv_s[:, m, e, NC * a:NC * a + NC])
                                        last.then_inc(hv_copied, 1)
                    if j == 35:
                        dve.wait_ge(cmp_done, 1)
                        dve.tensor_copy(kc_s[0:96, :], bank[7][0:96, 0:NG * NC]).then_inc(cmp_kept, 1)
                        dve.wait_ge(cmp_done, 2)
                        dve.wait_ge(pads_zero, 2)
                        for i in range(4):
                            rows = slice(32 * i, 32 * i + 32)
                            dve.tensor_copy(vc_s[rows, :, i, :], bank[6][rows, 0:NG * 64].rearrange("p (g v) -> p g v", g=NG))\
                               .then_inc(cmp_kept, 1)
                    if j >= 34 and j < 50 and j % 2:
                        u = (j - 34) // 2
                        dve.wait_ge(half_used, half0 + j + 1)
                        dve.scalar_tensor_tensor(q_s[0:96, 2 * u:2 * u + 2, :], two(bank[u % 4][0:96, :]), 96.0 ** -0.5,
                                                 rstd[0:96, None, :].broadcast_to([96, 2, T]), ALU.mult, ALU.mult).then_inc(proj_read, 1)
                    if s5_early() and j == 37:
                        s5_turns()
                    if s5_early() and j == 48:
                        s5_coefs()
                dve.wait_ge(half_used, half0 + 52)
                for b in range(2):
                    dve.scalar_tensor_tensor(gates_s[:, b, :], bank[4][:, 48 * b:48 * b + 48], rstd_tok[:, b:b + 1],
                                             na_small[:, NA_GATE:NA_GATE + 48], ALU.mult, ALU.add).then_inc(gate_lin, 1)
                sc = score_c[:, :, :, 0:NC]
                sc_m = sc.rearrange("p b h n -> p (b h) n")
                dve.wait_ge(sc_done, 1)
                dve.wait_ge(pads_zero, 3)
                for b in range(2):
                    own(dve.tensor_tensor(sc[:, b, :, :], bank[7][:, NH * NC * b:NH * NC * (b + 1)].rearrange("p (h n) -> p h n", h=NH),
                                          na_tab[:, NA_CMASK + NC * b:NA_CMASK + NC * b + NC][:, None, :].broadcast_to([P, NH, NC]), ALU.add))
                flat_max, flat_den = (x[:, :, :].rearrange("p b h -> p (b h)") for x in (cmp_max, cmp_den))
                own(dve.tensor_reduce(flat_max, sc_m, AX.X, ALU.max))
                own(dve.tensor_scalar(flat_max, flat_max, -1e29, None, ALU.max))
                dve.tensor_tensor(sc_m, sc_m, flat_max[:, :, None].broadcast_to([P, 2 * NH, NC]), ALU.subtract).then_inc(sc_ready, 1)
                dve.wait_ge(sc_exp, 1)
                own(dve.tensor_reduce(flat_den, sc_m, AX.X, ALU.add))
                own(dve.tensor_scalar(flat_den, flat_den, 0.5, None, ALU.max))
                own(dve.reciprocal(flat_den, flat_den))
                dve.wait_ge(gates_made, 1)
                g0 = gates_s[:, :, :].rearrange("p b (h s) -> p (b h) s", s=3)[:, :, 0]
                own(dve.tensor_tensor(flat_den, flat_den, g0, ALU.mult))
                dve.tensor_tensor(sc_m, sc_m, flat_den[:, :, None].broadcast_to([P, 2 * NH, NC]), ALU.mult).then_inc(pc_made, 1)
                attention(Attention("nsa"))
                project(ph, half0 + 52, 1)

            def moba_phase(ph):
                half0 = 2 * ph["u0"]
                for j in range(24):
                    split_lo(half0 + j + SPLIT)
                    if j == 1:
                        invert(ph["norm"])
                        invert_by_token("moba")
                    if j < 16 and j % 2:
                        u = j // 2
                        dve.wait_ge(half_used, half0 + j + 1)
                        if u >= 2:
                            dve.wait_ge(q_copied, turn_q["moba"] + u - 1)
                        dve.tensor_tensor(qk_f[u % 2][:, :, :], two(bank[u % 4][:, :]), twice(rstd), ALU.mult).then_inc(qkf_made, 1)
                    if j == 17:
                        dve.wait_ge(qkrms_made, 1)
                        own(dve.reciprocal(qk_rstd[:, :, :], qk_rms[:, :, :]))
                        dve.tensor_scalar(qk_rstd[:, :, 0:8], qk_rstd[:, :, 0:8], float(P) ** -0.5, None, ALU.mult).then_inc(qkrstd_made, 1)
                    if j >= 16 and j % 2:
                        u = (j - 16) // 2
                        dve.wait_ge(half_used, half0 + j + 1)
                        for b in range(2):
                            last = dve.tensor_scalar(v_s[:, b, T * u:T * u + T], two(bank[u % 4][:, :])[:, b, :], rstd_tok[:, b:b + 1],
                                                     None, ALU.mult)
                            if b == 0:
                                steps[0] += 1
                                last.then_inc(dve_step, 1)
                        last.then_inc(proj_read, 1)
                dve.wait_ge(tabs_in, 16 * (2 * ("nsa" in sub_n) + 1))
                for u in range(4):
                    dve.wait_ge(krs_made, u + 1)
                    dve.wait_ge(turned, turn_n["moba"] + 4 + u + 1)
                    k = qk_s[:, 8 + 2 * u:10 + 2 * u, :]
                    dve.tensor_tensor(k, k, two(bank[u][:, :]), ALU.mult).then_inc(k_scaled, 1)
                attention(Attention("moba"))
                project(ph, half0 + 24, 1)

            def s5_turns():
                a_re, a_im, log_dt = (s5_par[:, ST * i:ST * i + ST] for i in range(3))
                magic = 12582912.0
                dve.wait_ge(s5_par_in, 16)
                exp_tiny(s5_tmp[:, :], log_dt, ST)
                own(dve.tensor_tensor(s5_turn[:, :], a_re, s5_tmp[:, :], ALU.mult))
                exp_tiny(s5_mag[:, :], s5_turn[:, :], ST)
                own(dve.tensor_tensor(s5_turn[:, :], a_im, s5_tmp[:, :], ALU.mult))
                own(dve.tensor_scalar(s5_den[:, :], s5_turn[:, :], float(1 / (2 * np.pi)), None, ALU.mult))
                own(dve.tensor_scalar(s5_tmp[:, :], s5_den[:, :], magic, magic, ALU.add, ALU.subtract))
                own(dve.tensor_tensor(s5_turn[:, :], s5_den[:, :], s5_tmp[:, :], ALU.subtract))
                own(dve.tensor_scalar(s5_turn_hi[:, :], s5_turn[:, :], magic / 65536, magic / 65536, ALU.add, ALU.subtract))
                own(dve.tensor_tensor(s5_turn_lo[:, :], s5_turn[:, :], s5_turn_hi[:, :], ALU.subtract))
                own(dve.tensor_scalar(s5_tmp[:, :], s5_turn[:, :], -1.0, None, ALU.mult))
                own(dve.tensor_tensor(s5_tmp[:, :], s5_tmp[:, :], s5_turn[:, :], ALU.max))
                own(dve.tensor_tensor(s5_den[:, :], a_re, a_re, ALU.mult))
                own(dve.tensor_tensor(s5_kre[:, :], a_im, a_im, ALU.mult))
                own(dve.tensor_tensor(s5_den[:, :], s5_den[:, :], s5_kre[:, :], ALU.add))
                dve.reciprocal(s5_den[:, :], s5_den[:, :]).then_inc(turn_made, 1)

            def s5_coefs():
                a_re, a_im = (s5_par[:, ST * i:ST * i + ST] for i in range(2))
                dve.wait_ge(lam_made, 2)
                dve.wait_ge(turn_made, 1)
                re, im, x, y = s5_cos[:, :], s5_sin[:, :], s5_kre[:, :], s5_kim[:, :]
                own(dve.tensor_tensor(re, re, s5_mag[:, :], ALU.mult))
                own(dve.tensor_scalar(re, re, -1.0, None, ALU.add))
                own(dve.tensor_tensor(im, im, s5_mag[:, :], ALU.mult))
                own(dve.tensor_tensor(x, re, a_re, ALU.mult))
                own(dve.tensor_tensor(s5_tmp[:, :], im, a_im, ALU.mult))
                own(dve.tensor_tensor(x, x, s5_tmp[:, :], ALU.add))
                own(dve.tensor_tensor(x, x, s5_den[:, :], ALU.mult))
                own(dve.tensor_tensor(y, im, a_re, ALU.mult))
                own(dve.tensor_tensor(s5_tmp[:, :], re, a_im, ALU.mult))
                own(dve.tensor_tensor(y, y, s5_tmp[:, :], ALU.subtract))
                dve.tensor_tensor(y, y, s5_den[:, :], ALU.mult).then_inc(coef_made, 1)

            def s5_phase(ph):
                half0 = 2 * ph["u0"]
                iota = s5_par[:, 3 * ST:3 * ST + T]
                magic = 12582912.0

                def several(instructions):
                    for x in instructions:
                        steps[0] += 1
                        x.then_inc(dve_step, 1)
                    dve.wait_ge(dve_step, steps[0])

                def turns(kt):
                    tab = table[kt % 4]
                    r, k = tab[:, :, 0, :], tab[:, :, 1, :]
                    dve.wait_ge(yout_made, 2 * (kt - 4) + 2)
                    several(dve.tensor_scalar(k[:, a, :], iota, s5_turn[:, 4 * kt + a:4 * kt + a + 1], magic, ALU.mult, ALU.add) for a in range(4))
                    own(dve.tensor_scalar(k, k, magic, None, ALU.subtract))
                    several(dve.scalar_tensor_tensor(r[:, a, :], iota, s5_turn_hi[:, 4 * kt + a:4 * kt + a + 1], k[:, a, :],
                                                     ALU.mult, ALU.subtract) for a in range(4))
                    several(dve.scalar_tensor_tensor(r[:, a, :], iota, s5_turn_lo[:, 4 * kt + a:4 * kt + a + 1], r[:, a, :],
                                                     ALU.mult, ALU.add) for a in range(4))
                    dve.tensor_scalar(r, r, 0.5, -0.5, ALU.min, ALU.max).then_inc(turns_dve, 1)

                def cos_of(n):
                    kt, q = divmod(n, 2)
                    return table[kt % 4][:, 2 * q:2 * q + 2, 1, :][:, :, None, :].broadcast_to([P, 2, 2, T])

                def skip(kt):
                    dve.wait_ge(c_done, 2 * kt + 2)
                    dve.scalar_tensor_tensor(u_s[:, kt, :], u_s[:, kt, :], gain("s5_d", kt), bank[(7, 4)[kt % 2]][:, 0:T],
                                             ALU.mult, ALU.add).then_inc(skip_made, 1)

                def lo_of_g(run):
                    a, b = G_RUNS[run]
                    dve.wait_ge(ghi_made, run + 1)
                    dve.tensor_tensor(hg_lo[:, a:b, :], u_s[:, a:b, :], hg_hi[:, a:b, :].bitcast(F32), ALU.subtract).then_inc(glo_made, 1)

                for n in range(17):
                    if n % 4 == 0 and n < 16:
                        u = n // 4
                        split_lo(half0 + n // 2 + SPLIT)
                        if n == 0:
                            invert(ph["norm"])
                        dve.wait_ge(half_used, half0 + 2 * u + 2)
                        dve.tensor_tensor(u_s[:, 2 * u:2 * u + 2, :], two(bank[5 + u % 2][:, :]), twice(rstd), ALU.mult).then_inc(u_made, 1)
                        split_lo(half0 + n // 2 + 1 + SPLIT)
                    if n < 16:
                        dve.wait_ge(bu_kept, 2 * n + 2)
                        if n % 2 == 0:
                            dve.wait_ge(table_made, 2 * (n // 2) + 2)
                        if n == 0:
                            dve.wait_ge(c_made, 2)
                        if n >= 3:
                            dve.wait_ge(c_done, n - 2)
                        dve.tensor_tensor(ring_x[n % 3][:, :, :, :], bu_s[:, :, :, :], cos_of(n), ALU.mult).then_inc(xin_made, 1)
                    if n >= 1:
                        m = n - 1
                        x, y = ring_x[m % 3], ring_y[m % 3]
                        dve.wait_ge(yin_made, m + 1)
                        dve.wait_ge(xin_made, m + 1)
                        several([dve.tensor_tensor(x[:, :, 0, :], x[:, :, 0, :], y[:, :, 1, :], ALU.add),
                                 dve.tensor_tensor(x[:, :, 1, :], x[:, :, 1, :], y[:, :, 0, :], ALU.subtract)])
                        for c in range(2):
                            j = 2 * m + c
                            for part in range(2):
                                dve.tensor_tensor_scan(x[:, c, part, :], s5_mag[:, j:j + 1].broadcast_to([P, T]), x[:, c, part, :],
                                                       0.0, ALU.mult, ALU.add).then_inc(z_made, 1)
                        dve.wait_ge(z_made, 4 * m + 4)
                        dve.tensor_tensor(y[:, :, :, :], x[:, :, :, :], cos_of(m), ALU.mult).then_inc(xout_made, 1)
                    if n % 2 and n >= 5:
                        skip((n - 5) // 2)
                    if n % 2 == 0 and 4 <= n < 12:
                        turns(4 + (n - 4) // 2)
                skip(6)
                skip(7)
                lo_of_g(0)
                lo_of_g(1)
                lo_of_g(2)
                for u in range(4):
                    dve.wait_ge(glu_sig, u + 1)
                    uu = u_s[:, 2 * u:2 * u + 2, :]
                    dve.tensor_tensor(uu, uu, bu_s[:, u % 2, :, :], ALU.mult).then_inc(gated, 1)
                    split_lo(half0 + 8 + 2 * u + SPLIT)
                    split_lo(half0 + 9 + 2 * u + SPLIT)
                    dve.wait_ge(outhi_made, u + 1)
                    dve.tensor_tensor(out_lo[:, 2 * u:2 * u + 2, :], uu, out_hi[:, 2 * u:2 * u + 2, :].bitcast(F32), ALU.subtract)\
                       .then_inc(outlo_made, 1)
                project(ph, half0 + 16, 1)
            dve.wait_ge(x_in, 16)
            dve.wait_ge(consts_in, 16)
            for m in range(KT):
                make_hg_lo(phases[0]["gain"], 0, m)
            for half in range(SPLIT):
                split_lo(half)
            if phase_of("rglru"):
                softplus_lambda()
            if phase_of("s5") and not s5_early():
                s5_turns()
                s5_coefs()
            for ph in phases:
                if ph["kind"] == "ffn":
                    ffn_phase(ph)
                elif ph["kind"] == "final":
                    invert(ph["norm"])
                    for m in range(KT):
                        dve.scalar_tensor_tensor(h[:, m, :], h[:, m, :], gain("final", m), rstd[:, :],
                                                 ALU.mult, ALU.mult).then_inc(h_written, 1)
                        if ph["next"] and m:
                            make_hg_lo(ph["next"], ph["next_hg"], m - 1)
                    if ph["next"]:
                        make_hg_lo(ph["next"], ph["next_hg"], KT - 1)
                elif ph["kind"] == "rglru":
                    rglru_phase(ph)

                elif ph["kind"] == "nsa":
                    nsa_phase(ph)
                elif ph["kind"] == "moba":
                    moba_phase(ph)
                elif ph["kind"] == "s5":
                    s5_phase(ph)

        @block.tensor
        def _(pe):
            def three_passes(psum, w_hi_ap, w_lo_ap, x_hi_ap, x_lo_ap, first, last, **kw):
                pe.matmul(psum, w_hi_ap, x_hi_ap, start=first, stop=False, **kw)
                pe.matmul(psum, w_hi_ap, x_lo_ap, start=False, stop=False, **kw)
                return pe.matmul(psum, w_lo_ap, x_hi_ap, start=False, stop=last, **kw)

            def weights(half, it=0):
                pe.wait_ge(lo_made, half + 1 + 2 * BODY * it)
                return w_hi[half % SPLIT], w_lo[half % SPLIT]

            def mean_square(norm):
                pe.wait_ge(sumsq_made, norm + 1)
                if norm == 0:
                    pe.wait_ge(pool_const, 2)
                pe.matmul(bank[NORM_BANK][:, 0:T], ones_d[:, :], sumsq[:, :], start=True, stop=True).then_inc(ms_made, 1)

            def from_hg(half, psum, it=0, hg=None, cols=P):
                hi, lo = weights(half, it)
                for k in range(KT):
                    if hg is not None:
                        pe.wait_ge(hg_made, KT * hg + k + 1)
                    last = three_passes(psum, hi[:, k * cols:(k + 1) * cols], lo[:, k * cols:(k + 1) * cols],
                                        hg_hi[:, k, :], hg_lo[:, k, :], k == 0, k == KT - 1)
                last.then_inc(half_used, 1)

            def project(ph, half0, halves, per_half, x_hi, x_lo, ready):
                for m in range(KT):
                    if m >= 2:
                        pe.wait_ge(h_written, h_count(ph["hw"], m - 2))
                    k = 0
                    for j in range(halves):
                        hi, lo = weights(half0 + m * halves + j)
                        for q in range(per_half):
                            if m == 0:
                                ready(k)
                            last = three_passes(bank[2 + m % 2][:, 0:T], hi[:, q * P:(q + 1) * P], lo[:, q * P:(q + 1) * P],
                                                x_hi(k), x_lo(k), k == 0, k == halves * per_half - 1)
                            k += 1
                        last.then_inc(half_used, 1)

            def ffn_phase(ph):
                half0 = 2 * ph["u0"]
                pairs0 = PAIRS * ph["f"]

                def pair(p, it=0):
                    half = half0 + 4 * p
                    for side in range(2):
                        psum = bank[2 * (p % 2) + side]
                        if p:
                            done = pairs0 + p - 1 + 2 * it
                            pe.wait_ge(up_scaled if side else gate_scaled, done)
                        for c in range(2):
                            from_hg(half + 2 * side + c, psum[:, c * T:(c + 1) * T], it,
                                    hg=ph["hg"] if p == 0 and side == 0 and c == 0 else None)
                        if p == 0 and side == 0:
                            mean_square(ph["norm"])

                pair(0)
                with pe.Fori(0, 5) as it:
                    pair(1, it)
                    pair(2, it)

                half1 = half0 + 4 * PAIRS

                def down(m, it=0):
                    if m >= 2:
                        pe.wait_ge(h_written, h_count(ph["hw"], m - 2) + 2 * it)
                    for j in range(2):
                        half = half1 + 2 * m + j
                        pe.wait_ge(lo_made, half + 1 + 4 * it)
                        hi, lo = w_hi[half % SPLIT], w_lo[half % SPLIT]
                        for q in range(FT // 2):
                            k = j * (FT // 2) + q
                            if m == 0 and k % 2 == 0:
                                pe.wait_ge(hid_made, pairs0 + k // 2 + 1)
                            last = three_passes(bank[2 + m % 2][:, 0:T], hi[:, q * P:(q + 1) * P], lo[:, q * P:(q + 1) * P],
                                                hid_hi[:, k * T:(k + 1) * T], hid_lo[:, k * T:(k + 1) * T],
                                                k == 0, k == FT - 1)
                        last.then_inc(half_used, 1)

                down(0)
                down(1)
                with pe.Fori(0, 3) as it:
                    down(2, it)
                    down(3, it)

            def rglru_phase(ph):
                half0 = 2 * ph["u0"]

                def gates(g):
                    pe.wait_ge(xc_made, g + 1)
                    if g == 0:
                        pe.wait_ge(gate_w_in, 16)
                    else:
                        pe.wait_ge(sigm_made, 2 * GT * g)
                    slot = GT * (g % 2)
                    for side in range(2):
                        for m in range(GT):
                            n = side * GT + m
                            psum = bank[5 + n // 2][:, n % 2 * T:(n % 2 + 1) * T]
                            tiles = [(i, k) for i, (k, mm) in enumerate(BD_TILES) if mm == m]
                            for i, k in tiles:
                                last = pe.matmul(psum, gate_w[:, (side * 4 + g) * 7 + i, :], xc[:, slot + k, :],
                                                 start=(i, k) == tiles[0], stop=(i, k) == tiles[-1])
                    last.then_inc(gates_done, 1)

                for j in range(2 * RT):
                    u = j // 2
                    if j % 2 == 0 and u >= 4:
                        if u - 4 < RT // 2:
                            pe.wait_ge(y_scaled, u - 3)
                        else:
                            pe.wait_ge(xb_made, u - 3 - RT // 2)
                    from_hg(half0 + j, bank[u % 4][:, j % 2 * T:(j % 2 + 1) * T], hg=ph["hg"] if j == 0 else None)
                    if j == 1:
                        mean_square(ph["norm"])
                    if j >= RT + 2 * GT - 1 and (j - RT - 2 * GT + 1) % GT == 0:
                        gates((j - RT - 2 * GT + 1) // GT)
                gates(3)
                project(ph, half0 + 2 * RT, 2, 6, lambda k: rec_hi[:, k, :], lambda k: rec_lo[:, k, :],
                        lambda k: pe.wait_ge(rec_made, k // GT + 1))

            def mean_square_by_token(norm):
                pe.wait_ge(sumsq_made, norm + 1)
                if norm == 0:
                    pe.wait_ge(pool_const, 2)
                pe.matmul(bank[NORM_BANK][:, 0:T], ones_d[:, :], sumsq[:, :], start=True, stop=True)
                for b in range(2):
                    last = pe.matmul(bank[NORM_BANK][:, T + b:T + b + 1], sumsq[:, P * b:P * b + P], ones_d[:, 0:1], start=True, stop=True)
                last.then_inc(ms_made, 1)

            def token_major(half, psum, cols, x_hi, x_lo):
                hi, lo = weights(half)
                for b in range(2):
                    t = slice(P * b, P * b + P)
                    for k in range(KT):
                        w = slice(k * cols, (k + 1) * cols)
                        pe.matmul(psum[b], x_hi[:, k, t], hi[:, w], start=k == 0, stop=False)
                        pe.matmul(psum[b], x_lo[:, k, t], hi[:, w], start=False, stop=False)
                        last = pe.matmul(psum[b], x_hi[:, k, t], lo[:, w], start=False, stop=k == KT - 1)
                last.then_inc(half_used, 1)

            def attention(att, score, pv, first_waits):
                def scores(n):
                    job, branch, group, b, keys = att.step(n)
                    if n >= 2:
                        pe.wait_ge(negmax, att.step0 + n - 1)
                    for i in range(4):
                        q, k = score(branch, 4 * group + i, b)
                        last = pe.matmul(att.score_bank(n, i, keys), q, k[:, 0:keys], start=True, stop=True)
                    last.then_inc(scores_done, 1)

                def turn(n):
                    job, branch, group, b, keys = att.step(n)
                    pe.wait_ge(prob_made, att.step0 + n + 1)
                    if n >= 1:
                        pe.wait_ge(prob_kept, kept_at(att, n))
                    for kt in range(b + 1):
                        for i in range(4):
                            last = pe.transpose(bank[5 + kt][:, P * i:P * i + P], att.prob[n % 3][:, i, P * kt:P * kt + P], att.ident)
                    last.then_inc(prob_turned, 1)

                def outputs(job):
                    group, b = divmod(job, 2)
                    pe.wait_ge(prob_kept, kept_at(att, (job + 1) * att.branches))
                    if job >= 2:
                        pe.wait_ge(o_made, att.job0 + job - 1)
                    psum = bank[(7, 4)[job % 2]]
                    for i in range(4):
                        last = pv(psum, group, b, i)
                    last.then_inc(pv_done, 1)

                def kept_at(att, n):
                    return kept0[0] + sum(att.step(x)[3] + 1 for x in range(n))

                first_waits()
                scores(0)
                scores(1)
                for n in range(att.steps):
                    job = n // att.branches
                    if n + 2 < att.steps:
                        scores(n + 2)
                    turn(n)
                    if n % att.branches == 0 and job >= 1:
                        outputs(job - 1)
                outputs(att.jobs - 1)
                kept0[0] = kept_at(att, att.steps)

            kept0 = [0]

            def nsa_phase(ph):
                half0 = 2 * ph["u0"]
                base = proj_n["nsa"]
                for j in range(18):
                    u = j // 2
                    if j % 2 == 0 and u >= 4:
                        pe.wait_ge(proj_read, base + u - 3)
                    if j in (4, 5):
                        from_hg(half0 + j, bank[u % 4][:, j % 2 * T:(j % 2 + 1) * T])
                    elif j < 14:
                        from_hg(half0 + j, bank[u % 4][0:96, j % 2 * T:(j % 2 + 1) * T], hg=ph["hg"] if j == 0 else None, cols=96)
                    else:
                        token_major(half0 + j, [bank[u % 4][:, T * b + P * (j % 2):T * b + P * (j % 2) + P] for b in range(2)], P, hg_hi, hg_lo)
                    if j == 1:
                        mean_square_by_token(ph["norm"])
                for j in range(18, 26):
                    hi, lo = weights(half0 + j)
                    if j == 18:
                        pe.wait_ge(proj_read, base + 9)
                        pe.wait_ge(blklo_made, 1)
                    for q in range(4):
                        tok = 4 * (j - 18) + q
                        for m in range(2):
                            w = slice(2 * P * q + P * m, 2 * P * q + P * m + P)
                            last = three_passes(bank[m][:, 0:NG * NC], hi[0:96, w], lo[0:96, w], blk_k_hi[0:96, tok, :], blk_k_lo[0:96, tok, :],
                                                tok == 0, tok == CB - 1)
                    last.then_inc(half_used, 1)
                for j in range(26, 34):
                    hi, lo = weights(half0 + j)
                    if j == 26:
                        pe.wait_ge(blklo_made, 2)
                    for q in range(4):
                        tok = 4 * (j - 26) + q
                        for m in range(2):
                            for e in range(2):
                                w = slice(2 * P * q + P * m, 2 * P * q + P * m + P)
                                rows = slice(64 * e, 64 * e + 64)
                                last = three_passes(bank[CMP_BANK[m][e]][:, 0:2 * NC], hi[rows, w], lo[rows, w], blk_v_hi[rows, tok, :],
                                                    blk_v_lo[rows, tok, :], tok == 0, tok == CB - 1)
                    last.then_inc(half_used, 1)
                for j in range(34, 50):
                    u = (j - 34) // 2
                    if j == 34:
                        pe.wait_ge(cmp_gelu, 6)
                        pe.wait_ge(hq_made, KT)
                    if j % 2 == 0 and u >= 4:
                        pe.wait_ge(proj_read, base + 9 + u - 3)
                    hi, lo = weights(half0 + j)
                    for k in range(KT):
                        last = three_passes(bank[u % 4][0:96, j % 2 * T:(j % 2 + 1) * T], hi[:, 96 * k:96 * k + 96], lo[:, 96 * k:96 * k + 96],
                                            hq_hi[:, k, :], hq_lo[:, k, :], k == 0, k == KT - 1)
                    last.then_inc(half_used, 1)
                    if j == 34:
                        for m in range(2):
                            last = pe.matmul(bank[7][0:96, 0:NG * NC], na_small[:, NA_W2K + 96 * m:NA_W2K + 96 * m + 96], hk_s[:, m, :],
                                             start=m == 0, stop=m == 1)
                        last.then_inc(cmp_done, 1)
                        pe.wait_ge(hv_copied, 32)
                        for g in range(NG):
                            for m in range(2):
                                last = pe.matmul(bank[6][:, 64 * g:64 * g + 64], hv_rep[:, m, g, :],
                                                 na_small[:, NA_W2V + 64 * m:NA_W2V + 64 * m + 64], start=m == 0, stop=m == 1)
                        last.then_inc(cmp_done, 1)
                for c in range(2):
                    token_major(half0 + 50 + c, [bank[4][:, 48 * b + 24 * c:48 * b + 24 * c + 24] for b in range(2)], 24, hq_hi, hq_lo)
                pe.wait_ge(cmp_kept, 5)
                pe.wait_ge(proj_read, base + 17)
                for b in range(2):
                    for hd in range(NH):
                        g = hd // 4
                        last = pe.matmul(bank[7][:, NC * (NH * b + hd):NC * (NH * b + hd + 1)], q_s[0:96, hd, P * b:P * b + P],
                                         kc_s[0:96, NC * g:NC * g + NC], start=True, stop=True)
                last.then_inc(sc_done, 1)
                att = Attention("nsa")
                pe.wait_ge(tabs_in, 32)
                pe.wait_ge(pc_made, 1)
                for b in range(2):
                    for g in range(NG):
                        last = pe.transpose(bank[5 + b][:, P * g:P * g + P], score_c[:, b, 4 * g:4 * g + 4, :].rearrange("p h n -> p (h n)"), att.ident)
                    last.then_inc(pc_turned, 1)

                def score(branch, hd, b):
                    return qr_s[0:96, hd, P * b:P * b + P], (ks_s, kw_s)[branch][0:96, hd // 4, :]

                def pv(psum, group, b, i):
                    out_ap = psum[64 * (i % 2):64 * (i % 2) + 64, P * (i // 2):P * (i // 2) + P]
                    for branch in range(2):
                        v = (v_sel, v_win)[branch]
                        for kt in range(b + 1):
                            pe.matmul(out_ap, v[:, kt, 64 * group:64 * group + 64], att.prob_t[branch][:, kt, i, :],
                                      start=branch == 0 and kt == 0, stop=False)
                    return pe.matmul(out_ap, vc_s[:, group, i, :], prob_c[:, b, group, :], start=False, stop=True)

                def first_waits():
                    pe.wait_ge(turned, turn_n["nsa"] + 12)
                    pe.wait_ge(pc_kept, 2)

                attention(att, score, pv, first_waits)
                project(ph, half0 + 52, 1, 8, lambda k: hq_hi[:, k, :], lambda k: hq_lo[:, k, :],
                        lambda k: pe.wait_ge(o_made, job_n["nsa"] + 2 * (k // 2) + 2))

            def moba_phase(ph):
                half0 = 2 * ph["u0"]

                def mean_of_heads(u):
                    pe.wait_ge(qksq_made, u + 1)
                    for c in range(2):
                        for b in range(2):
                            n = 16 * b + 2 * u + c
                            last = pe.matmul(bank[5][:, n:n + 1], qk_sq[u % 2][:, c, P * b:P * b + P], ones_d[:, 0:1], start=True, stop=True)
                    last.then_inc(qkms_made, 1)

                for j in range(16):
                    u = j // 2
                    if j % 2 == 0 and u >= 4:
                        pe.wait_ge(qkf_made, u - 3)
                    from_hg(half0 + j, bank[u % 4][:, j % 2 * T:(j % 2 + 1) * T], hg=ph["hg"] if j == 0 else None)
                    if j == 1:
                        mean_square_by_token(ph["norm"])
                    if j % 2 and u >= 1:
                        mean_of_heads(u - 1)
                for j in range(16, 24):
                    u = (j - 16) // 2
                    if j % 2 == 0:
                        pe.wait_ge(qkf_made, 4 + u + 1)
                    token_major(half0 + j, [bank[u % 4][:, T * b + P * (j % 2):T * b + P * (j % 2) + P] for b in range(2)], P, hg_hi, hg_lo)
                    if j == 16:
                        mean_of_heads(7)
                att = Attention("moba")
                pe.wait_ge(tabs_in, 16 * (2 * ("nsa" in sub_n) + 1))
                pe.wait_ge(qkrstd_made, 1)
                pe.wait_ge(proj_read, proj_n["moba"] + 4)
                for u in range(4):
                    for c in range(2):
                        for b in range(2):
                            r = qk_rstd[:, b, 8 + 2 * u + c:9 + 2 * u + c].broadcast_to([P, P])
                            last = pe.matmul(bank[u][:, T * c + P * b:T * c + P * b + P], r, att.ident, start=True, stop=True)
                    last.then_inc(krs_made, 1)

                def score(branch, hd, b):
                    return qk_s[:, hd, P * b:P * b + P], qk_s[:, 8 + hd, :]

                def pv(psum, group, b, i):
                    hd = 4 * group + i
                    job = 2 * group + b
                    for kt in range(b + 1):
                        last = pe.matmul(psum[:, P * i:P * i + P], v_s[:, kt, P * hd:P * hd + P], att.prob_t[job % 2][:, kt, i, :],
                                         start=kt == 0, stop=kt == b)
                    return last

                attention(att, score, pv, lambda: pe.wait_ge(k_scaled, 4))
                project(ph, half0 + 24, 1, 8, lambda k: mo_o_hi[:, k, :], lambda k: mo_o_lo[:, k, :],
                        lambda k: pe.wait_ge(o_made, job_n["moba"] + 2 * (k // 4) + 2))

            def s5_phase(ph):
                half0 = 2 * ph["u0"]

                def b_products(n):
                    kt, q = divmod(n, 2)
                    pe.wait_ge(u_made, kt // 2 + 1)
                    pe.wait_ge(bt_in[kt % 4], 16 * (kt // 4 + 1))
                    if n >= 2:
                        pe.wait_ge(bu_kept, 2 * (n - 2) + 2)
                    for c in range(2):
                        rows = slice(32 * (2 * q + c), 32 * (2 * q + c) + 32)
                        for part in range(2):
                            last = pe.matmul(bank[2 * q + c][:, T * part:T * part + T], bt_s[kt % 4][rows, part, :], u_s[rows, kt, :],
                                             start=True, stop=True)
                    last.then_inc(b_done, 1)

                def c_products(n):
                    kt, q = divmod(n, 2)
                    x, y = ring_x[n % 3], ring_y[n % 3]
                    if n == 0:
                        pe.wait_ge(c_made, 2)
                    if n % 2 == 0 and n >= 4:
                        pe.wait_ge(skip_made, kt - 1)
                    for step, (src, sems, terms) in enumerate((
                            (y, xout_made, ((0, 0), (1, 1))),
                            (x, yout_made, ((0, 1), (1, 2))))):
                        pe.wait_ge(sems, n + 1)
                        for c in range(2):
                            j = 2 * n + c
                            rows = slice(32 * (2 * q + c), 32 * (2 * q + c) + 32)
                            for part, w in terms:
                                last = pe.matmul(bank[(7, 4)[kt % 2]][rows, 0:T], c_s[:, w, j, :], src[:, c, part, :],
                                                 start=step == 0 and part == 0, stop=step == 1 and part == 1)
                    last.then_inc(c_done, 1)

                for n in range(16):
                    if n % 4 == 0:
                        u = n // 4
                        for c in range(2):
                            if c == 0 and u >= 2:
                                pe.wait_ge(u_made, u - 1)
                            from_hg(half0 + 2 * u + c, bank[5 + u % 2][:, c * T:(c + 1) * T], hg=ph["hg"] if u == 0 and c == 0 else None)
                        if u == 0:
                            mean_square(ph["norm"])
                    b_products(n)
                    if n >= 2:
                        c_products(n - 2)
                c_products(14)
                c_products(15)
                for u in range(4):
                    for c in range(2):
                        hi, lo = weights(half0 + 8 + 2 * u + c)
                        for k in range(KT):
                            if u == 0 and c == 0:
                                pe.wait_ge(glo_made, 1 + sum(k >= b for a, b in G_RUNS))
                            last = three_passes(bank[u][:, c * T:(c + 1) * T], hi[:, k * P:(k + 1) * P], lo[:, k * P:(k + 1) * P],
                                                hg_hi[:, k, :], hg_lo[:, k, :], k == 0, k == KT - 1)
                        last.then_inc(half_used, 1)
                pe.wait_ge(glu_sig, 4)
                project(ph, half0 + 16, 1, 8, lambda k: out_hi[:, k, :], lambda k: out_lo[:, k, :],
                        lambda k: pe.wait_ge(outlo_made, k // 2 + 1))
            for ph in phases:
                if ph["kind"] == "ffn":
                    ffn_phase(ph)
                elif ph["kind"] == "final":
                    mean_square(ph["norm"])
                elif ph["kind"] == "rglru":
                    rglru_phase(ph)

                elif ph["kind"] == "nsa":
                    nsa_phase(ph)
                elif ph["kind"] == "moba":
                    moba_phase(ph)
                elif ph["kind"] == "s5":
                    s5_phase(ph)


def units_8(w):
    n = w.shape[1]
    return w.reshape(KT, P, n // 256, 2, P).transpose(2, 1, 3, 0, 4).reshape(n // 256, P, 2 * KT * P)


def units_k(w):
    kt = w.shape[0] // P
    return w.reshape(kt, P, D // P, P).transpose(2, 1, 0, 3).reshape(D // P, P, kt * P)


def units_cols(w, cols):
    n = w.shape[1]
    return w.reshape(KT, P, n // (2 * cols), 2, cols).transpose(2, 1, 3, 0, 4).reshape(n // (2 * cols), P, 2 * KT * cols)


def gate_up(gate, up):
    return np.stack([units_8(gate), units_8(up)], axis=1).reshape(-1, P, 2 * KT * P)


def columns(v):
    return v.reshape(-1, P).T


def block_diagonal(matrices):
    tiles = []
    for w in matrices:
        for g in range(4):
            full = np.zeros((3 * P, 3 * P), w.dtype)
            for b in range(4):
                full[96 * b:96 * b + 96, 96 * b:96 * b + 96] = w[4 * g + b]
            for k, m in [(0, 0), (1, 0), (0, 1), (1, 1), (2, 1), (1, 2), (2, 2)]:
                tiles.append(full[P * k:P * k + P, P * m:P * m + P])
    return np.stack(tiles, axis=1)


def rotary_table(rows, half):
    inv = np.power(np.float32(500000.0), -np.arange(half, dtype=np.float32) * np.float32(2.0) / np.float32(2 * half))
    ang = (np.arange(T, dtype=np.float32)[None, :] * inv[:, None].astype(np.float32)).astype(np.float64)
    cos, sin = np.cos(ang), np.sin(ang)
    out = np.zeros((rows, 2 * T), np.float32)
    out[:2 * half, :T] = np.concatenate([cos, cos])
    out[:2 * half, T:] = np.concatenate([-sin, sin])
    return out


def shape_tables():
    masked = np.float32(-1e30)
    q = np.arange(P)
    causal = np.zeros((P, T), np.float32)
    causal[:, P:] = np.where(q[None, :] <= q[:, None], np.float32(0), masked)
    ident = np.eye(P, dtype=np.float32)
    ends = np.arange(NC) * CS + CB - 1
    blocks = [np.where(ends[None, :] <= (q + P * b)[:, None], np.float32(0), masked) for b in range(2)]
    na_tab = np.concatenate([rotary_table(P, 12), causal, ident, *blocks], axis=1).astype(np.float32)
    mo_tab = np.concatenate([rotary_table(P, 16), causal, ident], axis=1).astype(np.float32)
    return na_tab, mo_tab


def rows_padded(a, rows=P):
    return np.concatenate([a, np.zeros((rows - a.shape[0],) + a.shape[1:], a.dtype)])


def compression(w, dims, copies):
    w = w.reshape(4, 8, dims, T).transpose(0, 2, 1, 3)
    w = np.concatenate([w] * copies, axis=1)
    if w.shape[1] < P:
        w = np.concatenate([w, np.zeros((4, P - w.shape[1], 8, T), w.dtype)], axis=1)
    return w.reshape(4, P, 8 * T)


def lay_out(i):
    gk, gv = NG * 96, NG * 64
    kv = i["kv_w"]
    k_cmp, v_cmp, k_sel, v_sel, k_win, v_win = np.split(kv, np.cumsum([gk, gv, gk, gv, gk]), axis=1)
    w_in = i["a_w_in"][0]
    w_q = i["b_w_q"][0]
    ffn_gu = [(w[:, :FF], w[:, FF:]) for w in i["ffn_w_gu"]]
    ffn_2 = [(i["ffn_w_gate_2"][a, b], i["ffn_w_up_2"][a, b]) for a in range(2) for b in range(2)]
    qkv = i["moba_w_qkv_2"][0]
    arrays = {
        "x": i["x"][0].T.reshape(KT, P, T).transpose(1, 0, 2),
        "w8": np.concatenate([
            units_8(np.concatenate([w_in[:, RT * P:], w_in[:, :RT * P]], axis=1)),
            gate_up(*ffn_gu[0]),
            units_8(v_cmp), units_8(v_sel), units_8(v_win),
            compression(i["cmp_w1_k"], 96, 1), compression(i["cmp_w1_v"], 64, 2),
            units_8(i["b_w_o"][0]),
            gate_up(*ffn_gu[1]),
            gate_up(*ffn_2[0]),
            units_8(i["s5_w_in_2"][0]), units_8(i["s5_w_glu_2"][0]), units_8(i["s5_w_out_2"][0]),
            gate_up(*ffn_2[1]), gate_up(*ffn_2[2]),
            units_8(qkv), units_8(i["moba_w_out_2"][0]),
            gate_up(*ffn_2[3])]),
        "w22": np.concatenate([units_k(w) for w in [*i["ffn_w_down"], *i["ffn_w_down_2"].reshape(4, FF, D)]]),
        "w12": units_k(i["a_w_out"][0]),
        "q96": np.concatenate([units_cols(w, 96) for w in (k_cmp, k_sel, k_win, w_q[:, :NH * 96])]),
        "gate": units_cols(w_q[:, NH * 96:], 24),
        "gate_w": block_diagonal([i["a_w_ra"][0], i["a_w_ix"][0]]),
    }
    vectors = {
        "norm_00": i["norm_g"][0, 0], "norm_01": i["norm_g"][0, 1], "norm_10": i["norm_g"][1, 0],
        "norm_11": i["norm_g"][1, 1], "kv": i["kv_norm_g"], "final": i["final_g"],
        "ffn_00": i["ffn_norm_2"][0, 0], "ffn_01": i["ffn_norm_2"][0, 1], "ffn_10": i["ffn_norm_2"][1, 0],
        "ffn_11": i["ffn_norm_2"][1, 1], "mix_0": i["mix_norm_2"][0], "mix_1": i["mix_norm_2"][1],
        "s5_d": i["s5_d_2"][0], "conv_b": i["a_conv_b"][0], "lam": i["a_lambda"][0],
        "b_ra": i["a_b_ra"][0], "b_ix": i["a_b_ix"][0], "q_gain": i["moba_q_norm_2"][0],
        "k_gain": i["moba_k_norm_2"][0], **{f"conv_{j}": i["a_conv_w"][0, j] for j in range(4)},
    }
    arrays["vec"] = np.concatenate([columns(vectors[name]) for name in VEC], axis=1)
    arrays["na_tab"], arrays["mo_tab"] = shape_tables()
    arrays["na_small"] = np.concatenate([
        rows_padded(i["cmp_pos_k"].T), np.concatenate([i["cmp_pos_v"].T] * 2),
        i["cmp_w2_k"].reshape(2, P, 96).transpose(1, 0, 2).reshape(P, 192),
        i["cmp_w2_v"].reshape(2, P, 64).transpose(1, 0, 2).reshape(P, 128),
        np.broadcast_to(i["b_gate_bias"][0], (P, 48))], axis=1)
    def by_state(a):
        return a.reshape(ST, P).T

    def block_pairs(a):
        out = np.zeros((ST, 2, 64, 2, 16), a.dtype)
        a = a.reshape(ST, 2, 64, 16)
        for g in range(2):
            out[:, g, :, g, :] = a[:, g]
        return out

    log_dt = np.repeat(i["s5_log_dt_2"][0], 64)
    arrays["s5_par"] = np.concatenate([
        by_state(i["s5_a_re_2"][0]), by_state(i["s5_a_im_2"][0]), by_state(log_dt),
        np.broadcast_to(np.arange(T, dtype=np.float32), (P, T))], axis=1)
    arrays["s5_b"] = np.stack([
        block_pairs(i[k][0]).reshape(KT, 4, P, 32).transpose(1, 3, 0, 2).reshape(P, KT, P)
        for k in ("s5_b_re_2", "s5_b_im_2")], axis=2)
    arrays["s5_c"] = np.stack([
        block_pairs(i[k][0].transpose(0, 2, 1)).reshape(ST, P, 32).transpose(1, 0, 2).reshape(P, 2, 2, T)
        for k in ("s5_c_re_2", "s5_c_im_2")], axis=1)
    return {k: np.ascontiguousarray(v) for k, v in arrays.items()}


def kernel(**inputs):
    import concourse.bacc as bacc
    from concourse.bass_utils import run_bass_kernel_spmd

    arrays = {f"in_{k}": v for k, v in lay_out({k: np.asarray(v) for k, v in inputs.items()}).items()}
    nc = bacc.Bacc("TRN2", target_bir_lowering=False, num_devices=1)
    ins = {k[3:]: nc.dram_tensor(k, v.shape, mybir.dt.from_np(v.dtype), kind="ExternalInput").ap()
           for k, v in arrays.items()}
    out = nc.dram_tensor("out_h", (P, KT, T), F32, kind="ExternalOutput").ap()
    two_blocks(nc, ins, out, layer_plan())
    result = run_bass_kernel_spmd(nc, [arrays], core_ids=[0]).results[0]["out_h"]
    return result.transpose(1, 0, 2).reshape(D, T).T[None]
```

```python
from contextlib import ExitStack

import numpy as np
import concourse.bass as bass
import concourse.mybir as mybir

ALU = mybir.AluOpType
ACT = mybir.ActivationFunctionType
AX = mybir.AxisListType
F32 = mybir.dt.float32
F32R = mybir.dt.float32r
I32 = mybir.dt.int32

P = 128
T = 256
D = 1024
KT = D // P
FF = 2816
FT = FF // P
PAIRS = FT // 2
EPS = 1e-6
RT = 12
GT = 3
CONV_AT = (3, 5, 10, 12)
GATES_AT = (6, 8, 12, 15)
RECUR_AT = (10, 13, 16, 19)
FINISH_AT = (17, 20, 22)
RAW = 4
SPLIT = 4
BODY = 4

NH = 16
NG = 4
CB = 32
CS = 16
NC = (T - CB) // CS + 1
NA_CMASK = 3 * T + P
NA_TAB = NA_CMASK + 2 * NC
MO_TAB = 3 * T + P
NA_V_BANKS = ((5, 6), (7, 3))
MO_V_BANKS = ((0, 1), (2, 3), (6, 7), (0, 1))
NA_W2K = 2 * CB
NA_W2V = NA_W2K + 2 * 96
NA_GATE = NA_W2V + 2 * 64
NA_SMALL = NA_GATE + 48

ST = 32
S5_PAR = 3 * ST + T
S5_PLACE = (S5_PAR + 10 * ST) * 4
TWO_PI = 6.283185

VEC = {}
for _name, _n in (("norm_00", 8), ("norm_01", 8), ("norm_10", 8), ("norm_11", 8), ("kv", 8), ("final", 8),
                  ("ffn_00", 8), ("ffn_01", 8), ("ffn_10", 8), ("ffn_11", 8), ("mix_0", 8), ("mix_1", 8),
                  ("s5_d", 8), ("conv_0", 12), ("conv_1", 12), ("conv_2", 12), ("conv_3", 12),
                  ("conv_b", 12), ("lam", 12), ("b_ra", 12), ("b_ix", 12), ("q_gain", 1), ("k_gain", 1)):
    VEC[_name] = (sum(n for _, n in VEC.values()), _n)
NVEC = sum(n for _, n in VEC.values())

HALF = {"w8": 8 * P, "w22": 11 * P, "w12": 6 * P, "q96": 8 * 96, "gate": 8 * 24}
UNIT_MAX = 2 * HALF["w22"]


def layer_plan():
    return [
        dict(kind="rglru", gain="norm_00", scale=1.0),
        dict(kind="ffn", gain="norm_01", scale=1.0),
        dict(kind="nsa", gain="kv", scale=1.0),
        dict(kind="ffn", gain="norm_11", scale=1.0),
        dict(kind="final", gain=None, scale=1.0),
        dict(kind="ffn", gain="ffn_00", scale=0.5),
        dict(kind="s5", gain="mix_0", scale=1.0),
        dict(kind="ffn", gain="ffn_01", scale=0.5),
        dict(kind="ffn", gain="ffn_10", scale=0.5),
        dict(kind="moba", gain="mix_1", scale=1.0),
        dict(kind="ffn", gain="ffn_11", scale=0.5),
    ]


UNITS = {
    "rglru": [("w8", 12), ("w12", 8)],
    "ffn": [("w8", 22), ("w22", 8)],
    "nsa": [("q96", 2), ("w8", 1), ("q96", 4), ("w8", 2), ("w8", 4), ("w8", 4), ("q96", 8), ("gate", 1), ("w8", 4)],
    "final": [],
    "s5": [("w8", 12)],
    "moba": [("w8", 16)],
}


def number_phases(phases):
    units, at = [], {k: 0 for k in HALF}
    hg = 0
    for n, ph in enumerate(phases):
        ph["u0"] = len(units)
        ph["norm"] = ph["hw"] = n
        ph["hg"] = hg if ph["gain"] else None
        hg += ph["gain"] is not None
        ph["next"] = phases[n + 1]["gain"] if n + 1 < len(phases) else None
        ph["next_hg"] = hg
        ph["last"] = n + 1 == len(phases)
        for kind, count in UNITS[ph["kind"]]:
            for _ in range(count):
                units.append((kind, at[kind]))
                at[kind] += 1
    ffns, after = [], False
    for ph in phases:
        ph["tables"] = ()
        if ph["kind"] == "ffn" and after:
            ffns.append(ph)
        after = after or ph["kind"] == "nsa"
        if ph["kind"] == "s5":
            if len(ffns) >= 2:
                ffns[0]["tables"], ffns[1]["tables"] = (4, 5, 6, 7), (0, 1, 2, 3)
            else:
                ph["tables"] = (4, 5, 6, 7, 0, 1, 2, 3)
    return units


def two_blocks(nc, ins, out, phases):
    units = number_phases(phases)
    n_halves = 2 * len(units)

    with ExitStack() as ctx:
        def sem(name):
            return ctx.enter_context(nc.semaphore(name))

        base = (nc.sbuf_base + 31) // 32 * 32
        place = [base]

        def sb(name, shape, dt=F32, at=None):
            size = int(np.prod(shape[1:])) * 4
            size = (size + 31) // 32 * 32
            if at is None:
                at = place[0]
                place[0] += size
                assert place[0] <= nc.sbuf_usable_end, (name, place[0])
            return nc.alloc_sbuf_tensor_at(name, list(shape), dt, offset=at)

        class Region:

            def __init__(self, start, end):
                self.at, self.end = start, end

            def sb(self, name, shape, dt=F32):
                size = (int(np.prod(shape[1:])) * 4 + 31) // 32 * 32
                t = sb(name, shape, dt, at=self.at)
                self.at += size
                assert self.at <= self.end, (name, self.at - self.end)
                return t

        h = sb("h", [P, KT, T])
        hg_at = place[0]
        hg_hi = sb("hg_hi", [P, KT, T], F32R)
        hg_lo = sb("hg_lo", [P, KT, T], F32R)
        raw = [sb(f"raw{r}", [P, UNIT_MAX]) for r in range(RAW)]
        w_hi = [sb(f"w_hi{s}", [P, UNIT_MAX // 2], F32R) for s in range(SPLIT)]
        w_lo = [sb(f"w_lo{s}", [P, UNIT_MAX // 2], F32R) for s in range(SPLIT)]
        vec = sb("vec", [P, NVEC])
        ones_d = sb("ones_d", [P, P])
        eps = sb("eps", [P, 1])
        sumsq = sb("sumsq", [P, T])
        square = sb("square", [P, T])
        rms = sb("rms", [P, T])
        rstd = sb("rstd", [P, T])

        sp4 = sb("sp4", [P, RT])
        tiny = [sb(f"tiny{i}", [P, 32]) for i in range(5)]
        tiny_i = sb("tiny_i", [P, 32], I32)

        sb_small = sb("sb_small", [P, 32])
        rms_tok = sb("rms_tok", [P, 2])
        rstd_tok = sb("rstd_tok", [P, 2])
        half_pi = sb("half_pi", [P, 1])

        region = (place[0], nc.sbuf_usable_end // 32 * 32)
        ffn = Region(*region)
        hid_hi = ffn.sb("hid_hi", [P, FT * T], F32R)
        hid_lo = ffn.sb("hid_lo", [P, FT * T], F32R)
        gate_s = ffn.sb("gate_s", [P, 2 * T])
        silu_s = ffn.sb("silu_s", [P, 2 * T])
        up_s = ffn.sb("up_s", [P, 2 * T])
        hid_f = ffn.sb("hid_f", [P, 2 * T])
        after_ffn = ffn.at

        bank = [nc.alloc_psum_tensor(f"bank{b}", [P, 512], F32) for b in range(8)]
        NORM_BANK = 4

        raw_loaded = [sem(f"raw_loaded{r}") for r in range(RAW)]
        hi_made = sem("hi_made")
        lo_made = sem("lo_made")
        half_used = sem("half_used")
        consts_in = sem("consts_in")
        x_in = sem("x_in")
        pool_const = sem("pool_const")
        h_written = sem("h_written")
        hghi_made = sem("hghi_made")
        hg_made = sem("hg_made")
        sq_step = sem("sq_step")
        sumsq_made = sem("sumsq_made")
        ms_made = sem("ms_made")
        rms_made = sem("rms_made")
        rstd_made = sem("rstd_made")
        gate_scaled = sem("gate_scaled")
        silu_made = sem("silu_made")
        up_scaled = sem("up_scaled")
        hidf_made = sem("hidf_made")
        hidhi_made = sem("hidhi_made")
        hid_made = sem("hid_made")
        out_sent = sem("out_sent")

        n_ffn = 0
        for ph in phases:
            if ph["kind"] == "ffn":
                ph["f"] = n_ffn
                n_ffn += 1

        def half_size(half):
            return HALF[units[half // 2][0]]

        def gain(name, m):
            return vec[:, VEC[name][0] + m:VEC[name][0] + m + 1]

        def h_count(hw, m):
            return KT * hw + m + 1

        def phase_of(kind):
            return next((ph for ph in phases if ph["kind"] == kind), None)

        BD_TILES = [(0, 0), (1, 0), (0, 1), (1, 1), (2, 1), (1, 2), (2, 2)]
        rg = Region(*region)
        y_gelu = rg.sb("y_gelu", [P, RT, T])
        xb = rg.sb("xb", [P, 2 * GT, T + 4])
        xc = rg.sb("xc", [P, 2 * GT, T])
        gate_w = rg.sb("gate_w", [P, 2 * 4 * 7, P])
        over_hi = Region(rg.at + GT * T * 4, region[1])
        rec_hi = rg.sb("rec_hi", [P, RT, T], F32R)
        rec_s = Region(rg.at, region[1]).sb("rec_s", [P, RT, T])
        rec_lo = rg.sb("rec_lo", [P, RT, T], F32R)
        r_s, i_s, root_s = ([rg.sb(f"{n}_even", [P, GT, T]), over_hi.sb(f"{n}_odd", [P, GT, T])] for n in ("r", "i", "root"))
        inv_s = rg.sb("inv_s", [P, GT, T])
        gate_w_in = sem("gate_w_in")
        pads_made = sem("pads_made")
        dve_step = sem("dve_step")
        y_scaled = sem("y_scaled")
        y_made = sem("y_made")
        xb_made = sem("xb_made")
        xc_made = sem("xc_made")
        gates_done = sem("gates_done")
        sigm_made = sem("sigm_made")
        tanh_made = sem("tanh_made")
        rroot_made = sem("rroot_made")
        ix_made = sem("ix_made")
        rec_scanned = sem("rec_scanned")
        recf_made = sem("recf_made")
        rechi_made = sem("rechi_made")
        rec_made = sem("rec_made")
        sp4_made = sem("sp4_made")

        def rec_f(g):
            slot = GT * (g % 2)
            return xb[:, slot:slot + GT, 0:T]

        na = Region(*region)
        hq_hi = na.sb("hq_hi", [P, KT, T], F32R)
        hq_lo = na.sb("hq_lo", [P, KT, T], F32R)
        early = Region(na.at, region[1])
        blk_k = early.sb("blk_k", [P, CB, NG * NC])
        blk_k_hi = early.sb("blk_k_hi", [P, CB, NG * NC], F32R)
        blk_k_lo = early.sb("blk_k_lo", [P, CB, NG * NC], F32R)
        blk_v = blk_k
        blk_v_hi = early.sb("blk_v_hi", [P, CB, NG * NC], F32R)
        blk_v_lo = early.sb("blk_v_lo", [P, CB, NG * NC], F32R)
        q_s = na.sb("q_s", [P, NH, T])
        qr_s = na.sb("qr_s", [P, NH, T])
        vc_s = na.sb("vc_s", [P, NG, 4, 64])
        na.at = max(na.at, early.at)
        early = Region(na.at, region[1])
        over_raw = Region(early.at, region[1])
        hid_t = over_raw.sb("hid_t", [NG * NC, 2, T])
        gate_f = over_raw.sb("gate_f", [48, T])
        kc_raw = early.sb("kc_raw", [P, NG, T])
        vc_raw = early.sb("vc_raw", [P, 2, T])
        swap_s = [early.sb(f"swap{i}", [P, 2, T]) for i in range(2)]
        turn_s = early.sb("turn_s", [P, 2, T])
        prob = [na.sb(f"prob{i}", [P, 4, T]) for i in range(3)]
        ks_s = na.sb("ks_s", [P, NG, T])
        kw_s = na.sb("kw_s", [P, NG, T])
        v_sel = na.sb("v_sel", [P, 2, NG * 64])
        v_win = na.sb("v_win", [P, 2, NG * 64])
        na_tab = na.sb("na_tab", [P, NA_TAB])
        na_small = na.sb("na_small", [P, NA_SMALL])
        kc_s = na.sb("kc_s", [P, NG * NC])
        hk_s = na.sb("hk_s", [P, 2, NG * NC])
        gates_s = na.sb("gates_s", [P, 2, 48])
        cmp_max = na.sb("cmp_max", [P, 2, NH])
        cmp_den = na.sb("cmp_den", [P, 2, NH])
        late = Region(hg_at, hg_at + 2 * KT * T * 4)
        score_c = late.sb("score_c", [P, 2, NH, 32])
        prob_c = late.sb("prob_c", [P, 2, NG, P])
        prob_t = [late.sb(f"prob_t{i}", [P, 2, 4, P]) for i in range(2)]
        hv_rep = prob_t[1]

        mo = Region(*region)
        mo_o_hi = mo.sb("mo_o_hi", [P, KT, T], F32R)
        mo_o_lo = mo.sb("mo_o_lo", [P, KT, T], F32R)
        qk_s = mo.sb("qk_s", [P, 16, T])
        qk_f = [mo.sb(f"qk_f{i}", [P, 2, T]) for i in range(2)]
        qk_sq = [mo.sb(f"qk_sq{i}", [P, 2, T]) for i in range(2)]
        v_s = mo.sb("v_s", [P, 2, D])
        mo_swap = [mo.sb(f"mo_swap{i}", [P, 2, T]) for i in range(2)]
        mo_turn = mo.sb("mo_turn", [P, 2, T])
        mo_prob = [mo.sb(f"mo_prob{i}", [P, 4, T]) for i in range(3)]
        mo_prob_t = [mo.sb(f"mo_prob_t{i}", [P, 2, 4, P]) for i in range(2)]
        mo_tab = mo.sb("mo_tab", [P, MO_TAB])
        qk_rms = mo.sb("qk_rms", [P, 2, 16])
        qk_rstd = mo.sb("qk_rstd", [P, 2, 16])

        tok_rms_made = sem("tok_rms_made")
        tok_rstd_made = sem("tok_rstd_made")
        tabs_in = sem("tabs_in")
        hqhi_made = sem("hqhi_made")
        hq_made = sem("hq_made")
        proj_read = sem("proj_read")
        pads_zero = sem("pads_zero")
        blk_made = sem("blk_made")
        blkhi_made = sem("blkhi_made")
        blklo_made = sem("blklo_made")
        cmp_gelu = sem("cmp_gelu")
        cmp_turned = sem("cmp_turned")
        hid_kept = sem("hid_kept")
        gate_scaled_na = sem("gate_scaled_na")
        gate_turned = sem("gate_turned")
        cmp_done = sem("cmp_done")
        cmp_kept = sem("cmp_kept")
        q_copied = sem("q_copied")
        swapped = [sem(f"swapped{i}") for i in range(2)]
        turn_step = sem("turn_step")
        turned = sem("turned")
        gate_lin = sem("gate_lin")
        gates_made = sem("gates_made")
        sc_done = sem("sc_done")
        sc_ready = sem("sc_ready")
        sc_exp = sem("sc_exp")
        pc_made = sem("pc_made")
        pc_turned = sem("pc_turned")
        pc_kept = sem("pc_kept")
        scores_done = sem("scores_done")
        masked = sem("masked")
        negmax = sem("negmax")
        exp_made = sem("exp_made")
        norm_made = sem("norm_made")
        prob_made = sem("prob_made")
        prob_turned = sem("prob_turned")
        prob_kept = sem("prob_kept")
        pv_done = sem("pv_done")
        ohi_made = sem("ohi_made")
        o_made = sem("o_made")
        qkf_made = sem("qkf_made")
        qksq_made = sem("qksq_made")
        qkms_made = sem("qkms_made")
        qkrms_made = sem("qkrms_made")
        qkrstd_made = sem("qkrstd_made")
        krs_made = sem("krs_made")
        k_scaled = sem("k_scaled")

        proj_n, turn_n, sub_n, job_n = {}, {}, {}, {}
        tot = [0, 0, 0, 0]
        for ph in phases:
            for k, table, c in ((0, proj_n, {"nsa": 19, "moba": 8}), (1, turn_n, {"nsa": 12, "moba": 8}),
                                (2, sub_n, {"nsa": 16, "moba": 4}), (3, job_n, {"nsa": 8, "moba": 4})):
                if ph["kind"] in c:
                    table[ph["kind"]] = tot[k]
                    tot[k] += c[ph["kind"]]

        class Attention:

            def __init__(self, kind):
                self.nsa = kind == "nsa"
                self.branches = 2 if self.nsa else 1
                self.jobs = 8 if self.nsa else 4
                self.steps = self.jobs * self.branches
                self.step0, self.job0 = sub_n[kind], job_n[kind]
                self.prob = prob if self.nsa else mo_prob
                self.prob_t = prob_t if self.nsa else mo_prob_t
                tab = na_tab if self.nsa else mo_tab
                self.mask = tab[:, 2 * T:3 * T]
                self.ident = tab[:, 3 * T:3 * T + P]
                self.o_hi, self.o_lo = (hq_hi, hq_lo) if self.nsa else (mo_o_hi, mo_o_lo)

            def step(self, n):
                job, branch = divmod(n, self.branches)
                group, b = divmod(job, 2)
                return job, branch, group, b, P * (b + 1)

            def score_bank(self, n, i, keys):
                first = 2 * (n % 2)
                return bank[first + i * keys // 512][:, i * keys % 512:i * keys % 512 + keys]

            def o_tile(self, group, b):
                tiles = slice(2 * group, 2 * group + 2) if self.nsa else slice(4 * group, 4 * group + 4)
                return tiles, slice(P * b, P * b + P)

        max_s = [sb_small[:, 0:4], sb_small[:, 4:8]]
        neg_s = [sb_small[:, 8:12], sb_small[:, 12:16]]
        den_s = [sb_small[:, 16:20], sb_small[:, 20:24]]
        fac_s = [sb_small[:, 24:28], sb_small[:, 28:32]]

        turn_q = {"nsa": 0, "moba": 8 if "nsa" in sub_n else 0}
        tok_n = {}
        for ph in phases:
            if ph["kind"] in ("nsa", "moba"):
                tok_n[ph["kind"]] = len(tok_n)

        s5_par_place = Region(region[1] - S5_PLACE, region[1])
        s5_par = s5_par_place.sb("s5_par", [P, S5_PAR])
        s5_mag, s5_turn, s5_turn_hi, s5_turn_lo, s5_kre, s5_kim, s5_den, s5_sin, s5_cos, s5_tmp = (
            s5_par_place.sb(f"s5_{n}", [P, ST]) for n in
            ("mag", "turn", "turn_hi", "turn_lo", "kre", "kim", "den", "sin", "cos", "tmp"))
        s5_tables = Region(after_ffn, region[1] - S5_PLACE)
        table = [s5_tables.sb(f"table{i}", [P, 4, 2, T]) for i in range(4)]
        s5 = Region(region[0], after_ffn)
        u_s = s5.sb("u_s", [P, KT, T])
        bt_s = [s5.sb(f"bt{i}", [P, 2, P]) for i in range(4)]
        c_s = s5.sb("c_s", [P, 3, ST, 32])
        bu_s = s5.sb("bu_s", [P, 2, 2, T])
        ring_at = s5.at
        ring_x = [s5.sb(f"ring_x{i}", [P, 2, 2, T]) for i in range(3)]
        ring_y = [s5.sb(f"ring_y{i}", [P, 2, 2, T]) for i in range(3)]
        c_raw = [ring_x[2][:, :, :, :], ring_y[2][:, :, :, :]]
        c_tmp = [ring_y[1][:, :, :, :], ring_x[1][:, :, :, :]]

        def by_tile(x):
            return x.rearrange("p a b t -> p (a b t)").rearrange("p (j n) -> p j n", n=32)

        def over_outputs(x):
            return x[:, :, None].broadcast_to([P, ST, 32])

        s5_late = Region(ring_at, after_ffn)
        out_hi = s5_late.sb("out_hi", [P, KT, T], F32R)
        out_lo = s5_late.sb("out_lo", [P, KT, T], F32R)
        s5_par_in = sem("s5_par_in")
        c_in = sem("c_in")
        bt_in = [sem(f"bt_in{i}") for i in range(4)]
        turn_made = sem("turn_made")
        lam_made = sem("lam_made")
        coef_made = sem("coef_made")
        pool_step = sem("pool_step")
        turns_pool = sem("turns_pool")
        abs_made = sem("abs_made")
        table_made = sem("table_made")
        spilled = [sem(f"spilled{i}") for i in range(4)]
        table_in = [sem(f"table_in{i}") for i in range(4)]
        c_made = sem("c_made")
        c_imag_made = sem("c_imag_made")
        u_made = sem("u_made")
        b_done = sem("b_done")
        bu_kept = sem("bu_kept")
        xin_made = sem("xin_made")
        yin_made = sem("yin_made")
        z_made = sem("z_made")
        xout_made = sem("xout_made")
        yout_made = sem("yout_made")
        c_done = sem("c_done")
        skip_made = sem("skip_made")
        g_made = sem("g_made")
        ghi_made = sem("ghi_made")
        glo_made = sem("glo_made")
        glu_sig = sem("glu_sig")
        gated = sem("gated")
        outhi_made = sem("outhi_made")
        outlo_made = sem("outlo_made")
        table_dram = nc.dram_tensor("s5_table", (4, P, 4 * 2 * T), F32, kind="Internal").ap() if phase_of("s5") else None
        TABLE_ORDER = (4, 5, 6, 7, 0, 1, 2, 3)
        G_RUNS = ((0, 6), (6, 7), (7, 8))

        def table_ready(kt):
            return (table_made, 2 * TABLE_ORDER.index(kt) + 2) if kt < 4 else (table_in[kt - 4], 16)

        def s5_early():
            return phase_of("s5") and phase_of("nsa")

        block = ctx.enter_context(nc.Block())

        @block.sync
        def _(sp):
            def load(unit, it=0, row_step=0):
                kind, row = units[unit]
                size = 2 * HALF[kind]
                if unit >= RAW:
                    sp.wait_ge(lo_made, 2 * (unit - RAW) + 2 + 2 * row_step * it)
                src = ins[kind]
                if row_step:
                    src = src[bass.ds(row + row_step * it, 1)].rearrange("a p n -> p (a n)")
                else:
                    src = src[row]
                sp.dma_start(raw[unit % RAW][:, 0:size], src).then_inc(raw_loaded[unit % RAW], 16)

            unit = 0
            while unit < len(units):
                run = 1
                while unit + run < len(units) and units[unit + run][0] == units[unit][0]:
                    run += 1
                if unit < RAW:
                    run = min(run, RAW)
                if run >= 2 * BODY:
                    trips = run // BODY
                    with sp.Fori(0, trips) as it:
                        for j in range(BODY):
                            load(unit + j, it, BODY)
                    unit += BODY * trips
                else:
                    for j in range(run):
                        load(unit + j)
                    unit += run

        @block.gpsimd
        def _(pool):
            steps = [0]
            pool.memset(ones_d[:, :], 1.0 / D).then_inc(pool_const, 1)
            pool.memset(eps[:, :], EPS).then_inc(pool_const, 1)
            if phase_of("s5") and not s5_early():
                pool.dma_start(s5_par[:, :], ins["s5_par"]).then_inc(s5_par_in, 16)
            if phase_of("rglru"):
                pool.memset(xb[:, :, 0:4], 0.0).then_inc(pads_made, 1)
            pool.memset(half_pi[:, :], float(np.pi / 2)).then_inc(pool_const, 1)

            def sum_squares(norm, ready):
                if norm >= 1:
                    pool.wait_ge(ms_made, norm)
                for m in range(KT):
                    ready(m)
                    if m == 0:
                        pool.tensor_tensor(sumsq[:, :], h[:, m, :], h[:, m, :], ALU.mult).then_inc(sq_step, 1)
                        steps[0] += 1
                        continue
                    pool.tensor_tensor(square[:, :], h[:, m, :], h[:, m, :], ALU.mult).then_inc(sq_step, 1)
                    steps[0] += 1
                    pool.wait_ge(sq_step, steps[0])
                    last = pool.tensor_tensor(sumsq[:, :], sumsq[:, :], square[:, :], ALU.add)
                    last.then_inc(sumsq_made if m == KT - 1 else sq_step, 1)
                    if m < KT - 1:
                        steps[0] += 1
                        pool.wait_ge(sq_step, steps[0])

            def rglru_phase(ph):
                for g in range(4):
                    slot = GT * (g % 2)
                    x, rt = i_s[g % 2], root_s[g % 2]
                    pool.wait_ge(sigm_made, 2 * GT * (g + 1))
                    pool.wait_ge(xc_made, g + 1)
                    pool.tensor_tensor(x[:, :, :], x[:, :, :], xc[:, slot:slot + GT, :], ALU.mult).then_inc(ix_made, 1)
                    pool.wait_ge(rroot_made, g + 1)
                    pool.wait_ge(ix_made, 2 * g + 1)
                    pool.tensor_tensor(x[:, :, :], x[:, :, :], rt[:, :, :], ALU.mult).then_inc(ix_made, 1)

            def load_tables(ph):
                if ph["u0"]:
                    pool.wait_ge(half_used, 2 * ph["u0"])
                if ph["kind"] == "nsa":
                    pool.dma_start(na_tab[:, :], ins["na_tab"]).then_inc(tabs_in, 16)
                    pool.dma_start(na_small[:, :], ins["na_small"]).then_inc(tabs_in, 16)
                    if phase_of("s5"):
                        load_s5_parameters()
                else:
                    pool.dma_start(mo_tab[:, :], ins["mo_tab"]).then_inc(tabs_in, 16)

            def rotations(items, base, tab, half_dim, swaps, turn):
                n2 = 2 * half_dim

                def swap(i):
                    src, _, (s, v) = items[i]
                    pool.wait_ge(s, v)
                    if base + i >= 2:
                        pool.wait_ge(turned, base + i - 1)
                    buf = swaps[i % 2]
                    pool.dma_start(buf[0:half_dim, :, :], src[half_dim:n2, :, :]).then_inc(swapped[i % 2], 16)
                    pool.dma_start(buf[half_dim:n2, :, :], src[0:half_dim, :, :]).then_inc(swapped[i % 2], 16)

                def bc(a):
                    return tab[0:n2, a * T:(a + 1) * T][:, None, :].broadcast_to([n2, 2, T])

                def rotate(i):
                    src, dst, _ = items[i]
                    buf = swaps[i % 2]
                    n = base + i
                    pool.wait_ge(swapped[i % 2], 32 * ((n - i % 2) // 2 + 1))
                    pool.tensor_tensor(buf[0:n2, :, :], buf[0:n2, :, :], bc(1), ALU.mult).then_inc(turn_step, 1)
                    if n:
                        pool.wait_ge(turned, n)
                    pool.tensor_tensor(turn[0:n2, :, :], src[0:n2, :, :], bc(0), ALU.mult).then_inc(turn_step, 1)
                    pool.wait_ge(turn_step, 2 * n + 2)
                    pool.tensor_tensor(dst[0:n2, :, :], turn[0:n2, :, :], buf[0:n2, :, :], ALU.add).then_inc(turned, 1)

                for i in range(len(items)):
                    swap(i)
                    if i:
                        rotate(i - 1)
                rotate(len(items) - 1)

            def scale_probs(att):
                for n in range(att.steps):
                    job, branch, group, b, keys = att.step(n)
                    pool.wait_ge(norm_made, att.step0 + n + 1)
                    p = att.prob[n % 3][:, :, 0:keys]
                    pool.tensor_tensor(p, p, fac_s[n % 2][:, :, None].broadcast_to([P, 4, keys]), ALU.mult).then_inc(prob_made, 1)

            def nsa_phase(ph):
                load_tables(ph)
                half0 = 2 * ph["u0"]
                base = proj_n["nsa"]
                pool.wait_ge(tabs_in, 32)
                items = []
                for u in range(4):
                    kt = (ks_s, kw_s)[u // 2][:, 2 * (u % 2):2 * (u % 2) + 2, :]
                    items.append((kt, kt, (proj_read, base + 4 + u)))
                for u in range(8):
                    items.append((q_s[:, 2 * u:2 * u + 2, :], qr_s[:, 2 * u:2 * u + 2, :], (q_copied, u + 1)))
                pool.wait_ge(half_used, half0 + 18)
                pool.memset(hv_rep[:, :, :, :], 0.0).then_inc(pads_zero, 1)
                pool.memset(score_c[:, :, :, :], 0.0).then_inc(pads_zero, 1)
                rotations(items[:4], turn_n["nsa"], na_tab, 12, swap_s, turn_s)
                pool.wait_ge(half_used, half0 + 34)
                pool.memset(vc_s[:, :, :, :], 0.0).then_inc(pads_zero, 1)
                rotations(items[4:], turn_n["nsa"] + 4, na_tab, 12, swap_s, turn_s)
                scale_probs(Attention("nsa"))

            def moba_phase(ph):
                load_tables(ph)
                pool.wait_ge(tabs_in, 16 * (2 * ("nsa" in sub_n) + 1))
                items = []
                for u in range(8):
                    x = qk_s[:, 2 * u:2 * u + 2, :]
                    items.append((x, x, (q_copied, turn_q["moba"] + u + 1)))
                rotations(items, turn_n["moba"], mo_tab, 16, mo_swap, mo_turn)
                scale_probs(Attention("moba"))

            small = [0]

            def own(instruction):
                small[0] += 1
                instruction.then_inc(pool_step, 1)
                pool.wait_ge(pool_step, small[0])

            def load_s5_parameters():
                pool.dma_start(s5_par[:, :], ins["s5_par"]).then_inc(s5_par_in, 16)

            def turns(kt, free):
                tab = table[kt % 4]
                r, k = tab[:, :, 0, :], tab[:, :, 1, :]
                iota = s5_par[:, 3 * ST:3 * ST + T]
                magic = 12582912.0

                def times(dst, factor):
                    for a in range(4):
                        last = pool.tensor_scalar(dst[:, a, :], iota, factor[:, 4 * kt + a:4 * kt + a + 1], None, ALU.mult)
                        if a < 3:
                            small[0] += 1
                            last.then_inc(pool_step, 1)
                    own(last)

                if kt == 4:
                    pool.wait_ge(turn_made, 1)
                    if free:
                        pool.wait_ge(half_used, free)
                if kt < 4:
                    pool.wait_ge(spilled[kt], 16)
                times(k, s5_turn)
                own(pool.tensor_scalar(k, k, magic, magic, ALU.add, ALU.subtract))
                times(r, s5_turn_hi)
                own(pool.tensor_tensor(r, r, k, ALU.subtract))
                times(k, s5_turn_lo)
                own(pool.tensor_tensor(r, r, k, ALU.add))
                pool.tensor_scalar(r, r, 0.5, -0.5, ALU.min, ALU.max).then_inc(turns_pool, 1)

            def s5_phase(ph):
                for kt in ph["tables"]:
                    turns(kt, 0)
                if ph["u0"]:
                    pool.wait_ge(half_used, 2 * ph["u0"])
                for part in range(2):
                    pool.dma_start(c_raw[part], ins["s5_c"][:, part]).then_inc(c_in, 16)
                pool.wait_ge(c_in, 32)
                pool.wait_ge(coef_made, 1)

                re, im, tmp = by_tile(c_raw[0]), by_tile(c_raw[1]), by_tile(c_tmp[0])
                own(pool.tensor_tensor(c_s[:, 0], re, over_outputs(s5_kre), ALU.mult))
                own(pool.tensor_tensor(tmp, im, over_outputs(s5_kim), ALU.mult))
                pool.tensor_tensor(c_s[:, 2], tmp, c_s[:, 0], ALU.subtract).then_inc(c_made, 1)
                pool.tensor_tensor(c_s[:, 0], c_s[:, 0], tmp, ALU.subtract).then_inc(c_made, 1)

                def sin_of(n):
                    kt, q = divmod(n, 2)
                    return table[kt % 4][:, 2 * q:2 * q + 2, 0, :][:, :, None, :].broadcast_to([P, 2, 2, T])

                for n in range(17):
                    if n < 16:
                        pool.wait_ge(bu_kept, 2 * n + 2)
                        if n % 2 == 0:
                            pool.wait_ge(*table_ready(n // 2))
                        if n == 0:
                            pool.wait_ge(c_made, 2)
                        if n == 2:
                            pool.wait_ge(c_imag_made, 1)
                        if n >= 3:
                            pool.wait_ge(c_done, n - 2)
                        pool.tensor_tensor(ring_y[n % 3][:, :, :, :], bu_s[:, :, :, :], sin_of(n), ALU.mult).then_inc(yin_made, 1)
                    if n >= 1:
                        m = n - 1
                        pool.wait_ge(z_made, 4 * m + 4)
                        pool.wait_ge(xout_made, m + 1)
                        x = ring_x[m % 3]
                        pool.tensor_tensor(x[:, :, :, :], x[:, :, :, :], sin_of(m), ALU.mult).then_inc(yout_made, 1)

            sum_squares(0, lambda m: pool.wait_ge(x_in, 16))
            for ph in phases:
                if ph["kind"] == "rglru":
                    rglru_phase(ph)


                if ph["kind"] == "nsa":
                    nsa_phase(ph)
                if ph["kind"] == "moba":
                    moba_phase(ph)
                if ph["kind"] == "ffn":
                    for kt in ph["tables"]:
                        turns(kt, 2 * ph["u0"])
                if ph["kind"] == "s5":
                    s5_phase(ph)
                if not ph["last"]:
                    sum_squares(ph["norm"] + 1, lambda m: pool.wait_ge(h_written, h_count(ph["hw"], m)))

        @block.scalar
        def _(act):
            act.dma_start(vec[:, :], ins["vec"]).then_inc(consts_in, 16)
            act.dma_start(h[:, :, :], ins["x"]).then_inc(x_in, 16)
            if phase_of("rglru"):
                act.dma_start(gate_w[:, :, :], ins["gate_w"]).then_inc(gate_w_in, 16)

            def split_hi(half, it=0):
                if half >= n_halves:
                    return
                n, s, r = half_size(half), half % SPLIT, half // 2 % RAW
                c = half % 2
                act.wait_ge(raw_loaded[r], 16 * (half // (2 * RAW) + 1) + 16 * it)
                if half >= SPLIT:
                    act.wait_ge(half_used, half - SPLIT + 1 + 2 * BODY * it)
                act.activation(w_hi[s][:, 0:n], raw[r][:, c * n:(c + 1) * n], ACT.Copy).then_inc(hi_made, 1)

            def make_hg_hi(gain_name, hg, m):
                act.activation(hg_hi[:, m, :], h[:, m, :], ACT.Copy, scale=gain(gain_name, m)).then_inc(hghi_made, 1)

            def root(norm):
                act.wait_ge(ms_made, norm + 1)
                if norm == 0:
                    act.wait_ge(pool_const, 2)
                act.activation(rms[:, :], bank[NORM_BANK][:, 0:T], ACT.Sqrt, bias=eps[:, :]).then_inc(rms_made, 1)

            def after_tile(ph, m):
                if ph["next"]:
                    act.wait_ge(h_written, h_count(ph["hw"], m))
                    make_hg_hi(ph["next"], ph["next_hg"], m)
                if ph["last"]:
                    act.wait_ge(h_written, h_count(ph["hw"], m))
                    act.dma_start(out[:, m, :], h[:, m, :]).then_inc(out_sent, 16)

            def project(ph, half0, per_tile):
                for m in range(KT):
                    for j in range(per_tile):
                        split_hi(half0 + m * per_tile + j + SPLIT)
                    if ph["kind"] == "ffn" and ph["tables"] and m % 2:
                        s5_table(ph["tables"][m // 2])
                    after_tile(ph, m)

            def ffn_phase(ph):
                half0 = 2 * ph["u0"]
                pairs0 = PAIRS * ph["f"]

                def pair(p, it=0):
                    half = half0 + 4 * p
                    split_hi(half + SPLIT, it)
                    split_hi(half + SPLIT + 1, it)
                    if p == 0:
                        root(ph["norm"])
                    act.wait_ge(gate_scaled, pairs0 + p + 1 + 2 * it)
                    act.activation(silu_s[:, :], gate_s[:, :], ACT.Silu).then_inc(silu_made, 1)
                    split_hi(half + SPLIT + 2, it)
                    split_hi(half + SPLIT + 3, it)
                    act.wait_ge(hidf_made, pairs0 + p + 1 + 2 * it)
                    act.activation(hid_hi[:, bass.ds(p * 2 * T + 4 * T * it, 2 * T)] if p else hid_hi[:, 0:2 * T],
                                   hid_f[:, :], ACT.Copy).then_inc(hidhi_made, 1)

                pair(0)
                with act.Fori(0, 4) as it:
                    pair(1, it)
                    pair(2, it)
                pair(9)
                pair(10)
                project(ph, half0 + 4 * PAIRS, 2)

            def rglru_phase(ph):
                half0 = 2 * ph["u0"]

                def gates(g):
                    r, i, rt = r_s[g % 2], i_s[g % 2], root_s[g % 2]
                    act.wait_ge(gates_done, g + 1)
                    if g >= 2:
                        act.wait_ge(rec_scanned, GT * (g - 1))
                    for q in range(GT):
                        act.activation(r[:, q, :], bank[5 + q // 2][:, q % 2 * T:(q % 2 + 1) * T], ACT.Sigmoid,
                                       bias=gain("b_ra", GT * g + q)).then_inc(sigm_made, 1)
                    for q in range(GT):
                        n = GT + q
                        act.activation(i[:, q, :], bank[5 + n // 2][:, n % 2 * T:(n % 2 + 1) * T], ACT.Sigmoid,
                                       bias=gain("b_ix", GT * g + q)).then_inc(sigm_made, 1)
                    if g == 0:
                        act.wait_ge(sp4_made, 1)
                    act.wait_ge(sigm_made, 2 * GT * g + GT)
                    for q in range(GT):
                        act.activation(r[:, q, :], r[:, q, :], ACT.Tanh,
                                       scale=sp4[:, GT * g + q:GT * g + q + 1]).then_inc(tanh_made, 1)
                    act.wait_ge(tanh_made, GT * g + GT)
                    act.activation(rt[:, :, :], r[:, :, :], ACT.Sqrt).then_inc(rroot_made, 1)

                def hi_of_rec(g):
                    if g == 1:
                        act.wait_ge(rec_scanned, 4 * GT)
                    act.wait_ge(recf_made, g + 1)
                    act.activation(rec_hi[:, GT * g:GT * g + GT, :], rec_f(g), ACT.Copy).then_inc(rechi_made, 1)

                for j in range(2 * RT):
                    split_hi(half0 + j + SPLIT)
                    if j == 1:
                        root(ph["norm"])
                    if j > RT and j % 2:
                        u = (j - RT) // 2
                        act.wait_ge(y_scaled, u + 1)
                        y = y_gelu[:, 2 * u:2 * u + 2, :]
                        act.activation(y, y, ACT.Gelu_apprx_tanh).then_inc(y_made, 1)
                    if j in GATES_AT:
                        gates(GATES_AT.index(j))
                    if j in FINISH_AT:
                        hi_of_rec(FINISH_AT.index(j))
                hi_of_rec(3)
                project(ph, half0 + 2 * RT, 2)

            def root_by_token(kind):
                act.activation(rms_tok[:, :], bank[NORM_BANK][:, T:T + 2], ACT.Sqrt, bias=eps[:, :]).then_inc(tok_rms_made, 1)

            def attention(att):
                def exps(n):
                    job, branch, group, b, keys = att.step(n)
                    act.wait_ge(negmax, att.step0 + n + 1)
                    p = att.prob[n % 3]
                    for i in range(4):
                        act.activation(p[:, i, 0:keys], p[:, i, 0:keys], ACT.Exp, bias=neg_s[n % 2][:, i:i + 1],
                                       accum_out=den_s[n % 2][:, i:i + 1]).then_inc(exp_made, 1)

                def keep(n):
                    job, branch, group, b, keys = att.step(n)
                    act.wait_ge(prob_turned, att.step0 + n + 1)
                    before = n // att.branches - (1 if att.branches == 2 else 2)
                    if before >= 0:
                        act.wait_ge(pv_done, att.job0 + before + 1)
                    for kt in range(b + 1):
                        act.activation(att.prob_t[n % 2][:, kt, :, :], bank[5 + kt][:, :].rearrange("p (i q) -> p i q", i=4),
                                       ACT.Copy).then_inc(prob_kept, 1)

                def hi_of_o(job):
                    group, b = divmod(job, 2)
                    tiles, tokens = att.o_tile(group, b)
                    width = 2 * P if att.nsa else 4 * P
                    act.wait_ge(pv_done, att.job0 + job + 1)
                    act.activation(att.o_hi[:, tiles, tokens], bank[(7, 4)[job % 2]][:, 0:width].rearrange("p (a q) -> p a q", q=P),
                                   ACT.Copy).then_inc(ohi_made, 1)

                for n in range(att.steps + 1):
                    if n < att.steps:
                        exps(n)
                    if n >= 1:
                        keep(n - 1)
                    if n >= 2 and (n - 1) % att.branches == att.branches - 1 and (n - 1) // att.branches >= 1:
                        hi_of_o((n - 1) // att.branches - 1)
                hi_of_o(att.jobs - 1)

            def nsa_phase(ph):
                half0 = 2 * ph["u0"]
                base = proj_n["nsa"]

                def hi_of_blocks(dst, src, made):
                    act.wait_ge(blk_made, made)
                    act.activation(dst[:, :, :], src[:, :, :], ACT.Copy).then_inc(blkhi_made, 1)

                for j in range(52):
                    split_hi(half0 + j + SPLIT)
                    if j == 1:
                        root(ph["norm"])
                        root_by_token("nsa")
                    if 2 <= j < 10:
                        act.activation(hq_hi[:, j - 2, :], h[:, j - 2, :], ACT.Copy, scale=gain("norm_10", j - 2)).then_inc(hqhi_made, 1)
                    if j == 9:
                        hi_of_blocks(blk_k_hi, blk_k, 2)
                    if j == 13:
                        hi_of_blocks(blk_v_hi, blk_v, 6)
                    if j == 33:
                        for side in range(2):
                            act.wait_ge(half_used, half0 + 26 + 8 * side)
                            act.activation(hid_t[:, side, :], bank[side][0:NG * NC, 0:T], ACT.Gelu_apprx_tanh).then_inc(cmp_gelu, 1)
                    if s5_early() and j == 44:
                        s5_lambda()
                    if j >= 34 and j < 50 and j % 2:
                        u = (j - 34) // 2
                        act.wait_ge(proj_read, base + 11 + u + 1)
                        act.activation(qr_s[0:96, 2 * u:2 * u + 2, :], q_s[0:96, 2 * u:2 * u + 2, :], ACT.Copy).then_inc(q_copied, 1)
                act.wait_ge(gate_lin, 2)
                act.activation(gates_s[:, :, :], gates_s[:, :, :], ACT.Sigmoid).then_inc(gates_made, 1)
                act.wait_ge(sc_ready, 1)
                act.activation(score_c[:, :, :, 0:NC], score_c[:, :, :, 0:NC], ACT.Exp).then_inc(sc_exp, 1)
                for b in range(2):
                    act.wait_ge(pc_turned, b + 1)
                    act.activation(prob_c[:, b, :, :], bank[5 + b][:, :].rearrange("p (g q) -> p g q", g=NG), ACT.Copy).then_inc(pc_kept, 1)
                attention(Attention("nsa"))
                project(ph, half0 + 52, 1)

            def moba_phase(ph):
                half0 = 2 * ph["u0"]
                for j in range(24):
                    split_hi(half0 + j + SPLIT)
                    if j == 1:
                        root(ph["norm"])
                        root_by_token("moba")
                    if j < 16 and j % 2:
                        u = j // 2
                        act.wait_ge(qkf_made, u + 1)
                        if u >= 2:
                            act.wait_ge(qkms_made, u - 1)
                        act.activation(qk_sq[u % 2][:, :, :], qk_f[u % 2][:, :, :], ACT.Square).then_inc(qksq_made, 1)
                        act.activation(qk_s[:, 2 * u:2 * u + 2, :], qk_f[u % 2][:, :, :], ACT.Copy,
                                       scale=gain("q_gain" if u < 4 else "k_gain", 0)).then_inc(q_copied, 1)
                    if j == 17:
                        act.wait_ge(qkms_made, 8)
                        act.activation(qk_rms[:, :, :], bank[5][:, 0:32].rearrange("p (b n) -> p b n", b=2), ACT.Sqrt,
                                       bias=eps[:, :], scale=float(D // P)).then_inc(qkrms_made, 1)
                attention(Attention("moba"))
                project(ph, half0 + 24, 1)

            def s5_lambda():
                act.wait_ge(turn_made, 1)
                act.wait_ge(pool_const, 3)
                act.activation(s5_sin[:, :], s5_turn[:, :], ACT.Sin, scale=TWO_PI).then_inc(lam_made, 1)
                act.activation(s5_cos[:, :], s5_tmp[:, :], ACT.Sin, scale=-TWO_PI, bias=half_pi[:, :]).then_inc(lam_made, 1)

            def s5_table(kt):
                nth = TABLE_ORDER.index(kt)
                act.wait_ge(turns_pool, nth + 1)
                tab = table[kt % 4]
                act.activation(tab[:, :, 1, :], tab[:, :, 0, :], ACT.Abs).then_inc(abs_made, 1)
                act.wait_ge(abs_made, nth + 1)
                act.activation(tab[:, :, 0, :], tab[:, :, 0, :], ACT.Sin, scale=TWO_PI).then_inc(table_made, 1)
                act.activation(tab[:, :, 1, :], tab[:, :, 1, :], ACT.Sin, scale=-TWO_PI, bias=half_pi[:, :]).then_inc(table_made, 1)
                if kt >= 4:
                    act.wait_ge(table_made, 2 * nth + 2)
                    act.dma_start(table_dram[kt - 4], tab.rearrange("p a b t -> p (a b t)")).then_inc(spilled[kt - 4], 16)

            def s5_phase(ph):
                half0 = 2 * ph["u0"]

                def load_b(kt):
                    if kt >= 4:
                        act.wait_ge(b_done, 2 * (kt - 4) + 2)
                    act.dma_start(bt_s[kt % 4][:, :, :], ins["s5_b"][:, kt, :, :]).then_inc(bt_in[kt % 4], 16)

                def gelu(kt):
                    act.wait_ge(skip_made, kt + 1)
                    act.activation(u_s[:, kt, :], u_s[:, kt, :], ACT.Gelu_apprx_tanh).then_inc(g_made, 1)

                def hi_of_g(run):
                    a, b = G_RUNS[run]
                    act.wait_ge(g_made, b)
                    act.activation(hg_hi[:, a:b, :], u_s[:, a:b, :], ACT.Copy).then_inc(ghi_made, 1)

                if not s5_early():
                    s5_lambda()
                for kt in ph["tables"]:
                    s5_table(kt)
                act.wait_ge(half_used, half0)
                for kt in range(4):
                    load_b(kt)
                for n in range(16):
                    if n % 4 == 0:
                        split_hi(half0 + n // 2 + SPLIT)
                        split_hi(half0 + n // 2 + 1 + SPLIT)
                        if n == 0:
                            root(ph["norm"])
                    act.wait_ge(b_done, n + 1)
                    if n:
                        act.wait_ge(xin_made, n)
                        act.wait_ge(yin_made, n)
                    q = 2 * (n % 2)
                    for c in range(2):
                        act.activation(bu_s[:, c, :, :], bank[q + c][:, :].rearrange("p (a t) -> p a t", a=2), ACT.Copy).then_inc(bu_kept, 1)
                    if n % 2 == 0 and 4 <= n < 12:
                        load_b(n // 2 + 2)
                    if n % 2 and 3 <= n < 11:
                        i = (n - 3) // 2
                        act.wait_ge(yout_made, 2 * i + 2)
                        act.dma_start(table[i].rearrange("p a b t -> p (a b t)"), table_dram[i]).then_inc(table_in[i], 16)
                    if n >= 7 and n % 2:
                        gelu((n - 7) // 2)
                act.wait_ge(half_used, half0 + 8)
                gelu(5)
                hi_of_g(0)
                gelu(6)
                hi_of_g(1)
                gelu(7)
                hi_of_g(2)
                for u in range(4):
                    for j in range(2):
                        split_hi(half0 + 8 + 2 * u + j + SPLIT)
                    act.wait_ge(half_used, half0 + 10 + 2 * u)
                    if u >= 2:
                        act.wait_ge(gated, u - 1)
                    act.activation(bu_s[:, u % 2, :, :], bank[u][:, :].rearrange("p (a t) -> p a t", a=2), ACT.Sigmoid).then_inc(glu_sig, 1)
                    act.wait_ge(gated, u + 1)
                    act.activation(out_hi[:, 2 * u:2 * u + 2, :], u_s[:, 2 * u:2 * u + 2, :], ACT.Copy).then_inc(outhi_made, 1)
                project(ph, half0 + 16, 1)
            act.wait_ge(x_in, 16)
            act.wait_ge(consts_in, 16)
            for m in range(KT):
                make_hg_hi(phases[0]["gain"], 0, m)
            for half in range(SPLIT):
                split_hi(half)
            for ph in phases:
                if ph["kind"] == "ffn":
                    ffn_phase(ph)
                elif ph["kind"] == "final":
                    root(ph["norm"])
                    for m in range(KT):
                        after_tile(ph, m)
                elif ph["kind"] == "rglru":
                    rglru_phase(ph)

                elif ph["kind"] == "nsa":
                    nsa_phase(ph)
                elif ph["kind"] == "moba":
                    moba_phase(ph)
                elif ph["kind"] == "s5":
                    s5_phase(ph)
            act.wait_ge(out_sent, 16 * KT)

        @block.vector
        def _(dve):
            def split_lo(half, it=0):
                if half >= n_halves:
                    return
                n, s, r = half_size(half), half % SPLIT, half // 2 % RAW
                c = half % 2
                dve.wait_ge(hi_made, half + 1 + 2 * BODY * it)
                dve.tensor_tensor(w_lo[s][:, 0:n], raw[r][:, c * n:(c + 1) * n], w_hi[s][:, 0:n].bitcast(F32),
                                  ALU.subtract).then_inc(lo_made, 1)

            def make_hg_lo(gain_name, hg, m):
                dve.wait_ge(hghi_made, KT * hg + m + 1)
                dve.scalar_tensor_tensor(hg_lo[:, m, :], h[:, m, :], gain(gain_name, m),
                                         hg_hi[:, m, :].bitcast(F32), ALU.mult, ALU.subtract).then_inc(hg_made, 1)

            def invert(norm):
                dve.wait_ge(rms_made, norm + 1)
                dve.reciprocal(rstd[:, :], rms[:, :]).then_inc(rstd_made, 1)
                dve.wait_ge(rstd_made, norm + 1)

            def twice(row):
                return row[:, None, :].broadcast_to([P, 2, T])

            def two(x):
                return x.rearrange("p (a t) -> p a t", a=2)

            def add_to_h(ph, m, psum):
                dve.scalar_tensor_tensor(h[:, m, :], psum, ph["scale"], h[:, m, :], ALU.mult, ALU.add)\
                   .then_inc(h_written, 1)

            def project(ph, half0, per_tile):
                for m in range(KT):
                    half = half0 + m * per_tile
                    if per_tile == 2:
                        split_lo(half + SPLIT)
                    dve.wait_ge(half_used, half + per_tile)
                    add_to_h(ph, m, bank[2 + m % 2][:, 0:T])
                    split_lo(half + per_tile - 1 + SPLIT)
                    if ph["next"]:
                        make_hg_lo(ph["next"], ph["next_hg"], m)

            def ffn_phase(ph):
                half0 = 2 * ph["u0"]
                pairs0 = PAIRS * ph["f"]

                def pair(p, it=0):
                    half = half0 + 4 * p
                    gate, up = bank[2 * (p % 2)], bank[2 * (p % 2) + 1]
                    nth = pairs0 + p + 1 + 2 * it
                    split_lo(half + SPLIT, it)
                    if p == 0:
                        invert(ph["norm"])
                    dve.wait_ge(half_used, half + 2 + 2 * BODY * it)
                    dve.tensor_tensor(two(gate_s[:, :]), two(gate[:, :]), twice(rstd), ALU.mult).then_inc(gate_scaled, 1)
                    split_lo(half + SPLIT + 1, it)
                    split_lo(half + SPLIT + 2, it)
                    dve.wait_ge(half_used, half + 4 + 2 * BODY * it)
                    dve.tensor_tensor(two(up_s[:, :]), two(up[:, :]), twice(rstd), ALU.mult).then_inc(up_scaled, 1)
                    dve.wait_ge(silu_made, nth)
                    dve.wait_ge(up_scaled, nth)
                    dve.tensor_tensor(hid_f[:, :], up_s[:, :], silu_s[:, :], ALU.mult).then_inc(hidf_made, 1)
                    split_lo(half + SPLIT + 3, it)
                    dve.wait_ge(hidhi_made, nth)
                    at = bass.ds(p * 2 * T + 4 * T * it, 2 * T) if p else slice(0, 2 * T)
                    dve.tensor_tensor(hid_lo[:, at], hid_f[:, :], hid_hi[:, at].bitcast(F32), ALU.subtract)\
                       .then_inc(hid_made, 1)

                pair(0)
                with dve.Fori(0, 4) as it:
                    pair(1, it)
                    pair(2, it)
                pair(9)
                pair(10)
                project(ph, half0 + 4 * PAIRS, 2)

            steps = [0]
            mask_count = [0]

            def own(instruction):
                steps[0] += 1
                instruction.then_inc(dve_step, 1)
                dve.wait_ge(dve_step, steps[0])

            def exp_tiny(out_ap, x, n):
                magic = 12582912.0
                k, r, p = (tiny[i][:, 0:n] for i in range(3))
                own(dve.tensor_scalar(k, x, 1.4426950408889634, magic, ALU.mult, ALU.add))
                own(dve.tensor_scalar(k, k, magic, -126.0, ALU.subtract, ALU.max))
                own(dve.tensor_scalar(k, k, 127.0, None, ALU.min))
                own(dve.scalar_tensor_tensor(r, k, -0.693359375, x, ALU.mult, ALU.add))
                own(dve.scalar_tensor_tensor(r, k, 2.12194440054690583e-4, r, ALU.mult, ALU.add))
                own(dve.tensor_scalar(r, r, 0.35, -0.35, ALU.min, ALU.max))
                own(dve.tensor_scalar(p, r, 1.0 / 5040.0, None, ALU.mult))
                for c in (1.0 / 720, 1.0 / 120, 1.0 / 24, 1.0 / 6, 0.5, 1.0):
                    own(dve.scalar_tensor_tensor(p, p, c, r, ALU.add, ALU.mult))
                own(dve.tensor_scalar(r, k, 127.0, None, ALU.add))
                own(dve.tensor_copy(tiny_i[:, 0:n], r))
                own(dve.tensor_scalar(tiny_i[:, 0:n], tiny_i[:, 0:n], 23, None, ALU.logical_shift_left))
                own(dve.scalar_tensor_tensor(out_ap, p, 1.0, tiny_i[:, 0:n].bitcast(F32), ALU.add, ALU.mult))

            def softplus_lambda():
                lam = vec[:, VEC["lam"][0]:VEC["lam"][0] + RT]
                a, e, s, s2, p = (t[:, 0:RT] for t in (tiny[3], tiny[4], tiny[3], tiny[0], tiny[1]))
                own(dve.tensor_scalar(a, lam, -1.0, None, ALU.mult))
                own(dve.tensor_tensor(a, a, lam, ALU.min))
                exp_tiny(e, a, RT)
                own(dve.tensor_scalar(s, e, 2.0, None, ALU.add))
                own(dve.reciprocal(s, s))
                own(dve.tensor_tensor(s, s, e, ALU.mult))
                own(dve.tensor_tensor(s2, s, s, ALU.mult))
                own(dve.tensor_scalar(p, s2, 1.0 / 17, None, ALU.mult))
                for n in (15, 13, 11, 9, 7, 5, 3):
                    own(dve.scalar_tensor_tensor(p, p, 1.0 / n, s2, ALU.add, ALU.mult))
                own(dve.scalar_tensor_tensor(p, p, 1.0, s, ALU.add, ALU.mult))
                own(dve.tensor_scalar(s, lam, -1.0, 0.0, ALU.mult, ALU.max))
                own(dve.scalar_tensor_tensor(p, p, 2.0, s, ALU.mult, ALU.add))
                dve.tensor_scalar(sp4[:, :], p, 4.0, None, ALU.mult).then_inc(sp4_made, 1)

            def rglru_phase(ph):
                half0 = 2 * ph["u0"]

                def conv(g):
                    slot = GT * (g % 2)
                    for j in range(4):
                        for q in range(GT):
                            m = GT * g + q
                            x = xb[:, slot + q, 1 + j:1 + j + T]
                            o = xc[:, slot + q, :]
                            if j == 0:
                                last = dve.tensor_scalar(o, x, gain("conv_0", m), gain("conv_b", m), ALU.mult, ALU.add)
                            else:
                                last = dve.scalar_tensor_tensor(o, x, gain(f"conv_{j}", m), o, ALU.mult, ALU.add)
                            if q < GT - 1:
                                steps[0] += 1
                                last.then_inc(dve_step, 1)
                        if j < 3:
                            own(last)
                        else:
                            last.then_inc(xc_made, 1)

                def recur(g):
                    a, x = r_s[g % 2], i_s[g % 2]
                    dve.wait_ge(tanh_made, GT * g + GT)
                    if g:
                        dve.wait_ge(rec_scanned, GT * g)
                    own(dve.tensor_scalar(inv_s[:, :, :], a[:, :, :], 1.0, None, ALU.add))
                    own(dve.reciprocal(inv_s[:, :, :], inv_s[:, :, :]))
                    dve.wait_ge(rroot_made, g + 1)
                    own(dve.tensor_scalar(a[:, :, :], inv_s[:, :, :], 2.0, -1.0, ALU.mult, ALU.add))
                    dve.wait_ge(ix_made, 2 * g + 2)
                    own(dve.scalar_tensor_tensor(x[:, :, :], x[:, :, :], 2.0, inv_s[:, :, :], ALU.mult, ALU.mult))
                    for q in range(GT):
                        dve.tensor_tensor_scan(rec_s[:, GT * g + q, :], a[:, q, :], x[:, q, :], 0.0, ALU.mult, ALU.add)\
                           .then_inc(rec_scanned, 1)

                def times_y(g):
                    dve.wait_ge(rec_scanned, GT * g + GT)
                    dve.wait_ge(y_made, (GT * g + GT + 1) // 2)
                    if g >= 2:
                        dve.wait_ge(rec_made, g - 1)
                    dve.tensor_tensor(rec_f(g), rec_s[:, GT * g:GT * g + GT, :], y_gelu[:, GT * g:GT * g + GT, :],
                                      ALU.mult).then_inc(recf_made, 1)

                def lo_of_rec(g):
                    dve.wait_ge(rechi_made, g + 1)
                    dve.tensor_tensor(rec_lo[:, GT * g:GT * g + GT, :], rec_f(g), rec_hi[:, GT * g:GT * g + GT, :].bitcast(F32),
                                      ALU.subtract).then_inc(rec_made, 1)

                for j in range(2 * RT):
                    split_lo(half0 + j + SPLIT)
                    if j == 1:
                        invert(ph["norm"])
                    if j < RT and j % 2:
                        m = j - 1
                        if m == 0:
                            dve.wait_ge(pads_made, 1)
                        if m // 2 in (3, 4):
                            dve.wait_ge(xc_made, m // 2 - 2)
                        dve.wait_ge(half_used, half0 + j + 1)
                        dve.tensor_tensor(xb[:, m % (2 * GT):m % (2 * GT) + 2, 4:4 + T], two(bank[m // 2 % 4][:, :]), twice(rstd),
                                          ALU.mult).then_inc(xb_made, 1)
                    if j > RT and j % 2:
                        u = (j - RT) // 2
                        dve.wait_ge(half_used, half0 + j + 1)
                        dve.tensor_tensor(y_gelu[:, 2 * u:2 * u + 2, :], two(bank[j // 2 % 4][:, :]), twice(rstd), ALU.mult)\
                           .then_inc(y_scaled, 1)
                    if j in CONV_AT:
                        g = CONV_AT.index(j)
                        dve.wait_ge(xb_made, (GT * g + GT + 1) // 2)
                        if g >= 2:
                            dve.wait_ge(gates_done, g - 1)
                            dve.wait_ge(ix_made, 2 * g - 3)
                        conv(g)
                    if j in RECUR_AT:
                        recur(RECUR_AT.index(j))
                    if j in FINISH_AT:
                        g = FINISH_AT.index(j)
                        if g == 0:
                            dve.wait_ge(xc_made, 4)
                        times_y(g)
                    if j - 1 in FINISH_AT:
                        lo_of_rec(FINISH_AT.index(j - 1))
                times_y(3)
                lo_of_rec(3)
                project(ph, half0 + 2 * RT, 2)

            def invert_by_token(kind):
                dve.wait_ge(tok_rms_made, tok_n[kind] + 1)
                dve.reciprocal(rstd_tok[:, :], rms_tok[:, :]).then_inc(tok_rstd_made, 1)
                dve.wait_ge(tok_rstd_made, tok_n[kind] + 1)

            def attention(att):
                def mask(n):
                    job, branch, group, b, keys = att.step(n)
                    dve.wait_ge(scores_done, att.step0 + n + 1)
                    if n >= 3:
                        dve.wait_ge(prob_turned, att.step0 + n - 2)
                    p = att.prob[n % 3]
                    m = att.mask[:, T - keys:T]
                    if att.nsa:
                        banks = 1 if keys == P else 2
                        per = 4 // banks
                        for a in range(banks):
                            last = dve.tensor_tensor(p[:, per * a:per * a + per, 0:keys],
                                                     bank[2 * (n % 2) + a][:, :].rearrange("p (i k) -> p i k", i=per),
                                                     m[:, None, :].broadcast_to([P, per, keys]), ALU.add)
                            last.then_inc(masked, 1)
                    else:
                        for i in range(4):
                            last = dve.scalar_tensor_tensor(p[:, i, 0:keys], att.score_bank(n, i, keys),
                                                            qk_rstd[:, b, 4 * group + i:4 * group + i + 1], m, ALU.mult, ALU.add)
                            last.then_inc(masked, 1)
                    mask_count[0] += (1 if keys == P else 2) if att.nsa else 4
                    dve.wait_ge(masked, mask_count[0])
                    own(dve.tensor_reduce(max_s[n % 2], p[:, :, 0:keys], AX.X, ALU.max))
                    dve.tensor_scalar(neg_s[n % 2], max_s[n % 2], -1.0, None, ALU.mult).then_inc(negmax, 1)

                def factor(n):
                    job, branch, group, b, keys = att.step(n)
                    dve.wait_ge(exp_made, 4 * (att.step0 + n) + 4)
                    if n >= 2:
                        dve.wait_ge(prob_made, att.step0 + n - 1)
                    if att.nsa:
                        own(dve.reciprocal(den_s[n % 2], den_s[n % 2]))
                        g = gates_s[:, b, :].rearrange("p (h s) -> p h s", s=3)[:, 4 * group:4 * group + 4, 1 + branch]
                        dve.tensor_tensor(fac_s[n % 2], den_s[n % 2], g, ALU.mult).then_inc(norm_made, 1)
                    else:
                        dve.reciprocal(fac_s[n % 2], den_s[n % 2]).then_inc(norm_made, 1)

                def lo_of_o(job):
                    group, b = divmod(job, 2)
                    tiles, tokens = att.o_tile(group, b)
                    width = 2 * P if att.nsa else 4 * P
                    dve.wait_ge(ohi_made, att.job0 + job + 1)
                    dve.tensor_tensor(att.o_lo[:, tiles, tokens], bank[(7, 4)[job % 2]][:, 0:width].rearrange("p (a q) -> p a q", q=P),
                                      att.o_hi[:, tiles, tokens].bitcast(F32), ALU.subtract).then_inc(o_made, 1)

                split_jobs = 0
                for n in range(att.steps + 1):
                    if n < att.steps:
                        mask(n)
                    if n >= 1:
                        factor(n - 1)
                    if n - 1 >= (split_jobs + 2) * att.branches:
                        lo_of_o(split_jobs)
                        split_jobs += 1
                for job in range(split_jobs, att.jobs):
                    lo_of_o(job)

            def nsa_phase(ph):
                half0 = 2 * ph["u0"]
                base = proj_n["nsa"]

                def blocks(dst, src, rows, col, groups, pos):
                    windows = src[rows].rearrange("p g (n j) -> p g n j", j=CS)
                    n_rows = rows.stop - rows.start
                    for part in range(2):
                        dve.tensor_tensor(
                            dst[rows, CS * part:CS * part + CS, col:col + groups * NC].rearrange("p j (g n) -> p j g n", g=groups),
                            windows[:, :, part:part + NC, :].rearrange("p g n j -> p j g n"),
                            pos[rows, CS * part:CS * part + CS][:, :, None, None].broadcast_to([n_rows, CS, groups, NC]), ALU.add)\
                           .then_inc(blk_made, 1)

                def lo_of_blocks(dst, src, hi, n):
                    dve.wait_ge(blkhi_made, n)
                    dve.tensor_tensor(dst[:, :, :], src[:, :, :], hi[:, :, :].bitcast(F32), ALU.subtract).then_inc(blklo_made, 1)

                targets = {0: kc_raw[0:96, 0:2, :], 1: kc_raw[0:96, 2:4, :], 2: vc_raw[:, :, :],
                           3: ks_s[0:96, 0:2, :], 4: ks_s[0:96, 2:4, :], 5: kw_s[0:96, 0:2, :], 6: kw_s[0:96, 2:4, :]}
                own(dve.memset(kc_raw[:, :, :], 0.0))
                for j in range(52):
                    split_lo(half0 + j + SPLIT)
                    if j == 1:
                        invert(ph["norm"])
                        invert_by_token("nsa")
                    if 2 <= j < 10:
                        dve.wait_ge(hqhi_made, j - 1)
                        dve.scalar_tensor_tensor(hq_lo[:, j - 2, :], h[:, j - 2, :], gain("norm_10", j - 2),
                                                 hq_hi[:, j - 2, :].bitcast(F32), ALU.mult, ALU.subtract).then_inc(hq_made, 1)
                    if j < 14 and j % 2:
                        u = j // 2
                        rows = P if u == 2 else 96
                        dve.wait_ge(half_used, half0 + j + 1)
                        dve.tensor_tensor(targets[u], two(bank[u % 4][0:rows, :]), rstd[0:rows, None, :].broadcast_to([rows, 2, T]),
                                          ALU.mult).then_inc(proj_read, 1)
                    if j in (15, 17):
                        u = j // 2
                        dve.wait_ge(half_used, half0 + j + 1)
                        dst = (v_sel, v_win)[u - 7]
                        for b in range(2):
                            dve.tensor_scalar(dst[:, b, :], bank[NA_V_BANKS[u - 7][b]][:, 0:T], rstd_tok[:, b:b + 1], None, ALU.mult)\
                               .then_inc(proj_read, 1)
                    if j == 7:
                        dve.wait_ge(tabs_in, 32)
                        dve.wait_ge(proj_read, base + 3)
                        blocks(blk_k, kc_raw, slice(0, P), 0, NG, na_small[:, 0:CB])
                    if j == 11:
                        dve.wait_ge(blklo_made, 1)
                        own(dve.memset(blk_v[:, :, :], 0.0))
                        for e in range(2):
                            blocks(blk_v, vc_raw, slice(64 * e, 64 * e + 64), 2 * NC * e, 2, na_small[:, CB:2 * CB])
                    if j == 9:
                        lo_of_blocks(blk_k_lo, blk_k, blk_k_hi, 1)
                    if j == 13:
                        lo_of_blocks(blk_v_lo, blk_v, blk_v_hi, 2)
                    if j == 36:
                        dve.wait_ge(cmp_turned, 1)
                        dve.wait_ge(pads_zero, 1)
                        turned_t = bank[5][:, 0:4 * 64].rearrange("p (s m n) -> p s m n", s=2, m=2)
                        dve.tensor_copy(hk_s[:, :, :], turned_t[:, 0, :, 0:NG * NC]).then_inc(hid_kept, 1)
                        for m in range(2):
                            for e in range(2):
                                for a in range(2):
                                    at = 2 * NC * e + NC * a
                                    dve.tensor_copy(hv_rep[:, m, 2 * a + e, :].rearrange("p (i n) -> p i n", i=4)[:, :, 0:NC],
                                                    turned_t[:, 1, m, at:at + NC][:, None, :].broadcast_to([P, 4, NC]))\
                                       .then_inc(hid_kept, 1)
                    if j == 38:
                        dve.wait_ge(cmp_done, 1)
                        dve.tensor_copy(kc_s[0:96, :], bank[7][0:96, 0:NG * NC]).then_inc(cmp_kept, 1)
                        dve.wait_ge(cmp_done, 2)
                        dve.wait_ge(pads_zero, 3)
                        for i in range(4):
                            rows = slice(32 * i, 32 * i + 32)
                            dve.tensor_copy(vc_s[rows, :, i, :], bank[6][rows, 0:NG * 64].rearrange("p (g v) -> p g v", g=NG))\
                               .then_inc(cmp_kept, 1)
                    if j >= 34 and j < 50 and j % 2:
                        u = (j - 34) // 2
                        dve.wait_ge(half_used, half0 + j + 1)
                        dve.scalar_tensor_tensor(q_s[0:96, 2 * u:2 * u + 2, :], two(bank[u % 4][0:96, :]), 96.0 ** -0.5,
                                                 rstd[0:96, None, :].broadcast_to([96, 2, T]), ALU.mult, ALU.mult).then_inc(proj_read, 1)
                    if s5_early() and j == 37:
                        s5_turns()
                    if s5_early() and j == 48:
                        s5_coefs()
                dve.wait_ge(half_used, half0 + 52)
                dve.tensor_tensor(gate_f[:, :], bank[4][0:48, 0:T], rstd[0:48, :], ALU.mult).then_inc(gate_scaled_na, 1)
                for b in range(2):
                    dve.wait_ge(gate_turned, 1)
                    dve.tensor_tensor(gates_s[:, b, :], bank[4][:, T + 64 * b:T + 64 * b + 48], na_small[:, NA_GATE:NA_GATE + 48],
                                      ALU.add).then_inc(gate_lin, 1)
                sc = score_c[:, :, :, 0:NC]
                sc_m = sc.rearrange("p b h n -> p (b h) n")
                dve.wait_ge(sc_done, 1)
                dve.wait_ge(pads_zero, 2)
                for b in range(2):
                    own(dve.tensor_tensor(sc[:, b, :, :], bank[7][:, NH * NC * b:NH * NC * (b + 1)].rearrange("p (h n) -> p h n", h=NH),
                                          na_tab[:, NA_CMASK + NC * b:NA_CMASK + NC * b + NC][:, None, :].broadcast_to([P, NH, NC]), ALU.add))
                flat_max, flat_den = (x[:, :, :].rearrange("p b h -> p (b h)") for x in (cmp_max, cmp_den))
                own(dve.tensor_reduce(flat_max, sc_m, AX.X, ALU.max))
                own(dve.tensor_scalar(flat_max, flat_max, -1e29, None, ALU.max))
                dve.tensor_tensor(sc_m, sc_m, flat_max[:, :, None].broadcast_to([P, 2 * NH, NC]), ALU.subtract).then_inc(sc_ready, 1)
                dve.wait_ge(sc_exp, 1)
                own(dve.tensor_reduce(flat_den, sc_m, AX.X, ALU.add))
                own(dve.tensor_scalar(flat_den, flat_den, 0.5, None, ALU.max))
                own(dve.reciprocal(flat_den, flat_den))
                dve.wait_ge(gates_made, 1)
                g0 = gates_s[:, :, :].rearrange("p b (h s) -> p (b h) s", s=3)[:, :, 0]
                own(dve.tensor_tensor(flat_den, flat_den, g0, ALU.mult))
                dve.tensor_tensor(sc_m, sc_m, flat_den[:, :, None].broadcast_to([P, 2 * NH, NC]), ALU.mult).then_inc(pc_made, 1)
                attention(Attention("nsa"))
                project(ph, half0 + 52, 1)

            def moba_phase(ph):
                half0 = 2 * ph["u0"]
                for j in range(24):
                    split_lo(half0 + j + SPLIT)
                    if j == 1:
                        invert(ph["norm"])
                        invert_by_token("moba")
                    if j < 16 and j % 2:
                        u = j // 2
                        dve.wait_ge(half_used, half0 + j + 1)
                        if u >= 2:
                            dve.wait_ge(q_copied, turn_q["moba"] + u - 1)
                        dve.tensor_tensor(qk_f[u % 2][:, :, :], two(bank[u % 4][:, :]), twice(rstd), ALU.mult).then_inc(qkf_made, 1)
                    if j == 17:
                        dve.wait_ge(qkrms_made, 1)
                        own(dve.reciprocal(qk_rstd[:, :, :], qk_rms[:, :, :]))
                        dve.tensor_scalar(qk_rstd[:, :, 0:8], qk_rstd[:, :, 0:8], float(P) ** -0.5, None, ALU.mult).then_inc(qkrstd_made, 1)
                    if j >= 16 and j % 2:
                        u = (j - 16) // 2
                        dve.wait_ge(half_used, half0 + j + 1)
                        for b in range(2):
                            dve.tensor_scalar(v_s[:, b, T * u:T * u + T], bank[MO_V_BANKS[u][b]][:, 0:T], rstd_tok[:, b:b + 1],
                                              None, ALU.mult).then_inc(proj_read, 1)
                dve.wait_ge(tabs_in, 16 * (2 * ("nsa" in sub_n) + 1))
                for u in range(4):
                    dve.wait_ge(krs_made, u + 1)
                    dve.wait_ge(turned, turn_n["moba"] + 4 + u + 1)
                    k = qk_s[:, 8 + 2 * u:10 + 2 * u, :]
                    dve.tensor_tensor(k, k, two(bank[u][:, :]), ALU.mult).then_inc(k_scaled, 1)
                attention(Attention("moba"))
                project(ph, half0 + 24, 1)

            def s5_turns():
                a_re, a_im, log_dt = (s5_par[:, ST * i:ST * i + ST] for i in range(3))
                magic = 12582912.0
                dve.wait_ge(s5_par_in, 16)
                exp_tiny(s5_tmp[:, :], log_dt, ST)
                own(dve.tensor_tensor(s5_turn[:, :], a_re, s5_tmp[:, :], ALU.mult))
                exp_tiny(s5_mag[:, :], s5_turn[:, :], ST)
                own(dve.tensor_tensor(s5_turn[:, :], a_im, s5_tmp[:, :], ALU.mult))
                own(dve.tensor_scalar(s5_den[:, :], s5_turn[:, :], float(1 / (2 * np.pi)), None, ALU.mult))
                own(dve.tensor_scalar(s5_tmp[:, :], s5_den[:, :], magic, magic, ALU.add, ALU.subtract))
                own(dve.tensor_tensor(s5_turn[:, :], s5_den[:, :], s5_tmp[:, :], ALU.subtract))
                own(dve.tensor_scalar(s5_turn_hi[:, :], s5_turn[:, :], magic / 65536, magic / 65536, ALU.add, ALU.subtract))
                own(dve.tensor_tensor(s5_turn_lo[:, :], s5_turn[:, :], s5_turn_hi[:, :], ALU.subtract))
                own(dve.tensor_scalar(s5_tmp[:, :], s5_turn[:, :], -1.0, None, ALU.mult))
                own(dve.tensor_tensor(s5_tmp[:, :], s5_tmp[:, :], s5_turn[:, :], ALU.max))
                own(dve.tensor_tensor(s5_den[:, :], a_re, a_re, ALU.mult))
                own(dve.tensor_tensor(s5_kre[:, :], a_im, a_im, ALU.mult))
                own(dve.tensor_tensor(s5_den[:, :], s5_den[:, :], s5_kre[:, :], ALU.add))
                dve.reciprocal(s5_den[:, :], s5_den[:, :]).then_inc(turn_made, 1)

            def s5_coefs():
                a_re, a_im = (s5_par[:, ST * i:ST * i + ST] for i in range(2))
                dve.wait_ge(lam_made, 2)
                dve.wait_ge(turn_made, 1)
                re, im, x, y = s5_cos[:, :], s5_sin[:, :], s5_kre[:, :], s5_kim[:, :]
                own(dve.tensor_tensor(re, re, s5_mag[:, :], ALU.mult))
                own(dve.tensor_scalar(re, re, -1.0, None, ALU.add))
                own(dve.tensor_tensor(im, im, s5_mag[:, :], ALU.mult))
                own(dve.tensor_tensor(x, re, a_re, ALU.mult))
                own(dve.tensor_tensor(s5_tmp[:, :], im, a_im, ALU.mult))
                own(dve.tensor_tensor(x, x, s5_tmp[:, :], ALU.add))
                own(dve.tensor_tensor(x, x, s5_den[:, :], ALU.mult))
                own(dve.tensor_tensor(y, im, a_re, ALU.mult))
                own(dve.tensor_tensor(s5_tmp[:, :], re, a_im, ALU.mult))
                own(dve.tensor_tensor(y, y, s5_tmp[:, :], ALU.subtract))
                dve.tensor_tensor(y, y, s5_den[:, :], ALU.mult).then_inc(coef_made, 1)

            def s5_phase(ph):
                half0 = 2 * ph["u0"]
                def several(instructions):
                    for x in instructions:
                        steps[0] += 1
                        x.then_inc(dve_step, 1)
                    dve.wait_ge(dve_step, steps[0])

                def cos_of(n):
                    kt, q = divmod(n, 2)
                    return table[kt % 4][:, 2 * q:2 * q + 2, 1, :][:, :, None, :].broadcast_to([P, 2, 2, T])

                def skip(kt):
                    dve.wait_ge(c_done, 2 * kt + 2)
                    dve.scalar_tensor_tensor(u_s[:, kt, :], u_s[:, kt, :], gain("s5_d", kt), bank[(7, 4)[kt % 2]][:, 0:T],
                                             ALU.mult, ALU.add).then_inc(skip_made, 1)

                def lo_of_g(run):
                    a, b = G_RUNS[run]
                    dve.wait_ge(ghi_made, run + 1)
                    dve.tensor_tensor(hg_lo[:, a:b, :], u_s[:, a:b, :], hg_hi[:, a:b, :].bitcast(F32), ALU.subtract).then_inc(glo_made, 1)

                for n in range(17):
                    if n % 4 == 0 and n < 16:
                        u = n // 4
                        split_lo(half0 + n // 2 + SPLIT)
                        if n == 0:
                            invert(ph["norm"])
                            dve.wait_ge(c_in, 32)
                            dve.wait_ge(coef_made, 1)
                            re, im, tmp = by_tile(c_raw[0]), by_tile(c_raw[1]), by_tile(c_tmp[1])
                            own(dve.tensor_tensor(tmp, re, over_outputs(s5_kim), ALU.mult))
                            own(dve.tensor_tensor(c_s[:, 1], im, over_outputs(s5_kre), ALU.mult))
                            dve.scalar_tensor_tensor(c_s[:, 1], c_s[:, 1], -1.0, tmp, ALU.mult, ALU.subtract).then_inc(c_imag_made, 1)
                        dve.wait_ge(half_used, half0 + 2 * u + 2)
                        dve.tensor_tensor(u_s[:, 2 * u:2 * u + 2, :], two(bank[5 + u % 2][:, :]), twice(rstd), ALU.mult).then_inc(u_made, 1)
                        split_lo(half0 + n // 2 + 1 + SPLIT)
                    if n >= 1:
                        m = n - 1
                        x, y = ring_x[m % 3], ring_y[m % 3]
                        dve.wait_ge(yin_made, m + 1)
                        dve.wait_ge(xin_made, m + 1)
                        several([dve.tensor_tensor(x[:, :, 0, :], x[:, :, 0, :], y[:, :, 1, :], ALU.add),
                                 dve.tensor_tensor(x[:, :, 1, :], x[:, :, 1, :], y[:, :, 0, :], ALU.subtract)])
                        for c in range(2):
                            j = 2 * m + c
                            for part in range(2):
                                dve.tensor_tensor_scan(x[:, c, part, :], s5_mag[:, j:j + 1].broadcast_to([P, T]), x[:, c, part, :],
                                                       0.0, ALU.mult, ALU.add).then_inc(z_made, 1)
                        dve.wait_ge(z_made, 4 * m + 4)
                        dve.tensor_tensor(y[:, :, :, :], x[:, :, :, :], cos_of(m), ALU.mult).then_inc(xout_made, 1)
                    if n < 16:
                        dve.wait_ge(bu_kept, 2 * n + 2)
                        if n % 2 == 0:
                            dve.wait_ge(*table_ready(n // 2))
                        if n == 1:
                            dve.wait_ge(c_imag_made, 1)
                        if n == 2:
                            dve.wait_ge(c_made, 2)
                        if n >= 3:
                            dve.wait_ge(c_done, n - 2)
                        dve.tensor_tensor(ring_x[n % 3][:, :, :, :], bu_s[:, :, :, :], cos_of(n), ALU.mult).then_inc(xin_made, 1)
                    if n % 2 and n >= 5:
                        skip((n - 5) // 2)
                skip(6)
                skip(7)
                lo_of_g(0)
                lo_of_g(1)
                lo_of_g(2)
                for u in range(4):
                    dve.wait_ge(glu_sig, u + 1)
                    uu = u_s[:, 2 * u:2 * u + 2, :]
                    dve.tensor_tensor(uu, uu, bu_s[:, u % 2, :, :], ALU.mult).then_inc(gated, 1)
                    split_lo(half0 + 8 + 2 * u + SPLIT)
                    split_lo(half0 + 9 + 2 * u + SPLIT)
                    dve.wait_ge(outhi_made, u + 1)
                    dve.tensor_tensor(out_lo[:, 2 * u:2 * u + 2, :], uu, out_hi[:, 2 * u:2 * u + 2, :].bitcast(F32), ALU.subtract)\
                       .then_inc(outlo_made, 1)
                project(ph, half0 + 16, 1)
            dve.wait_ge(x_in, 16)
            dve.wait_ge(consts_in, 16)
            for m in range(KT):
                make_hg_lo(phases[0]["gain"], 0, m)
            for half in range(SPLIT):
                split_lo(half)
            if phase_of("rglru"):
                softplus_lambda()
            if phase_of("s5") and not s5_early():
                s5_turns()
                s5_coefs()
            for ph in phases:
                if ph["kind"] == "ffn":
                    ffn_phase(ph)
                elif ph["kind"] == "final":
                    invert(ph["norm"])
                    for m in range(KT):
                        dve.scalar_tensor_tensor(h[:, m, :], h[:, m, :], gain("final", m), rstd[:, :],
                                                 ALU.mult, ALU.mult).then_inc(h_written, 1)
                        if ph["next"] and m:
                            make_hg_lo(ph["next"], ph["next_hg"], m - 1)
                    if ph["next"]:
                        make_hg_lo(ph["next"], ph["next_hg"], KT - 1)
                elif ph["kind"] == "rglru":
                    rglru_phase(ph)

                elif ph["kind"] == "nsa":
                    nsa_phase(ph)
                elif ph["kind"] == "moba":
                    moba_phase(ph)
                elif ph["kind"] == "s5":
                    s5_phase(ph)

        @block.tensor
        def _(pe):
            def three_passes(psum, w_hi_ap, w_lo_ap, x_hi_ap, x_lo_ap, first, last, **kw):
                pe.matmul(psum, w_hi_ap, x_hi_ap, start=first, stop=False, **kw)
                pe.matmul(psum, w_hi_ap, x_lo_ap, start=False, stop=False, **kw)
                return pe.matmul(psum, w_lo_ap, x_hi_ap, start=False, stop=last, **kw)

            def weights(half, it=0):
                pe.wait_ge(lo_made, half + 1 + 2 * BODY * it)
                return w_hi[half % SPLIT], w_lo[half % SPLIT]

            def mean_square(norm):
                pe.wait_ge(sumsq_made, norm + 1)
                if norm == 0:
                    pe.wait_ge(pool_const, 2)
                pe.matmul(bank[NORM_BANK][:, 0:T], ones_d[:, :], sumsq[:, :], start=True, stop=True).then_inc(ms_made, 1)

            def from_hg(half, psum, it=0, hg=None, cols=P):
                hi, lo = weights(half, it)
                for k in range(KT):
                    if hg is not None:
                        pe.wait_ge(hg_made, KT * hg + k + 1)
                    last = three_passes(psum, hi[:, k * cols:(k + 1) * cols], lo[:, k * cols:(k + 1) * cols],
                                        hg_hi[:, k, :], hg_lo[:, k, :], k == 0, k == KT - 1)
                last.then_inc(half_used, 1)

            def project(ph, half0, halves, per_half, x_hi, x_lo, ready):
                for m in range(KT):
                    if m >= 2:
                        pe.wait_ge(h_written, h_count(ph["hw"], m - 2))
                    k = 0
                    for j in range(halves):
                        hi, lo = weights(half0 + m * halves + j)
                        for q in range(per_half):
                            if m == 0:
                                ready(k)
                            last = three_passes(bank[2 + m % 2][:, 0:T], hi[:, q * P:(q + 1) * P], lo[:, q * P:(q + 1) * P],
                                                x_hi(k), x_lo(k), k == 0, k == halves * per_half - 1)
                            k += 1
                        last.then_inc(half_used, 1)

            def ffn_phase(ph):
                half0 = 2 * ph["u0"]
                pairs0 = PAIRS * ph["f"]

                def pair(p, it=0):
                    half = half0 + 4 * p
                    for side in range(2):
                        psum = bank[2 * (p % 2) + side]
                        if p:
                            done = pairs0 + p - 1 + 2 * it
                            pe.wait_ge(up_scaled if side else gate_scaled, done)
                        for c in range(2):
                            from_hg(half + 2 * side + c, psum[:, c * T:(c + 1) * T], it,
                                    hg=ph["hg"] if p == 0 and side == 0 and c == 0 else None)
                        if p == 0 and side == 0:
                            mean_square(ph["norm"])

                pair(0)
                with pe.Fori(0, 5) as it:
                    pair(1, it)
                    pair(2, it)

                half1 = half0 + 4 * PAIRS

                def down(m, it=0):
                    if m >= 2:
                        pe.wait_ge(h_written, h_count(ph["hw"], m - 2) + 2 * it)
                    for j in range(2):
                        half = half1 + 2 * m + j
                        pe.wait_ge(lo_made, half + 1 + 4 * it)
                        hi, lo = w_hi[half % SPLIT], w_lo[half % SPLIT]
                        for q in range(FT // 2):
                            k = j * (FT // 2) + q
                            if m == 0 and k % 2 == 0:
                                pe.wait_ge(hid_made, pairs0 + k // 2 + 1)
                            last = three_passes(bank[2 + m % 2][:, 0:T], hi[:, q * P:(q + 1) * P], lo[:, q * P:(q + 1) * P],
                                                hid_hi[:, k * T:(k + 1) * T], hid_lo[:, k * T:(k + 1) * T],
                                                k == 0, k == FT - 1)
                        last.then_inc(half_used, 1)

                down(0)
                down(1)
                with pe.Fori(0, 3) as it:
                    down(2, it)
                    down(3, it)

            def rglru_phase(ph):
                half0 = 2 * ph["u0"]

                def gates(g):
                    pe.wait_ge(xc_made, g + 1)
                    if g == 0:
                        pe.wait_ge(gate_w_in, 16)
                    else:
                        pe.wait_ge(sigm_made, 2 * GT * g)
                    slot = GT * (g % 2)
                    for side in range(2):
                        for m in range(GT):
                            n = side * GT + m
                            psum = bank[5 + n // 2][:, n % 2 * T:(n % 2 + 1) * T]
                            tiles = [(i, k) for i, (k, mm) in enumerate(BD_TILES) if mm == m]
                            for i, k in tiles:
                                last = pe.matmul(psum, gate_w[:, (side * 4 + g) * 7 + i, :], xc[:, slot + k, :],
                                                 start=(i, k) == tiles[0], stop=(i, k) == tiles[-1])
                    last.then_inc(gates_done, 1)

                for j in range(2 * RT):
                    u = j // 2
                    if j % 2 == 0 and u >= 4:
                        if u - 4 < RT // 2:
                            pe.wait_ge(xb_made, u - 3)
                        else:
                            pe.wait_ge(y_scaled, u - 3 - RT // 2)
                    from_hg(half0 + j, bank[u % 4][:, j % 2 * T:(j % 2 + 1) * T], hg=ph["hg"] if j == 0 else None)
                    if j == 1:
                        mean_square(ph["norm"])
                    if j in GATES_AT:
                        gates(GATES_AT.index(j))
                pe.wait_ge(y_scaled, RT // 2)
                project(ph, half0 + 2 * RT, 2, 6, lambda k: rec_hi[:, k, :], lambda k: rec_lo[:, k, :],
                        lambda k: pe.wait_ge(rec_made, k // GT + 1))

            def mean_square_by_token(norm):
                pe.wait_ge(sumsq_made, norm + 1)
                if norm == 0:
                    pe.wait_ge(pool_const, 2)
                pe.matmul(bank[NORM_BANK][:, 0:T], ones_d[:, :], sumsq[:, :], start=True, stop=True)
                for b in range(2):
                    last = pe.matmul(bank[NORM_BANK][:, T + b:T + b + 1], sumsq[:, P * b:P * b + P], ones_d[:, 0:1], start=True, stop=True)
                last.then_inc(ms_made, 1)

            def token_major(half, side, psum):
                hi, lo = weights(half)
                for b in range(2):
                    t = slice(P * b, P * b + P)
                    for q in range(KT // 2):
                        k = side * (KT // 2) + q
                        w = slice(q * T, (q + 1) * T)
                        out_ap = psum[b][:, 0:T]
                        pe.matmul(out_ap, hg_hi[:, k, t], hi[:, w], start=k == 0, stop=False)
                        pe.matmul(out_ap, hg_lo[:, k, t], hi[:, w], start=False, stop=False)
                        last = pe.matmul(out_ap, hg_hi[:, k, t], lo[:, w], start=False, stop=k == KT - 1)
                last.then_inc(half_used, 1)

            def attention(att, score, pv, first_waits):
                def scores(n):
                    job, branch, group, b, keys = att.step(n)
                    if n >= 2:
                        pe.wait_ge(negmax, att.step0 + n - 1)
                    for i in range(4):
                        q, k = score(branch, 4 * group + i, b)
                        last = pe.matmul(att.score_bank(n, i, keys), q, k[:, 0:keys], start=True, stop=True)
                    last.then_inc(scores_done, 1)

                def turn(n):
                    job, branch, group, b, keys = att.step(n)
                    pe.wait_ge(prob_made, att.step0 + n + 1)
                    if n >= 1:
                        pe.wait_ge(prob_kept, kept_at(att, n))
                    for kt in range(b + 1):
                        for i in range(4):
                            last = pe.transpose(bank[5 + kt][:, P * i:P * i + P], att.prob[n % 3][:, i, P * kt:P * kt + P], att.ident)
                    last.then_inc(prob_turned, 1)

                def outputs(job):
                    group, b = divmod(job, 2)
                    pe.wait_ge(prob_kept, kept_at(att, (job + 1) * att.branches))
                    if job >= 2:
                        pe.wait_ge(o_made, att.job0 + job - 1)
                    psum = bank[(7, 4)[job % 2]]
                    for i in range(4):
                        last = pv(psum, group, b, i)
                    last.then_inc(pv_done, 1)

                def kept_at(att, n):
                    return kept0[0] + sum(att.step(x)[3] + 1 for x in range(n))

                first_waits()
                scores(0)
                scores(1)
                for n in range(att.steps):
                    job = n // att.branches
                    if n + 2 < att.steps:
                        scores(n + 2)
                    turn(n)
                    if n % att.branches == 0 and job >= 1:
                        outputs(job - 1)
                outputs(att.jobs - 1)
                kept0[0] = kept_at(att, att.steps)

            kept0 = [0]

            def nsa_phase(ph):
                half0 = 2 * ph["u0"]
                base = proj_n["nsa"]
                for j in range(18):
                    u = j // 2
                    if j % 2 == 0 and u >= 4:
                        pe.wait_ge(proj_read, base + u - 3)
                    if j in (4, 5):
                        from_hg(half0 + j, bank[u % 4][:, j % 2 * T:(j % 2 + 1) * T])
                    elif j < 14:
                        from_hg(half0 + j, bank[u % 4][0:96, j % 2 * T:(j % 2 + 1) * T], hg=ph["hg"] if j == 0 else None, cols=96)
                    else:
                        token_major(half0 + j, j % 2, [bank[i] for i in NA_V_BANKS[u - 7]])
                    if j == 1:
                        mean_square_by_token(ph["norm"])
                for j in range(18, 26):
                    hi, lo = weights(half0 + j)
                    if j == 18:
                        pe.wait_ge(proj_read, base + 11)
                        pe.wait_ge(blklo_made, 1)
                    for q in range(4):
                        tok = 4 * (j - 18) + q
                        w = slice(T * q, T * q + T)
                        last = three_passes(bank[0][0:NG * NC, 0:T], blk_k_hi[0:96, tok, :], blk_k_lo[0:96, tok, :], hi[0:96, w], lo[0:96, w],
                                            tok == 0, tok == CB - 1)
                    last.then_inc(half_used, 1)
                for j in range(26, 34):
                    hi, lo = weights(half0 + j)
                    if j == 26:
                        pe.wait_ge(blklo_made, 2)
                    for q in range(4):
                        tok = 4 * (j - 26) + q
                        w = slice(T * q, T * q + T)
                        last = three_passes(bank[1][0:NG * NC, 0:T], blk_v_hi[:, tok, :], blk_v_lo[:, tok, :], hi[:, w], lo[:, w],
                                            tok == 0, tok == CB - 1)
                    last.then_inc(half_used, 1)
                for j in range(34, 50):
                    u = (j - 34) // 2
                    if j == 34:
                        pe.wait_ge(hq_made, KT)
                        pe.wait_ge(tabs_in, 32)
                    if j in (34, 36):
                        pe.wait_ge(cmp_gelu, (j - 32) // 2)
                    if j % 2 == 0 and u >= 4:
                        pe.wait_ge(proj_read, base + 11 + u - 3)
                    hi, lo = weights(half0 + j)
                    for k in range(KT):
                        last = three_passes(bank[u % 4][0:96, j % 2 * T:(j % 2 + 1) * T], hi[:, 96 * k:96 * k + 96], lo[:, 96 * k:96 * k + 96],
                                            hq_hi[:, k, :], hq_lo[:, k, :], k == 0, k == KT - 1)
                    last.then_inc(half_used, 1)
                    if j == 36:
                        pe.wait_ge(cmp_gelu, 2)
                        for side in range(2):
                            for m in range(2):
                                at = 64 * (2 * side + m)
                                last = pe.transpose(bank[5][:, at:at + NG * NC], hid_t[:, side, P * m:P * m + P],
                                                    na_tab[0:NG * NC, 3 * T:3 * T + NG * NC])
                        last.then_inc(cmp_turned, 1)
                    if j == 38:
                        pe.wait_ge(hid_kept, 9)
                        for m in range(2):
                            last = pe.matmul(bank[7][0:96, 0:NG * NC], na_small[:, NA_W2K + 96 * m:NA_W2K + 96 * m + 96], hk_s[:, m, :],
                                             start=m == 0, stop=m == 1)
                        last.then_inc(cmp_done, 1)
                        for g in range(NG):
                            for m in range(2):
                                last = pe.matmul(bank[6][:, 64 * g:64 * g + 64], hv_rep[:, m, g, :],
                                                 na_small[:, NA_W2V + 64 * m:NA_W2V + 64 * m + 64], start=m == 0, stop=m == 1)
                        last.then_inc(cmp_done, 1)
                for c in range(2):
                    hi, lo = weights(half0 + 50 + c)
                    for q in range(KT // 2):
                        k = c * (KT // 2) + q
                        last = three_passes(bank[4][0:48, 0:T], hi[:, 48 * q:48 * q + 48], lo[:, 48 * q:48 * q + 48],
                                            hq_hi[:, k, :], hq_lo[:, k, :], k == 0, k == KT - 1)
                    last.then_inc(half_used, 1)
                pe.wait_ge(cmp_kept, 5)
                pe.wait_ge(proj_read, base + 19)
                for b in range(2):
                    for hd in range(NH):
                        g = hd // 4
                        last = pe.matmul(bank[7][:, NC * (NH * b + hd):NC * (NH * b + hd + 1)], q_s[0:96, hd, P * b:P * b + P],
                                         kc_s[0:96, NC * g:NC * g + NC], start=True, stop=True)
                last.then_inc(sc_done, 1)
                pe.wait_ge(gate_scaled_na, 1)
                for b in range(2):
                    last = pe.transpose(bank[4][:, T + 64 * b:T + 64 * b + 48], gate_f[:, P * b:P * b + P], na_tab[0:48, 3 * T:3 * T + 48])
                last.then_inc(gate_turned, 1)
                att = Attention("nsa")
                pe.wait_ge(pc_made, 1)
                for b in range(2):
                    for g in range(NG):
                        last = pe.transpose(bank[5 + b][:, P * g:P * g + P], score_c[:, b, 4 * g:4 * g + 4, :].rearrange("p h n -> p (h n)"), att.ident)
                    last.then_inc(pc_turned, 1)

                def score(branch, hd, b):
                    return qr_s[0:96, hd, P * b:P * b + P], (ks_s, kw_s)[branch][0:96, hd // 4, :]

                def pv(psum, group, b, i):
                    out_ap = psum[64 * (i % 2):64 * (i % 2) + 64, P * (i // 2):P * (i // 2) + P]
                    for branch in range(2):
                        v = (v_sel, v_win)[branch]
                        for kt in range(b + 1):
                            pe.matmul(out_ap, v[:, kt, 64 * group:64 * group + 64], att.prob_t[branch][:, kt, i, :],
                                      start=branch == 0 and kt == 0, stop=False)
                    return pe.matmul(out_ap, vc_s[:, group, i, :], prob_c[:, b, group, :], start=False, stop=True)

                def first_waits():
                    pe.wait_ge(turned, turn_n["nsa"] + 12)
                    pe.wait_ge(pc_kept, 2)

                attention(att, score, pv, first_waits)
                project(ph, half0 + 52, 1, 8, lambda k: hq_hi[:, k, :], lambda k: hq_lo[:, k, :],
                        lambda k: pe.wait_ge(o_made, job_n["nsa"] + 2 * (k // 2) + 2))

            def moba_phase(ph):
                half0 = 2 * ph["u0"]

                def mean_of_heads(u):
                    pe.wait_ge(qksq_made, u + 1)
                    for c in range(2):
                        for b in range(2):
                            n = 16 * b + 2 * u + c
                            last = pe.matmul(bank[5][:, n:n + 1], qk_sq[u % 2][:, c, P * b:P * b + P], ones_d[:, 0:1], start=True, stop=True)
                    last.then_inc(qkms_made, 1)

                for j in range(16):
                    u = j // 2
                    if j % 2 == 0 and u >= 4:
                        pe.wait_ge(qkf_made, u - 3)
                    from_hg(half0 + j, bank[u % 4][:, j % 2 * T:(j % 2 + 1) * T], hg=ph["hg"] if j == 0 else None)
                    if j == 1:
                        mean_square_by_token(ph["norm"])
                    if j % 2 and u >= 1:
                        mean_of_heads(u - 1)
                for j in range(16, 24):
                    u = (j - 16) // 2
                    if j in (16, 18):
                        pe.wait_ge(qkf_made, 6 + 2 * u)
                    if j == 22:
                        pe.wait_ge(proj_read, proj_n["moba"] + 2)
                    token_major(half0 + j, j % 2, [bank[i] for i in MO_V_BANKS[u]])
                    if j == 16:
                        mean_of_heads(7)
                att = Attention("moba")
                pe.wait_ge(tabs_in, 16 * (2 * ("nsa" in sub_n) + 1))
                pe.wait_ge(qkrstd_made, 1)
                pe.wait_ge(proj_read, proj_n["moba"] + 8)
                for u in range(4):
                    for c in range(2):
                        for b in range(2):
                            r = qk_rstd[:, b, 8 + 2 * u + c:9 + 2 * u + c].broadcast_to([P, P])
                            last = pe.matmul(bank[u][:, T * c + P * b:T * c + P * b + P], r, att.ident, start=True, stop=True)
                    last.then_inc(krs_made, 1)

                def score(branch, hd, b):
                    return qk_s[:, hd, P * b:P * b + P], qk_s[:, 8 + hd, :]

                def pv(psum, group, b, i):
                    hd = 4 * group + i
                    job = 2 * group + b
                    for kt in range(b + 1):
                        last = pe.matmul(psum[:, P * i:P * i + P], v_s[:, kt, P * hd:P * hd + P], att.prob_t[job % 2][:, kt, i, :],
                                         start=kt == 0, stop=kt == b)
                    return last

                attention(att, score, pv, lambda: pe.wait_ge(k_scaled, 4))
                project(ph, half0 + 24, 1, 8, lambda k: mo_o_hi[:, k, :], lambda k: mo_o_lo[:, k, :],
                        lambda k: pe.wait_ge(o_made, job_n["moba"] + 2 * (k // 4) + 2))

            def s5_phase(ph):
                half0 = 2 * ph["u0"]

                def b_products(n):
                    kt, q = divmod(n, 2)
                    pe.wait_ge(u_made, kt // 2 + 1)
                    pe.wait_ge(bt_in[kt % 4], 16 * (kt // 4 + 1))
                    if n >= 2:
                        pe.wait_ge(bu_kept, 2 * (n - 2) + 2)
                    for c in range(2):
                        rows = slice(32 * (2 * q + c), 32 * (2 * q + c) + 32)
                        for part in range(2):
                            last = pe.matmul(bank[2 * q + c][:, T * part:T * part + T], bt_s[kt % 4][rows, part, :], u_s[rows, kt, :],
                                             start=True, stop=True)
                    last.then_inc(b_done, 1)

                def c_products(n):
                    kt, q = divmod(n, 2)
                    x, y = ring_x[n % 3], ring_y[n % 3]
                    if n == 0:
                        pe.wait_ge(c_made, 2)
                        pe.wait_ge(c_imag_made, 1)
                    if n % 2 == 0 and n >= 4:
                        pe.wait_ge(skip_made, kt - 1)
                    for step, (src, sems, terms) in enumerate((
                            (y, xout_made, ((0, 0), (1, 1))),
                            (x, yout_made, ((0, 1), (1, 2))))):
                        pe.wait_ge(sems, n + 1)
                        for c in range(2):
                            j = 2 * n + c
                            rows = slice(32 * (2 * q + c), 32 * (2 * q + c) + 32)
                            for part, w in terms:
                                last = pe.matmul(bank[(7, 4)[kt % 2]][rows, 0:T], c_s[:, w, j, :], src[:, c, part, :],
                                                 start=step == 0 and part == 0, stop=step == 1 and part == 1)
                    last.then_inc(c_done, 1)

                for n in range(16):
                    if n % 4 == 0:
                        u = n // 4
                        for c in range(2):
                            if c == 0 and u >= 2:
                                pe.wait_ge(u_made, u - 1)
                            from_hg(half0 + 2 * u + c, bank[5 + u % 2][:, c * T:(c + 1) * T], hg=ph["hg"] if u == 0 and c == 0 else None)
                        if u == 0:
                            mean_square(ph["norm"])
                    b_products(n)
                    if n >= 2:
                        c_products(n - 2)
                c_products(14)
                c_products(15)
                for u in range(4):
                    for c in range(2):
                        hi, lo = weights(half0 + 8 + 2 * u + c)
                        for k in range(KT):
                            if u == 0 and c == 0:
                                pe.wait_ge(glo_made, 1 + sum(k >= b for a, b in G_RUNS))
                            last = three_passes(bank[u][:, c * T:(c + 1) * T], hi[:, k * P:(k + 1) * P], lo[:, k * P:(k + 1) * P],
                                                hg_hi[:, k, :], hg_lo[:, k, :], k == 0, k == KT - 1)
                        last.then_inc(half_used, 1)
                pe.wait_ge(glu_sig, 4)
                project(ph, half0 + 16, 1, 8, lambda k: out_hi[:, k, :], lambda k: out_lo[:, k, :],
                        lambda k: pe.wait_ge(outlo_made, k // 2 + 1))
            for ph in phases:
                if ph["kind"] == "ffn":
                    ffn_phase(ph)
                elif ph["kind"] == "final":
                    mean_square(ph["norm"])
                elif ph["kind"] == "rglru":
                    rglru_phase(ph)

                elif ph["kind"] == "nsa":
                    nsa_phase(ph)
                elif ph["kind"] == "moba":
                    moba_phase(ph)
                elif ph["kind"] == "s5":
                    s5_phase(ph)


def units_8(w):
    n = w.shape[1]
    return w.reshape(KT, P, n // 256, 2, P).transpose(2, 1, 3, 0, 4).reshape(n // 256, P, 2 * KT * P)


def units_k(w):
    kt = w.shape[0] // P
    return w.reshape(kt, P, D // P, P).transpose(2, 1, 0, 3).reshape(D // P, P, kt * P)


def units_cols(w, cols):
    n = w.shape[1]
    return w.reshape(KT, P, n // (2 * cols), 2, cols).transpose(2, 1, 3, 0, 4).reshape(n // (2 * cols), P, 2 * KT * cols)


def units_moving(w, cols):
    n = w.shape[1]
    return w.reshape(2, KT // 2, P, n // cols, cols).transpose(3, 2, 0, 1, 4).reshape(n // cols, P, KT * cols)


def gate_up(gate, up):
    return np.stack([units_8(gate), units_8(up)], axis=1).reshape(-1, P, 2 * KT * P)


def columns(v):
    return v.reshape(-1, P).T


def block_diagonal(matrices):
    tiles = []
    for w in matrices:
        for g in range(4):
            full = np.zeros((3 * P, 3 * P), w.dtype)
            for b in range(4):
                full[96 * b:96 * b + 96, 96 * b:96 * b + 96] = w[4 * g + b]
            for k, m in [(0, 0), (1, 0), (0, 1), (1, 1), (2, 1), (1, 2), (2, 2)]:
                tiles.append(full[P * k:P * k + P, P * m:P * m + P])
    return np.stack(tiles, axis=1)


def rotary_table(rows, half):
    inv = np.power(np.float32(500000.0), -np.arange(half, dtype=np.float32) * np.float32(2.0) / np.float32(2 * half))
    ang = (np.arange(T, dtype=np.float32)[None, :] * inv[:, None].astype(np.float32)).astype(np.float64)
    cos, sin = np.cos(ang), np.sin(ang)
    out = np.zeros((rows, 2 * T), np.float32)
    out[:2 * half, :T] = np.concatenate([cos, cos])
    out[:2 * half, T:] = np.concatenate([-sin, sin])
    return out


def shape_tables():
    masked = np.float32(-1e30)
    q = np.arange(P)
    causal = np.zeros((P, T), np.float32)
    causal[:, P:] = np.where(q[None, :] <= q[:, None], np.float32(0), masked)
    ident = np.eye(P, dtype=np.float32)
    ends = np.arange(NC) * CS + CB - 1
    blocks = [np.where(ends[None, :] <= (q + P * b)[:, None], np.float32(0), masked) for b in range(2)]
    na_tab = np.concatenate([rotary_table(P, 12), causal, ident, *blocks], axis=1).astype(np.float32)
    mo_tab = np.concatenate([rotary_table(P, 16), causal, ident], axis=1).astype(np.float32)
    return na_tab, mo_tab


def rows_padded(a, rows=P):
    return np.concatenate([a, np.zeros((rows - a.shape[0],) + a.shape[1:], a.dtype)])


def compression(w, dims, copies):
    w = w.reshape(4, 8, dims, T).transpose(0, 2, 1, 3)
    w = np.concatenate([w] * copies, axis=1)
    if w.shape[1] < P:
        w = np.concatenate([w, np.zeros((4, P - w.shape[1], 8, T), w.dtype)], axis=1)
    return w.reshape(4, P, 8 * T)


def lay_out(i):
    gk, gv = NG * 96, NG * 64
    kv = i["kv_w"]
    k_cmp, v_cmp, k_sel, v_sel, k_win, v_win = np.split(kv, np.cumsum([gk, gv, gk, gv, gk]), axis=1)
    w_in = i["a_w_in"][0]
    w_q = i["b_w_q"][0]
    ffn_gu = [(w[:, :FF], w[:, FF:]) for w in i["ffn_w_gu"]]
    ffn_2 = [(i["ffn_w_gate_2"][a, b], i["ffn_w_up_2"][a, b]) for a in range(2) for b in range(2)]
    qkv = i["moba_w_qkv_2"][0]
    arrays = {
        "x": i["x"][0].T.reshape(KT, P, T).transpose(1, 0, 2),
        "w8": np.concatenate([
            units_8(w_in),
            gate_up(*ffn_gu[0]),
            units_8(v_cmp), units_moving(v_sel, T), units_moving(v_win, T),
            compression(i["cmp_w1_k"], 96, 1), compression(i["cmp_w1_v"], 64, 2),
            units_8(i["b_w_o"][0]),
            gate_up(*ffn_gu[1]),
            gate_up(*ffn_2[0]),
            units_8(i["s5_w_in_2"][0]), units_8(i["s5_w_glu_2"][0]), units_8(i["s5_w_out_2"][0]),
            gate_up(*ffn_2[1]), gate_up(*ffn_2[2]),
            units_8(qkv[:, :2 * D]), units_moving(qkv[:, 2 * D:], T), units_8(i["moba_w_out_2"][0]),
            gate_up(*ffn_2[3])]),
        "w22": np.concatenate([units_k(w) for w in [*i["ffn_w_down"], *i["ffn_w_down_2"].reshape(4, FF, D)]]),
        "w12": units_k(i["a_w_out"][0]),
        "q96": np.concatenate([units_cols(w, 96) for w in (k_cmp, k_sel, k_win, w_q[:, :NH * 96])]),
        "gate": units_moving(w_q[:, NH * 96:], 48),
        "gate_w": block_diagonal([i["a_w_ra"][0], i["a_w_ix"][0]]),
    }
    vectors = {
        "norm_00": i["norm_g"][0, 0], "norm_01": i["norm_g"][0, 1], "norm_10": i["norm_g"][1, 0],
        "norm_11": i["norm_g"][1, 1], "kv": i["kv_norm_g"], "final": i["final_g"],
        "ffn_00": i["ffn_norm_2"][0, 0], "ffn_01": i["ffn_norm_2"][0, 1], "ffn_10": i["ffn_norm_2"][1, 0],
        "ffn_11": i["ffn_norm_2"][1, 1], "mix_0": i["mix_norm_2"][0], "mix_1": i["mix_norm_2"][1],
        "s5_d": i["s5_d_2"][0], "conv_b": i["a_conv_b"][0], "lam": i["a_lambda"][0],
        "b_ra": i["a_b_ra"][0], "b_ix": i["a_b_ix"][0], "q_gain": i["moba_q_norm_2"][0],
        "k_gain": i["moba_k_norm_2"][0], **{f"conv_{j}": i["a_conv_w"][0, j] for j in range(4)},
    }
    arrays["vec"] = np.concatenate([columns(vectors[name]) for name in VEC], axis=1)
    arrays["na_tab"], arrays["mo_tab"] = shape_tables()
    arrays["na_small"] = np.concatenate([
        rows_padded(i["cmp_pos_k"].T), np.concatenate([i["cmp_pos_v"].T] * 2),
        i["cmp_w2_k"].reshape(2, P, 96).transpose(1, 0, 2).reshape(P, 192),
        i["cmp_w2_v"].reshape(2, P, 64).transpose(1, 0, 2).reshape(P, 128),
        np.broadcast_to(i["b_gate_bias"][0], (P, 48))], axis=1)
    def by_state(a):
        return a.reshape(ST, P).T

    def block_pairs(a):
        out = np.zeros((ST, 2, 64, 2, 16), a.dtype)
        a = a.reshape(ST, 2, 64, 16)
        for g in range(2):
            out[:, g, :, g, :] = a[:, g]
        return out

    log_dt = np.repeat(i["s5_log_dt_2"][0], 64)
    arrays["s5_par"] = np.concatenate([
        by_state(i["s5_a_re_2"][0]), by_state(i["s5_a_im_2"][0]), by_state(log_dt),
        np.broadcast_to(np.arange(T, dtype=np.float32), (P, T))], axis=1)
    arrays["s5_b"] = np.stack([
        block_pairs(i[k][0]).reshape(KT, 4, P, 32).transpose(1, 3, 0, 2).reshape(P, KT, P)
        for k in ("s5_b_re_2", "s5_b_im_2")], axis=2)
    arrays["s5_c"] = np.stack([
        block_pairs(i[k][0].transpose(0, 2, 1)).reshape(ST, P, 32).transpose(1, 0, 2).reshape(P, 2, 2, T)
        for k in ("s5_c_re_2", "s5_c_im_2")], axis=1)
    return {k: np.ascontiguousarray(v) for k, v in arrays.items()}


def kernel(**inputs):
    import concourse.bacc as bacc
    from concourse.bass_utils import run_bass_kernel_spmd

    arrays = {f"in_{k}": v for k, v in lay_out({k: np.asarray(v) for k, v in inputs.items()}).items()}
    nc = bacc.Bacc("TRN2", target_bir_lowering=False, num_devices=1)
    ins = {k[3:]: nc.dram_tensor(k, v.shape, mybir.dt.from_np(v.dtype), kind="ExternalInput").ap()
           for k, v in arrays.items()}
    out = nc.dram_tensor("out_h", (P, KT, T), F32, kind="ExternalOutput").ap()
    two_blocks(nc, ins, out, layer_plan())
    result = run_bass_kernel_spmd(nc, [arrays], core_ids=[0]).results[0]["out_h"]
    return result.transpose(1, 0, 2).reshape(D, T).T[None]
```
